# Optimizing a Trainium2 kernel written in Bass

```python
import math
import jax, jax.numpy as jnp
from jax import lax
import numpy as np

D_MODEL = 1024
BATCH = 1
SEQ = 256
DEPTH = 2

FOX_HEADS = 4
FOX_HEAD_DIM = 64
MOBA_HEADS = 4
MOBA_HEAD_DIM = 64
MOBA_BLOCK = 256
MOBA_TOPK = 3
MOBA_Q_CHUNK = 32
MLA_HEADS = 8
MLA_NOPE_DIM = 64
MLA_ROPE_DIM = 32
MLA_V_DIM = 64
MLA_Q_RANK = 256
MLA_KV_RANK = 128
ROPE_THETA = 10000.0
T5_BUCKETS = 32
T5_MAX_DISTANCE = 128
Q_BLOCK = 128
D_FF = -(-8 * D_MODEL // (3 * 256)) * 256
RMS_EPS = 1e-6

FOX_W = FOX_HEADS * FOX_HEAD_DIM
MOBA_W = MOBA_HEADS * MOBA_HEAD_DIM
MLA_W = MLA_HEADS * MLA_V_DIM
MIX_WIDTH = FOX_W + MOBA_W + MLA_W
IN_SIZES = (FOX_W, FOX_W, FOX_W, FOX_HEADS, MOBA_W, MOBA_W, MOBA_W, MLA_Q_RANK, MLA_KV_RANK, MLA_ROPE_DIM)
IN_WIDTH = 3 * FOX_W + FOX_HEADS + 3 * MOBA_W + MLA_Q_RANK + MLA_KV_RANK + MLA_ROPE_DIM


def rmsnorm(x, g):
    x32 = x.astype(jnp.float32)
    y = x32 * lax.rsqrt(jnp.mean(x32 * x32, axis=-1, keepdims=True) + RMS_EPS)
    return (y * g.astype(jnp.float32)).astype(x.dtype)

def rope(x, pos):
    half = x.shape[-1] // 2
    inv_freq = 1.0 / (ROPE_THETA ** (jnp.arange(half, dtype=jnp.float32) / half))
    ang = pos.astype(jnp.float32)[:, None] * inv_freq[None, :]
    cos, sin = jnp.cos(ang), jnp.sin(ang)
    x32 = x.astype(jnp.float32)
    x1, x2 = x32[..., :half], x32[..., half:]
    return jnp.concatenate([x1 * cos - x2 * sin, x2 * cos + x1 * sin], axis=-1).astype(x.dtype)

def t5_bucket(dist):
    n = jnp.maximum(dist, 0)
    max_exact = T5_BUCKETS // 2
    nf = jnp.maximum(n, max_exact).astype(jnp.float32)
    large = max_exact + (jnp.log(nf / max_exact) / math.log(T5_MAX_DISTANCE / max_exact)
                         * (T5_BUCKETS - max_exact)).astype(jnp.int32)
    large = jnp.minimum(large, T5_BUCKETS - 1)
    return jnp.where(n < max_exact, n, large)

def dense_causal_attention(q, k, v, log_decay_cum=None):
    B, H, S, dk = q.shape
    dv = v.shape[-1]
    nqb = S // Q_BLOCK
    scale = dk ** -0.5
    kpos = jnp.arange(S)
    q_blocks = q.reshape(B, H, nqb, Q_BLOCK, dk).transpose(2, 0, 1, 3, 4)
    starts = jnp.arange(nqb, dtype=jnp.int32) * Q_BLOCK
    if log_decay_cum is None:
        xs = (q_blocks, starts)
    else:
        xs = (q_blocks, starts, log_decay_cum.reshape(B, H, nqb, Q_BLOCK).transpose(2, 0, 1, 3))

    def step(blk):
        q_i, t0 = blk[0], blk[1]
        s = jnp.einsum('bhqd,bhkd->bhqk', q_i, k).astype(jnp.float32) * scale
        if log_decay_cum is not None:
            s = s + blk[2][..., None] - log_decay_cum[:, :, None, :]
        qpos = t0 + jnp.arange(Q_BLOCK)
        s = jnp.where(kpos[None, :] <= qpos[:, None], s, -jnp.inf)
        p = jax.nn.softmax(s, axis=-1)
        return jnp.einsum('bhqk,bhkd->bhqd', p.astype(v.dtype), v)

    out = lax.map(step, xs)
    return out.transpose(1, 2, 0, 3, 4).reshape(B, H, S, dv)

def moba_attention(q, k, v, t5_table):
    B, H, S, d = q.shape
    nb = -(-S // MOBA_BLOCK)
    s_pad = nb * MOBA_BLOCK
    n_sel = min(MOBA_TOPK, nb)
    scale = d ** -0.5
    pad = ((0, 0), (0, 0), (0, s_pad - S), (0, 0))
    k_blocks = jnp.pad(k, pad).reshape(B, H, nb, MOBA_BLOCK, d)
    v_blocks = jnp.pad(v, pad).reshape(B, H, nb, MOBA_BLOCK, d)
    k_mean = jnp.mean(k_blocks.astype(jnp.float32), axis=3)
    qpos = jnp.arange(S)
    gate = jnp.einsum('bhsd,bhnd->bhsn', q.astype(jnp.float32), k_mean)
    past = jnp.arange(nb)[None, :] < (qpos // MOBA_BLOCK)[:, None]
    gate = jnp.where(past, gate, -jnp.inf)
    _, sel = lax.top_k(gate, n_sel)

    nc = S // MOBA_Q_CHUNK
    q_c = q.reshape(B, H, nc, MOBA_Q_CHUNK, d).transpose(2, 0, 1, 3, 4)
    sel_c = sel.reshape(B, H, nc, MOBA_Q_CHUNK, n_sel).transpose(2, 0, 1, 3, 4)
    starts = jnp.arange(nc, dtype=jnp.int32) * MOBA_Q_CHUNK
    table_t = t5_table.T
    b_ix = jnp.arange(B)[:, None, None, None]
    h_ix = jnp.arange(H)[None, :, None, None]
    offs = jnp.arange(MOBA_BLOCK)

    def step(blk):
        q_i, sel_i, t0 = blk
        own = t0 // MOBA_BLOCK
        qp = t0 + jnp.arange(MOBA_Q_CHUNK)
        k_g = k_blocks[b_ix, h_ix, sel_i]
        v_g = v_blocks[b_ix, h_ix, sel_i]
        kp_sel = sel_i[..., None] * MOBA_BLOCK + offs
        bias_sel = table_t[h_ix[..., None], t5_bucket(qp[:, None, None] - kp_sel)]
        s_sel = jnp.einsum('bhqd,bhqnkd->bhqnk', q_i, k_g).astype(jnp.float32) * scale + bias_sel
        s_sel = jnp.where((sel_i < own)[..., None], s_sel, -jnp.inf)
        k_own = lax.dynamic_index_in_dim(k_blocks, own, axis=2, keepdims=False)
        v_own = lax.dynamic_index_in_dim(v_blocks, own, axis=2, keepdims=False)
        dist_own = qp[:, None] - (own * MOBA_BLOCK + offs)[None, :]
        s_own = (jnp.einsum('bhqd,bhkd->bhqk', q_i, k_own).astype(jnp.float32) * scale
                 + table_t[:, t5_bucket(dist_own)])
        s_own = jnp.where(dist_own >= 0, s_own, -jnp.inf)
        n_flat = n_sel * MOBA_BLOCK
        s = jnp.concatenate([s_sel.reshape(B, H, MOBA_Q_CHUNK, n_flat), s_own], axis=-1)
        p = jax.nn.softmax(s, axis=-1).astype(v.dtype)
        p_sel = p[..., :n_flat].reshape(B, H, MOBA_Q_CHUNK, n_sel, MOBA_BLOCK)
        p_own = p[..., n_flat:]
        return (jnp.einsum('bhqnk,bhqnkd->bhqd', p_sel, v_g)
                + jnp.einsum('bhqk,bhkd->bhqd', p_own, v_own))

    out = lax.map(step, (q_c, sel_c, starts))
    return out.transpose(1, 2, 0, 3, 4).reshape(B, H, S, d)

def hybrid_mixer(h, w_in, b_forget, g_q_lat, w_uq, g_kv_lat, w_ukv, g_group, w_out, t5_table):
    B, S, _ = h.shape
    proj = h @ w_in
    split_points = np.cumsum(IN_SIZES)[:-1].tolist()
    q_f, k_f, v_f, f_logit, q_m, k_m, v_m, c_q, c_kv, k_r = jnp.split(proj, split_points, axis=-1)

    def heads(t, n):
        return t.reshape(B, S, n, -1).transpose(0, 2, 1, 3)

    def flat(o):
        return o.transpose(0, 2, 1, 3).reshape(B, S, -1)

    pos = jnp.arange(S)
    log_f = jax.nn.log_sigmoid((f_logit + b_forget).astype(jnp.float32))
    F = jnp.cumsum(log_f, axis=1).transpose(0, 2, 1)
    o_f = dense_causal_attention(heads(q_f, FOX_HEADS), heads(k_f, FOX_HEADS), heads(v_f, FOX_HEADS), F)
    o_m = moba_attention(heads(q_m, MOBA_HEADS), heads(k_m, MOBA_HEADS), heads(v_m, MOBA_HEADS), t5_table)
    q_lat = heads(rmsnorm(c_q, g_q_lat) @ w_uq, MLA_HEADS)
    q_nope, q_rot = q_lat[..., :MLA_NOPE_DIM], q_lat[..., MLA_NOPE_DIM:]
    kv = heads(rmsnorm(c_kv, g_kv_lat) @ w_ukv, MLA_HEADS)
    k_nope, v_c = kv[..., :MLA_NOPE_DIM], kv[..., MLA_NOPE_DIM:]
    k_rot = rope(k_r[:, None], pos)
    q_c = jnp.concatenate([q_nope, rope(q_rot, pos)], axis=-1)
    k_c = jnp.concatenate([k_nope, jnp.broadcast_to(k_rot, (B, MLA_HEADS, S, MLA_ROPE_DIM))], axis=-1)
    o_c = dense_causal_attention(q_c, k_c, v_c)
    g_a, g_b, g_c = jnp.split(g_group, [FOX_W, FOX_W + MOBA_W])
    o = jnp.concatenate([rmsnorm(flat(o_f), g_a), rmsnorm(flat(o_m), g_b), rmsnorm(flat(o_c), g_c)], axis=-1)
    return o @ w_out

def swiglu(h, w_gate_up, w_down):
    g, u = jnp.split(h @ w_gate_up, 2, axis=-1)
    return (jax.nn.silu(g) * u) @ w_down

def first_inputs(seed: int = 0) -> dict:
    key = jax.random.key(seed)
    ks = jax.random.split(key, 20)
    f32 = jnp.float32

    def nrm(k, shape, scale):
        return jax.random.normal(k, shape, f32) * scale

    def gain(k, shape):
        return 1.0 + 0.1 * jax.random.normal(k, shape, f32)

    L = DEPTH
    return {
        'x': nrm(ks[0], (BATCH, SEQ, D_MODEL), 1.0),
        'c': nrm(ks[1], (BATCH, D_MODEL), 1.0),
        't5_table': nrm(ks[2], (T5_BUCKETS, MOBA_HEADS), 0.5),
        'w_ada': nrm(ks[3], (L, D_MODEL, 6 * D_MODEL), D_MODEL ** -0.5),
        'b_ada': nrm(ks[4], (L, 6 * D_MODEL), 0.02),
        'g_mix_pre': gain(ks[5], (L, D_MODEL)),
        'g_mix_post': gain(ks[6], (L, D_MODEL)),
        'w_in': nrm(ks[7], (L, D_MODEL, IN_WIDTH), D_MODEL ** -0.5),
        'b_forget': 2.0 + 0.5 * jax.random.normal(ks[8], (L, FOX_HEADS), f32),
        'g_q_lat': gain(ks[9], (L, MLA_Q_RANK)),
        'w_uq': nrm(ks[10], (L, MLA_Q_RANK, MLA_HEADS * (MLA_NOPE_DIM + MLA_ROPE_DIM)), MLA_Q_RANK ** -0.5),
        'g_kv_lat': gain(ks[11], (L, MLA_KV_RANK)),
        'w_ukv': nrm(ks[12], (L, MLA_KV_RANK, MLA_HEADS * (MLA_NOPE_DIM + MLA_V_DIM)), MLA_KV_RANK ** -0.5),
        'g_group': gain(ks[13], (L, MIX_WIDTH)),
        'w_out': nrm(ks[14], (L, MIX_WIDTH, D_MODEL), MIX_WIDTH ** -0.5),
        'g_ffn_pre': gain(ks[15], (L, D_MODEL)),
        'g_ffn_post': gain(ks[16], (L, D_MODEL)),
        'w_gate_up': nrm(ks[17], (L, D_MODEL, 2 * D_FF), D_MODEL ** -0.5),
        'w_down': nrm(ks[18], (L, D_FF, D_MODEL), D_FF ** -0.5),
    }

def first_block(x, c, t5_table, w_ada, b_ada, g_mix_pre, g_mix_post, w_in, b_forget, g_q_lat, w_uq,
              g_kv_lat, w_ukv, g_group, w_out, g_ffn_pre, g_ffn_post, w_gate_up, w_down):
    c_act = jax.nn.silu(c)
    for l in range(DEPTH):
        mod = (c_act @ w_ada[l] + b_ada[l])[:, None, :]
        shift_a, scale_a, gate_a, shift_f, scale_f, gate_f = jnp.split(mod, 6, axis=-1)
        h = rmsnorm(x, g_mix_pre[l]) * (1.0 + scale_a) + shift_a
        y = hybrid_mixer(h, w_in[l], b_forget[l], g_q_lat[l], w_uq[l], g_kv_lat[l], w_ukv[l],
                         g_group[l], w_out[l], t5_table)
        x = x + gate_a * rmsnorm(y, g_mix_post[l])
        h = rmsnorm(x, g_ffn_pre[l]) * (1.0 + scale_f) + shift_f
        x = x + gate_f * rmsnorm(swiglu(h, w_gate_up[l], w_down[l]), g_ffn_post[l])
    return x


DEPTH_2 = 4

CHUNK = 64
N_MIXERS = 3
NORM_EPS = 1e-6
N_SUBLAYER_NORMS = 6

HG_EXPAND = 128
HG_HEADS = D_MODEL // HG_EXPAND
HG_F_DIM = HG_HEADS * HG_EXPAND
HG_V_DIM = D_MODEL // HG_HEADS
HG_BLOCK = 16
HG_MID = HG_BLOCK // 2

DA_HEAD_DIM = 64
DA_HEADS = D_MODEL // (2 * DA_HEAD_DIM)
DA_Q_BLOCK = 128

POOL_WINDOWS = (2, 4, 8, 16)
POOL_GROUPS = len(POOL_WINDOWS)
POOL_GROUP_DIM = D_MODEL // POOL_GROUPS

D_FF_2 = 2816

N_A = (DEPTH_2 + 2) // 3
N_B = (DEPTH_2 + 1) // 3
N_C = DEPTH_2 // 3


def rmsnorm_2(x, w):
    xf = x.astype(jnp.float32)
    y = xf * lax.rsqrt(jnp.mean(xf * xf, axis=-1, keepdims=True) + NORM_EPS)
    return (y * w.astype(jnp.float32)).astype(x.dtype)

def swiglu_2(x, w_in, w_out):
    g, u = jnp.split(x @ w_in, 2, axis=-1)
    return (jax.nn.silu(g) * u) @ w_out

def alibi_slopes(n_heads):
    return jnp.exp2(-8.0 * jnp.arange(1, n_heads + 1, dtype=jnp.float32) / n_heads)

def hgrn_lower_bound(lb_raw, layer):
    p = jax.nn.softmax(lb_raw.astype(jnp.float32), axis=0)
    return jnp.cumsum(p, axis=0)[layer] - p[0]

def hgrn2_mixer(x, w_in, gnorm_w, w_out, lb):
    f32 = jnp.float32
    B, S, _ = x.shape
    nb = S // HG_BLOCK
    q, f_pre, i_in, g = jnp.split(
        x @ w_in, [HG_F_DIM, 2 * HG_F_DIM, 2 * HG_F_DIM + D_MODEL], axis=-1)
    f = lb + (1.0 - lb) * jax.nn.sigmoid(f_pre.astype(f32))
    k = 1.0 - f
    log_f = jnp.log(f)

    def heads(t, dim):
        return t.reshape(B, nb, HG_BLOCK, HG_HEADS, dim).transpose(0, 3, 1, 2, 4)

    qh = heads(q.astype(f32), HG_EXPAND)
    kh = heads(k, HG_EXPAND)
    vh = heads(i_in.astype(f32), HG_V_DIM)
    b = jnp.cumsum(heads(log_f, HG_EXPAND), axis=3)
    b_last = b[:, :, :, -1:, :]
    b_mid = b[:, :, :, HG_MID:HG_MID + 1, :]

    q_r = qh * jnp.exp(b - b_mid)
    k_r = kh * jnp.exp(b_mid - b)
    causal = jnp.tril(jnp.ones((HG_BLOCK, HG_BLOCK), dtype=bool))
    a = jnp.where(causal, jnp.einsum('bhntk,bhnsk->bhnts', q_r, k_r), 0.0)
    o_intra = jnp.einsum('bhnts,bhnsv->bhntv', a, vh)

    q_inter = qh * jnp.exp(b)
    k_state = kh * jnp.exp(b_last - b)
    decay = jnp.exp(b_last[:, :, :, 0, :])

    def step(state, xs):
        qi, ks, vs, dec = xs
        o = jnp.einsum('bhtk,bhkv->bhtv', qi, state)
        state = state * dec[..., None] + jnp.einsum('bhtk,bhtv->bhkv', ks, vs)
        return state, o

    xs = (jnp.moveaxis(q_inter, 2, 0), jnp.moveaxis(k_state, 2, 0),
          jnp.moveaxis(vh, 2, 0), jnp.moveaxis(decay, 2, 0))
    s0 = jnp.zeros((B, HG_HEADS, HG_EXPAND, HG_V_DIM), f32)
    _, o_inter = lax.scan(step, s0, xs)

    o = o_intra + jnp.moveaxis(o_inter, 0, 2)
    o = o.transpose(0, 2, 3, 1, 4).reshape(B, S, HG_HEADS, HG_V_DIM)
    gate = jax.nn.silu(g.astype(f32).reshape(B, S, HG_HEADS, HG_V_DIM))
    o = rmsnorm_2(o, gnorm_w) * gate
    return o.reshape(B, S, D_MODEL).astype(x.dtype) @ w_out

def diff_attention(x, w_in, lam, subln_w, w_out, layer):
    f32 = jnp.float32
    B, S, _ = x.shape
    H, dh = DA_HEADS, DA_HEAD_DIM
    q, k, v = jnp.split(x @ w_in, 3, axis=-1)
    q = q.reshape(B, S, H, 2, dh).transpose(0, 2, 3, 1, 4)
    k = k.reshape(B, S, H, 2, dh).transpose(0, 2, 3, 1, 4)
    v = v.reshape(B, S, H, 2 * dh).transpose(0, 2, 1, 3)

    lam_init = 0.8 - 0.6 * math.exp(-0.3 * layer)
    lam_f = lam.astype(f32)
    lam_full = (jnp.exp(jnp.sum(lam_f[0] * lam_f[1]))
                - jnp.exp(jnp.sum(lam_f[2] * lam_f[3])) + lam_init)
    slopes = alibi_slopes(H)
    scale = dh ** -0.5
    n_qb = S // DA_Q_BLOCK
    q_blocks = q.reshape(B, H, 2, n_qb, DA_Q_BLOCK, dh).transpose(3, 0, 1, 2, 4, 5)
    key_pos = jnp.arange(S)

    def block(args):
        qb, start = args
        q_pos = start + jnp.arange(DA_Q_BLOCK)
        s = jnp.einsum('bhgqd,bhgkd->bhgqk', qb, k).astype(f32) * scale
        dist = jnp.abs(q_pos[:, None] - key_pos[None, :]).astype(f32)
        allowed = (key_pos[None, :] // CHUNK) <= (q_pos[:, None] // CHUNK)
        s = s - slopes[None, :, None, None, None] * dist
        p = jax.nn.softmax(jnp.where(allowed, s, -jnp.inf), axis=-1)
        w = p[:, :, 0] - lam_full * p[:, :, 1]
        return jnp.einsum('bhqk,bhkv->bhqv', w.astype(v.dtype), v)

    starts = jnp.arange(n_qb, dtype=jnp.int32) * DA_Q_BLOCK
    o = lax.map(block, (q_blocks, starts))
    o = o.transpose(1, 0, 3, 2, 4).reshape(B, S, H, 2 * dh)
    o = rmsnorm_2(o, subln_w) * (1.0 - lam_init)
    return o.reshape(B, S, D_MODEL) @ w_out

def pool_mixer(x, w_in, w_group, scale, w_out):
    f32 = jnp.float32
    B, S, _ = x.shape
    u = (x @ w_in).astype(f32).reshape(B, S, POOL_GROUPS, POOL_GROUP_DIM)
    csum = jnp.cumsum(u, axis=1)
    count_pos = jnp.arange(S)
    outs = []
    for g_idx, w in enumerate(POOL_WINDOWS):
        cs = csum[:, :, g_idx]
        lag = jnp.pad(cs[:, :S - w], ((0, 0), (w, 0), (0, 0)))
        count = jnp.minimum(count_pos + 1, w).astype(f32)
        mean = (cs - lag) / count[None, :, None]
        outs.append(mean - u[:, :, g_idx])
    p = jnp.stack(outs, axis=2)
    y = jnp.einsum('bsgc,gcd->bsgd', p, w_group.astype(f32))
    y = y * scale.astype(f32).reshape(POOL_GROUPS, POOL_GROUP_DIM)
    return y.reshape(B, S, D_MODEL).astype(x.dtype) @ w_out

def second_inputs(seed: int = 0) -> dict:
    key = jax.random.key(seed)
    ks = jax.random.split(key, 18)
    f32 = jnp.float32

    def dense(k, shape, fan_in):
        return jax.random.normal(k, shape, f32) * fan_in ** -0.5

    def gain(k, shape, s=0.05):
        return 1.0 + s * jax.random.normal(k, shape, f32)

    G, C = POOL_GROUPS, POOL_GROUP_DIM
    return {
        "x": jax.random.normal(ks[0], (BATCH, SEQ, D_MODEL), f32),
        "norm_gains": gain(ks[1], (DEPTH_2, N_SUBLAYER_NORMS, D_MODEL)),
        "ffn1_w_in": dense(ks[2], (DEPTH_2, D_MODEL, 2 * D_FF_2), D_MODEL),
        "ffn1_w_out": dense(ks[3], (DEPTH_2, D_FF_2, D_MODEL), D_FF_2),
        "ffn2_w_in": dense(ks[4], (DEPTH_2, D_MODEL, 2 * D_FF_2), D_MODEL),
        "ffn2_w_out": dense(ks[5], (DEPTH_2, D_FF_2, D_MODEL), D_FF_2),
        "hgrn_w_in": dense(ks[6], (N_A, D_MODEL, 2 * HG_F_DIM + 2 * D_MODEL), D_MODEL),
        "hgrn_gnorm": gain(ks[7], (N_A, HG_V_DIM)),
        "hgrn_w_out": dense(ks[8], (N_A, D_MODEL, D_MODEL), D_MODEL),
        "hgrn_lb_raw": 0.5 * jax.random.normal(ks[9], (DEPTH_2, HG_F_DIM), f32),
        "diff_w_in": dense(ks[10], (N_B, D_MODEL, 3 * D_MODEL), D_MODEL),
        "diff_lambda": 0.1 * jax.random.normal(ks[11], (N_B, 4, DA_HEAD_DIM), f32),
        "diff_subln": gain(ks[12], (N_B, 2 * DA_HEAD_DIM)),
        "diff_w_out": dense(ks[13], (N_B, D_MODEL, D_MODEL), D_MODEL),
        "pool_w_in": dense(ks[14], (N_C, D_MODEL, D_MODEL), D_MODEL),
        "pool_w_group": dense(ks[15], (N_C, G, C, C), C),
        "pool_scale": gain(ks[16], (N_C, D_MODEL), 0.1),
        "pool_w_out": dense(ks[17], (N_C, D_MODEL, D_MODEL), D_MODEL),
    }

def second_block(x, norm_gains, ffn1_w_in, ffn1_w_out, ffn2_w_in, ffn2_w_out,
              hgrn_w_in, hgrn_gnorm, hgrn_w_out, hgrn_lb_raw,
              diff_w_in, diff_lambda, diff_subln, diff_w_out,
              pool_w_in, pool_w_group, pool_scale, pool_w_out):
    h = x
    for i in range(DEPTH_2):
        kind, j = i % N_MIXERS, i // N_MIXERS
        gn = norm_gains[i]
        h = h + 0.5 * rmsnorm_2(swiglu_2(rmsnorm_2(h, gn[0]), ffn1_w_in[i], ffn1_w_out[i]), gn[1])
        hn = rmsnorm_2(h, gn[2])
        if kind == 0:
            lb = hgrn_lower_bound(hgrn_lb_raw, i)
            m = hgrn2_mixer(hn, hgrn_w_in[j], hgrn_gnorm[j], hgrn_w_out[j], lb)
        elif kind == 1:
            m = diff_attention(hn, diff_w_in[j], diff_lambda[j], diff_subln[j], diff_w_out[j], i)
        else:
            m = pool_mixer(hn, pool_w_in[j], pool_w_group[j], pool_scale[j], pool_w_out[j])
        h = h + rmsnorm_2(m, gn[3])
        h = h + 0.5 * rmsnorm_2(swiglu_2(rmsnorm_2(h, gn[4]), ffn2_w_in[i], ffn2_w_out[i]), gn[5])
    return h


def setup_inputs(seed=0):
    out = dict(first_inputs(seed))
    for name, value in second_inputs(seed + 1).items():
        if name != "x":
            out[name + "_2"] = value
    return out


def reference(
    x, c, t5_table, w_ada, b_ada, g_mix_pre, g_mix_post, w_in, b_forget, g_q_lat, w_uq,
    g_kv_lat, w_ukv, g_group, w_out, g_ffn_pre, g_ffn_post, w_gate_up, w_down, norm_gains_2,
    ffn1_w_in_2, ffn1_w_out_2, ffn2_w_in_2, ffn2_w_out_2, hgrn_w_in_2, hgrn_gnorm_2,
    hgrn_w_out_2, hgrn_lb_raw_2, diff_w_in_2, diff_lambda_2, diff_subln_2, diff_w_out_2,
    pool_w_in_2, pool_w_group_2, pool_scale_2, pool_w_out_2,
):
    x = first_block(
        x, c, t5_table, w_ada, b_ada, g_mix_pre, g_mix_post, w_in, b_forget, g_q_lat, w_uq,
        g_kv_lat, w_ukv, g_group, w_out, g_ffn_pre, g_ffn_post, w_gate_up, w_down,
    )
    return second_block(
        x, norm_gains_2, ffn1_w_in_2, ffn1_w_out_2, ffn2_w_in_2, ffn2_w_out_2, hgrn_w_in_2,
        hgrn_gnorm_2, hgrn_w_out_2, hgrn_lb_raw_2, diff_w_in_2, diff_lambda_2, diff_subln_2,
        diff_w_out_2, pool_w_in_2, pool_w_group_2, pool_scale_2, pool_w_out_2,
    )


_drawn_inputs = setup_inputs


def setup_inputs(seed=0):
    import zlib

    import numpy as np

    out = dict(_drawn_inputs(seed))
    spreads = {}
    factors = {}
    for name, (base, spread) in spreads.items():
        noise = np.random.default_rng([zlib.crc32(name.encode()), seed]).standard_normal(out[name].shape)
        drawn = base * np.exp(spread * noise) if base else spread * noise
        out[name] = __import__('jax').numpy.asarray(drawn.astype(out[name].dtype))
    for name, factor in factors.items():
        out[name] = (out[name] * factor).astype(out[name].dtype)
    return out
```

```python
from contextlib import ExitStack, contextmanager

import numpy as np

import concourse.bass as bass
from concourse import mybir

F32 = mybir.dt.float32
F32R = mybir.dt.float32r
U32 = mybir.dt.uint32
ALU = mybir.AluOpType
ACT = mybir.ActivationFunctionType
AXX = mybir.AxisListType.X

P = 128
S = 256
NT = S // P
D = 1024
KD = D // P
LAYERS = 2
FF = 2816
CH = 256
NCH = FF // CH
UNIT = 2080
RING = 3
EPS = 1e-6
NEG = -1e30
BIG = 3e38
HD = 64
IN_W = 1956
FOX_Q, FOX_K, FOX_V, MOBA_Q, MOBA_K, MOBA_V, C_Q, C_KV = 0, 256, 512, 772, 1028, 1284, 1540, 1796
ROPE = 32
MLA_QK = HD + ROPE
MLA_H = 8
HB = 16
NHB = P // HB
ADA_W = 2 * D
T5_W = 384
POOL_WINDOWS = (2, 4, 8, 16)
DIFF_LAYER, DIFF_H = 1, 8

LAYER_UNITS = (3 * KD + 15 + 3 * NCH, 15 + 3 * NCH)
STEP_UNITS = (3, 3)


def constants():
    p = np.arange(P)
    f = np.float32
    c = {}
    c["ident"] = np.eye(P, dtype=f)
    c["tri"] = np.stack([(t * P + p[:, None] <= np.arange(S)[None]) for t in range(NT)], 1).astype(f).reshape(P, -1)
    dist = P + p[:, None] - np.arange(S)[None]
    c["causal"] = np.where(dist >= 0, 0, NEG).astype(f)
    chunk = (np.arange(S)[None] // 64) <= ((P + p[:, None]) // 64)
    c["chunk_dist"] = np.where(chunk, np.abs(dist), 1e33).astype(f)
    half = ROPE // 2
    inv = (f(1.0) / (f(10000.0) ** (np.arange(half, dtype=f) / f(half)))).astype(f)
    ang = np.arange(S, dtype=f)[:, None] * inv[None]
    for n, fn in (("cos", np.cos), ("sin", np.sin)):
        c[n] = fn(ang).astype(f).reshape(NT, P, half).transpose(1, 0, 2).reshape(P, -1)
    d = (S - 1) - np.arange(T5_W)
    n = np.maximum(d, 0)
    large = 16 + (np.log(np.maximum(n, 16).astype(f) / f(16)) / f(np.log(8.0)) * f(16)).astype(np.int32)
    bucket = np.where(n < 16, n, np.minimum(large, 31))
    hot = np.zeros((P, T5_W), f)
    hot[np.where(d >= 0, bucket, 32), np.arange(T5_W)] = 1
    c["bucket"] = hot
    c["first"] = np.stack([p == 0, p < 0], 1).astype(f)
    c["scan"] = np.tile((np.arange(2 * S) % HB != 0).astype(f), (P, 1))
    c["block"] = (p[:, None] // HB == np.arange(NHB)[None]).astype(f)
    s, t = p[:, None], p[None]
    c["intra"] = np.tile(((s <= t) & (s // HB == t // HB)), (1, 4)).astype(f)
    c["counts"] = np.tile(np.concatenate([1.0 / np.minimum(np.arange(S) + 1, w) for w in POOL_WINDOWS]), (P, 1)).astype(f)
    return c


class Steps:

    def __init__(self, eng, own, apart, table, per, trips, start=()):
        self.eng, self.own, self.nobody, self.table, self.per, self.trips = eng, own, apart, table, per, trips
        self.count = dict(start)
        self.loops = []
        self.r = self.n = 0

    def step(self, name, sem=None, by=1):
        sem = sem or self.own
        key = sem.name
        self.count[key] = self.count.get(key, 0) + by
        if name:
            self.table[name] = (sem, self.count[key], tuple(i for i, _, _ in self.loops))
        return by

    def alias(self, other, name):
        self.table[other] = self.table[name]

    def sem_of(self, name):
        return self.table[name][0] if name in self.table else self.own

    def at(self, name, back=0):
        if name not in self.table:
            return 1
        sem, value, where = self.table[name]
        mine = {i: reg for i, reg, _ in self.loops}
        for i in where:
            if i not in mine:
                value += (self.trips[i] - 1) * self.per.get((i, sem.name), 0)
        if back:
            value -= back * self.per.get((self.loops[-1][0], sem.name), 0)
        for i in where:
            if i in mine:
                value = mine[i] * self.per.get((i, sem.name), 0) + value
        return value

    def units(self, value, which, ring=None):
        for i, reg, units in self.loops:
            value = reg * (16 * units[which] // ring if ring else units[which]) + value
        return value

    def apart(self):
        if self.loops:
            self.eng.sem_inc(self.nobody, 1)

    @contextmanager
    def loop(self, name, turns, units):
        self.trips[name] = turns
        before, r, n = dict(self.count), self.r, self.n
        with self.eng.Fori(0, turns) as i:
            self.loops.append((name, i, units))
            yield i
            self.loops.pop()
        assert (self.r - r, self.n - n) == units
        self.r, self.n = r + turns * units[0], n + turns * units[1]
        for key, c in self.count.items():
            one = c - before.get(key, 0)
            self.per[name, key] = one
            self.count[key] = c + (turns - 1) * one


def program(nc, A, out, table, per, trips):
    ctx = ExitStack()
    with ctx:
        def sb(name, shape, dt=F32):
            return ctx.enter_context(nc.sbuf_tensor(name, shape, dt))

        x = sb("x", [P, NT, D])
        xn = sb("xn", [P, NT, D])
        tmp = sb("tmp", [P, D])
        junk = sb("junk", [P, D], mybir.dt.bfloat16)
        raw = [sb(f"raw{i}", [P, UNIT]) for i in range(RING)]
        w_hi = [sb(f"w_hi{i}", [P, UNIT], F32R) for i in range(RING)]
        w_lo = [sb(f"w_lo{i}", [P, UNIT], F32R) for i in range(RING)]
        h_hi = sb("h_hi", [P, KD, S], F32R)
        h_lo = sb("h_lo", [P, KD, S], F32R)
        a_hi = sb("a_hi", [P, 3, S], F32R)
        a_lo = sb("a_lo", [P, 3, S], F32R)
        ident = sb("ident", [P, P])
        ones = sb("ones", [P, P])
        stat = sb("stat", [P, 4, 8])
        half_power = sb("half_power", [P, 8])
        post = [sb(f"post{i}", [P, D]) for i in range(2)]
        rows = sb("rows", [P, P])
        col = sb("col", [P, 180])
        M = sb("M", [P, 19850])
        at = [0]

        def m(shape):
            n = int(np.prod(shape))
            v = M[:, at[0]:at[0] + n]
            at[0] += n
            assert at[0] <= M.shape[1], at[0]
            names = "abcd"[:len(shape)]
            if len(shape) == 1:
                return v
            return v.rearrange(f"p ({' '.join(names)}) -> p {' '.join(names)}", **dict(zip(names[1:], shape[1:])))

        C_MIX, C_FFN, C_GROUP, C_QLAT, C_KVLAT, C_C = 0, 8, 16, 24, 26, 27
        C_MIXA, C_MIXB, C_FFNA, C_FFNB = 40, 48, 56, 64
        C_SUB = 0
        C_LB, C_GN, C_SUBLN, C_PSCALE, C_LBV, C_OML, C_SUBS = 96, 128, 130, 131, 140, 156, 172

        B = [ctx.enter_context(nc.psum_tensor(f"B{i}", [P, 512], F32)) for i in range(4)]
        Yt = ctx.enter_context(nc.psum_tensor("Y", [P, NT, D], F32))
        B += [Yt[:, i // 2, (i % 2) * 512:(i % 2) * 512 + 512] for i in range(4)]
        B = [b[:, :] for b in B]

        def sem(name):
            return ctx.enter_context(nc.semaphore(name))

        tensor_step, scalar_step = sem("tensor_step"), sem("scalar_step")
        vector_step, gpsimd_step = sem("vector_step"), sem("gpsimd_step")
        unit_loaded = [sem(f"unit_loaded{i}") for i in range(RING)]
        unit_rounded = sem("unit_rounded")
        unit_split = sem("unit_split")
        unit_multiplied = sem("unit_multiplied")
        inputs_loaded, vectors_loaded, bias_loaded = sem("inputs_loaded"), sem("vectors_loaded"), sem("bias_loaded")
        post_gain_loaded = [sem(f"post_gain_loaded{i}") for i in range(2)]
        t5_moved, output_stored = sem("t5_moved"), sem("output_stored")
        nobody_waits = sem("nobody_waits")

        def steps(eng, own, start=()):
            return Steps(eng, own, nobody_waits, table, per, trips, start)

        skew = nc.dram_tensor("skew", (4, P * (T5_W + 1)), F32, kind="Internal").ap()

        block = ctx.enter_context(nc.Block())

        def shape3(v, k):
            return v.rearrange("p (k n) -> p k n", k=k)

        acc = m([ADA_W])
        tri = m([NT, S])
        causal = m([S])
        cs = m([2, NT, ROPE // 2])
        bforget = m([4])
        firstc = m([2])
        t5_bias = m([4, S])
        qf, kf, qm, km = m([2, S]), m([4, S]), m([2, S]), m([4, S])
        vfm = m([NT, 512])
        lat = m([NT, 420])
        logf = m([NT, 4]); fa = m([NT, 4, 2]); fb = m([NT, 4, 2]); ft = m([2, NT, 4])
        FQ = tmp[:, :].rearrange("p (h s) -> p h s", h=4)
        FK = xn[:, :, 0:512].rearrange("p t (h s) -> p t h s", h=2)
        qlat = m([NT, MLA_H, MLA_QK]); klat = m([NT, MLA_H, MLA_QK]); vc = m([NT, 512])
        rot = [xn[:, i // 2, 512 + (i % 2) * 256:768 + (i % 2) * 256] for i in range(4)]
        krot = m([NT, ROPE])
        qcT, kcT = m([MLA_H, S]), m([MLA_H, S])
        bucket = kcT[:, 0:2, :].rearrange("p a b -> p (a b)")[:, 0:T5_W]
        t5_lhs = qf.rearrange("p a b -> p (a b)")
        t5_rows = klat.rearrange("p a b c -> p (a b c)").rearrange("p (h j) -> p h j", h=4)
        ssb, pb, pT = m([2, S]), m([2, S]), m([2, S])
        stats = m([4, 32])
        osb = xn
        at[0] = 0
        scan_mask = m([2 * S]); intra = m([4 * P]); blockm = m([NHB])
        hv, hg = m([NT, D]), m([KD, S])
        hq, hf, hk, hl = (m([2, S]) for _ in range(4))
        hb = hf
        osq, hd = (tmp[:, i * 512:i * 512 + 512].rearrange("p (a b) -> p a b", a=2) for i in range(2))
        oms = osq
        q_r, k_r, q_i, k_s, e_b = ([m([2, S]) for _ in range(2)] for _ in range(5))
        ksT, atm = m([4, P]), m([4, P])
        vmask = [m([NHB, P]) for _ in range(2)]
        hist = [m([2 * NHB, P]) for _ in range(2)]
        ho = xn[:, :, :].rearrange("p t n -> p (t n)").rearrange("p (h s) -> p h s", h=KD)
        at[0] = 0
        dbias = m([DIFF_H, S])
        cdist = m([S])
        dq, dk = m([DIFF_H, S]), m([2 * DIFF_H, S])
        dv = m([NT, D])
        dss, dp = m([4, S]), m([4, S])
        dt1, dw = m([2, S]), m([2, S])
        dpT = m([2, S])
        dstat = m([4, 32])
        lamrow = m([4, HD])
        lam2 = m([16])
        do = xn
        at[0] = 0
        counts = m([4, S])
        pu = m([KD, S])
        ps_a = [m([2, S]) for _ in range(2)]
        ppT = m([KD, S])

        def cols(w, c0, n):
            return w[:, c0:c0 + n].rearrange("(k p) n -> p k n", p=P)

        def wrows(w, r0, k):
            return w[r0:r0 + k * P, :].rearrange("(k p) n -> p k n", p=P)

        hgrn_units = [(g * D + c * CH) for c in range(4) for g in (0, 1, 3, 2)]

        def gains(p):
            if p in "MF":
                a, b = {"M": (C_MIXA, C_MIXB), "F": (C_FFNA, C_FFNB)}[p]
                return (lambda k: col[:, a + k:a + k + 1]), (lambda k: col[:, b + k:b + k + 1])
            c = C_SUB + (3 * int(p[0]) + "amb".index(p[1])) * KD
            return (lambda k: col[:, c + k:c + k + 1]), None

        def attention_jobs():
            js = [(kind, h, t) for kind, n in (("fox", 4), ("moba", 4), ("mla", MLA_H)) for h in range(n)
                  for t in range(NT)]
            return [(*j, s) for s, j in enumerate(js)]

        @block.sync
        def _(sp):
            st = steps(sp, output_stored)

            def load(src, k=KD):
                slot = st.r % RING
                sp.wait_ge(unit_split, st.units(st.r + 1, 0))
                st.apart()
                n = src.shape[-1]
                sp.dma_start(shape3(raw[slot][:, 0:k * n], k) if k > 1 else raw[slot][:, 0:n], src)\
                    .then_inc(unit_loaded[slot], 16)
                st.r += 1
                st.n += 1

            def layer(t, l):
                return t[bass.ds(l, 1), :, :].rearrange("a k n -> (a k) n")

            def ada(l, third):
                for k in range(KD):
                    load(layer(A["w_ada"], l)[k * P:k * P + P, third * ADA_W:third * ADA_W + ADA_W], 1)
                    st.n -= 1

            def ffn(p, wgu, wdn):
                def gate(i):
                    load(wgu[:, bass.ds(i * CH, CH)].rearrange("(k p) n -> p k n", p=P))

                def up(i):
                    load(wgu[:, bass.ds(i * CH + FF, CH)].rearrange("(k p) n -> p k n", p=P))

                def down(i):
                    load(wdn[bass.ds(i * CH, CH), :].rearrange("(k p) n -> p k n", p=P), 2)

                gate(0)
                up(0)
                gate(1)
                up(1)
                down(0)
                with st.loop(p, NCH - 3, STEP_UNITS) as j:
                    gate(j + 2)
                    up(j + 2)
                    down(j + 1)
                gate(NCH - 1)
                up(NCH - 1)
                down(NCH - 2)
                down(NCH - 1)

            def out_rows(w):
                for u in range(4):
                    load(wrows(w, u * 2 * P, 2), 2)

            with st.loop("layers", LAYERS, LAYER_UNITS) as l:
                w_in, w_ukv = layer(A["w_in"], l), layer(A["w_ukv"], l)
                ada(l, 0)
                load(cols(w_in, C_Q, CH))
                load(cols(w_in, C_KV, IN_W - C_KV))
                load(cols(w_in, FOX_V, CH + 4))
                for c in (FOX_Q, FOX_K, MOBA_Q, MOBA_K, MOBA_V):
                    load(cols(w_in, c, CH))
                load(wrows(layer(A["w_uq"], l), 0, 2), 2)
                for c in range(2):
                    load(w_ukv[:, c * 512:c * 512 + 512], 1)
                ada(l, 1)
                ada(l, 2)
                out_rows(layer(A["w_out"], l))
                ffn("F", layer(A["w_gate_up"], l), layer(A["w_down"], l))
            for i in range(4):
                ffn(f"{i}a", A["ffn1_w_in_2"][i], A["ffn1_w_out_2"][i])
                if i % 3 == 0:
                    for c in hgrn_units:
                        load(cols(A["hgrn_w_in_2"][i // 3], c, CH))
                    out_rows(A["hgrn_w_out_2"][i // 3])
                elif i == DIFF_LAYER:
                    for c in range(12):
                        load(cols(A["diff_w_in_2"][0], c * CH, CH))
                    out_rows(A["diff_w_out_2"][0])
                else:
                    for c in range(4):
                        load(cols(A["pool_w_in_2"][0], c * CH, CH))
                    load(A["pool_w_group_2"][0].rearrange("g (k p) n -> p (g k) n", p=P))
                    out_rows(A["pool_w_out_2"][0])
                ffn(f"{i}b", A["ffn2_w_in_2"][i], A["ffn2_w_out_2"][i])
            for t in range(NT):
                sp.wait_ge(vector_step, st.at(f"3b.x{t}"))
                sp.dma_start(out[0, t * P:t * P + P, :], x[:, t, :]).then_inc(output_stored, st.step(f"out{t}", output_stored, 16))
            sp.wait_ge(output_stored, st.at("out1"))

        @block.tensor
        def _(pe):
            st = steps(pe, tensor_step, {unit_multiplied.name: RING})
            pe.sem_inc(unit_multiplied, RING)

            def mm3(o, lh, ll, rh, rl, first, last):
                pe.matmul(o, lh, rh, start=first, stop=False)
                pe.matmul(o, lh, rl, start=False, stop=False)
                return pe.matmul(o, ll, rh, start=False, stop=last)

            def unit():
                pe.wait_ge(unit_split, st.units(st.r + 1 + RING, 0))
                slot = st.n % RING
                st.r += 1
                st.n += 1
                return w_hi[slot], w_lo[slot]

            def stationary(o, name, chunks=None, kt=KD):
                hi, lo = unit()
                for c in range(2):
                    for k in range(kt):
                        if chunks and k % 2 == 0:
                            pe.wait_ge(vector_step, st.at(f"{chunks}.h{k // 2}"))
                        s = slice(k * CH + c * P, k * CH + c * P + P)
                        mm = mm3(o[:, c * S:c * S + S], hi[:, s], lo[:, s], h_hi[:, k, :], h_lo[:, k, :],
                                 k == 0, k == kt - 1)
                mm.then_inc(unit_multiplied, st.step(name, unit_multiplied))

            def moving(os, name, n, lh, ll, kt, stride, chunks=None):
                hi, lo = unit()
                for t in range(NT):
                    for c, (o, w) in enumerate(os[t]):
                        for k in range(kt):
                            if chunks and k % 2 == 0:
                                pe.wait_ge(vector_step, st.at(f"{chunks}.h{k // 2}"))
                            s = slice(k * stride + c * 512, k * stride + c * 512 + w)
                            mm = mm3(o, lh[:, k, t * P:t * P + P], ll[:, k, t * P:t * P + P], hi[:, s], lo[:, s],
                                     k == 0, k == kt - 1)
                mm.then_inc(unit_multiplied, st.step(name, unit_multiplied))

            def into_y(name, lh, ll, first, last, ready=None):
                hi, lo = unit()
                for t in range(NT):
                    for k in range(2):
                        for c in range(2):
                            s = slice(k * D + c * 512, k * D + c * 512 + 512)
                            mm = mm3(B[4 + 2 * t + c], lh[:, k, t * P:t * P + P], ll[:, k, t * P:t * P + P],
                                     hi[:, s], lo[:, s], first and k == 0, last and k == 1)
                    if ready and t == 0:
                        mm.then_inc(tensor_step, st.step(f"{ready}.y0"))
                mm.then_inc(unit_multiplied, st.step(name, unit_multiplied))
                if ready:
                    st.alias(f"{ready}.y1", name)

            def transposes(p, src, name="xn"):
                for t in range(NT):
                    pe.wait_ge(vector_step, st.at(f"{p}.{name}{t}"))
                    for k in range(KD):
                        mm = pe.transpose(B[k // 2][:, (k % 2) * S + t * P:(k % 2) * S + t * P + P],
                                          src[:, t, k * P:k * P + P], ident[:, :])
                        if t == NT - 1 and k % 2:
                            mm.then_inc(tensor_step, st.step(f"{p}.tr{k // 2}"))

            def ffn(p):
                def body(tag, prev):
                    back = 1 if tag == "loop" else 0
                    first = tag == "first"
                    if not first:
                        pe.wait_ge(scalar_step, st.at(f"{p}.{prev}.silu", back))
                    stationary(B[0], f"{p}.{tag}.gate", p if first else None)
                    if not first:
                        pe.wait_ge(vector_step, st.at(f"{p}.{prev}.mul", back))
                    stationary(B[1], f"{p}.{tag}.up")

                def down(tag, prev, back, first, last):
                    pe.wait_ge(vector_step, st.at(f"{p}.{prev}.act", back))
                    into_y(f"{p}.{tag}.down", a_hi, a_lo, first, last, p if last else None)

                transposes(p, xn)
                body("first", None)
                body("second", "first")
                down("second", "first", 0, True, False)
                with st.loop(p, NCH - 3, STEP_UNITS):
                    body("loop", "loop")
                    down("loop", "loop", 1, False, False)
                body("last", "loop")
                down("last", "loop", 0, False, False)
                down("end", "last", 0, False, True)

            def out_product(p):
                for b in range(4):
                    pe.wait_ge(vector_step, st.at(f"{p}o.h{b}"))
                for u in range(4):
                    into_y(f"{p}.out{u}", h_hi[:, 2 * u:2 * u + 2, :], h_lo[:, 2 * u:2 * u + 2, :], u == 0, u == 3,
                           p if u == 3 else None)

            def mixer1():
                p = "M"
                halves = lambda b, w: [[(b[:, t * CH:t * CH + w], w)] for t in range(NT)]
                pe.wait_ge(vector_step, st.at("M.ada0"))
                transposes(p, xn)
                moving(halves(B[0], CH), "M.c_q", CH, h_hi, h_lo, KD, CH, p)
                moving([[(B[1][:, t * 160:t * 160 + 160], 160)] for t in range(NT)], "M.c_kv", 160, h_hi, h_lo, KD, 160)
                moving([[(B[2 + t][:, 0:CH + 4], CH + 4)] for t in range(NT)], "M.v_f", CH + 4, h_hi, h_lo, KD, CH + 4)
                pe.wait_ge(scalar_step, st.at("M.c_q.ev"))
                stationary(B[0], "M.q_f")
                for t in range(NT):
                    pe.wait_ge(vector_step, st.at(f"M.latn{t}"))
                    for k in range(3):
                        mm = pe.transpose(B[4 + (k // 2)][:, (k % 2) * S + t * P:(k % 2) * S + t * P + P],
                                          lat[:, t, k * P:k * P + P], ident[:, :])
                mm.then_inc(tensor_step, st.step("M.latT"))
                pe.wait_ge(scalar_step, st.at("M.c_kv.ev"))
                stationary(B[1], "M.k_f")
                pe.wait_ge(gpsimd_step, st.at("M.logf"))
                for n, (src, b) in enumerate(((fa, 6), (fb, 6))):
                    if n:
                        pe.wait_ge(scalar_step, st.at("M.FQ"))
                    for h in range(4):
                        for t in range(NT):
                            mm = pe.matmul(B[b + h // 2][0:2, (h % 2) * S:(h % 2) * S + S], src[:, t, h, :],
                                           tri[:, t, :], start=t == 0, stop=t == NT - 1)
                    mm.then_inc(tensor_step, st.step(f"M.F{n}"))
                    if n == 0:
                        pe.wait_ge(scalar_step, st.at("M.v_f.ev"))
                        stationary(B[2], "M.q_m")
                stationary(B[3], "M.k_m")
                pe.wait_ge(scalar_step, st.at("M.q_f.ev"))
                moving(halves(B[0], CH), "M.v_m", CH, h_hi, h_lo, KD, CH)
                pe.wait_ge(vector_step, st.at("M.latT.h"))
                pe.wait_ge(vector_step, st.at("M.k_f.ev"))
                pe.wait_ge(scalar_step, st.at("M.q_m.ev"))
                pe.wait_ge(vector_step, st.at("M.k_m.ev"))
                pe.wait_ge(scalar_step, st.at("M.FK"))
                moving([[(B[1], 512), (B[2][:, 0:256], 256)], [(B[3], 512), (B[6][:, 0:256], 256)]],
                       "M.uq", 768, a_hi, a_lo, 2, 768)
                pe.wait_ge(scalar_step, st.at("M.v_m.ev"))
                for c in range(2):
                    bs = [(0, 7), (4, 5)][c]
                    moving([[(B[bs[t]], 512)] for t in range(NT)], f"M.ukv{c}", 512, a_hi[:, 2:3, :], a_lo[:, 2:3, :],
                           1, 512)

                def attend(js):
                    def scores(j):
                        kind, h, t, s = js[j]
                        w = (t + 1) * P
                        if j >= 2:
                            pe.wait_ge(vector_step, st.at(f"M.m{js[j - 2][3]}"))
                        if s == 0:
                            for e in ("uq.ev", "uq.ev1", "ukv0.ev", "ukv1.ev"):
                                pe.wait_ge(st.sem_of(f"M.{e}"), st.at(f"M.{e}"))
                        o, qs = B[s % 2][:, 0:w], slice(t * P, t * P + P)
                        if kind == "fox":
                            pe.matmul(o, qf[:, h // 2, qs], kf[:, h, 0:w], start=True, stop=False)
                            mm = pe.matmul(o, FQ[0:2, h, qs], FK[0:2, h // 2, h % 2, 0:w], start=False, stop=True)
                        elif kind == "moba":
                            mm = pe.matmul(o, qm[:, h // 2, qs], km[:, h, 0:w], start=True, stop=True)
                        else:
                            mm = pe.matmul(o, qcT[0:MLA_QK, h, qs], kcT[0:MLA_QK, h, 0:w], start=True, stop=True)
                        mm.then_inc(tensor_step, st.step(f"M.s{s}"))

                    def turn(j):
                        _, h, t, s = js[j]
                        pe.wait_ge(scalar_step, st.at(f"M.e{s}"))
                        if j >= 2:
                            pe.wait_ge(scalar_step, st.at(f"M.pT{js[j - 2][3]}"))
                        for k in range(t + 1):
                            mm = pe.transpose(B[2 + s % 2][:, k * P:k * P + P], pb[:, s % 2, k * P:k * P + P], ident[:, :])
                        mm.then_inc(tensor_step, st.step(f"M.t{s}"))

                    def values(j):
                        kind, h, t, s = js[j]
                        pe.wait_ge(scalar_step, st.at(f"M.pT{s}"))
                        c = {"fox": 0, "moba": 4, "mla": 8}[kind] + h
                        v, vcol = (vc, h) if kind == "mla" else (vfm, c)
                        for k in range(t + 1):
                            mm = pe.matmul(Yt[:, t, c * HD:c * HD + HD], pT[:, s % 2, k * P:k * P + P],
                                           v[:, k, vcol * HD:vcol * HD + HD], start=k == 0, stop=k == t)
                        mm.then_inc(tensor_step, st.step(f"M.o{s}"))

                    scores(0)
                    for j in range(len(js)):
                        if j + 1 < len(js):
                            scores(j + 1)
                        turn(j)
                        if j:
                            values(j - 1)
                    values(len(js) - 1)

                jobs = attention_jobs()
                attend(jobs[:16])
                pe.wait_ge(vector_step, st.at("M.m15"))
                pe.wait_ge(scalar_step, st.at("M.pT15"))
                ada_reduce(1)
                pe.wait_ge(vector_step, st.at("M.ada1"))
                pe.wait_ge(vector_step, st.at("M.gate1"))
                for n in range(8):
                    src, hh = (qlat, klat)[n // 4], (n % 4) * 2
                    pe.wait_ge(gpsimd_step, st.at("M.rope"))
                    if n >= 4:
                        pe.wait_ge(st.sem_of(f"M.cT{n - 4}"), st.at(f"M.cT{n - 4}"))
                    for h in range(2):
                        for t in range(NT):
                            mm = pe.transpose(B[n % 4][0:MLA_QK, h * S + t * P:h * S + t * P + P],
                                              src[:, t, hh + h, :], ident[:, :])
                    mm.then_inc(tensor_step, st.step(f"M.ct{n}"))
                for n in range(4, 8):
                    pe.wait_ge(st.sem_of(f"M.cT{n}"), st.at(f"M.cT{n}"))
                attend(jobs[16:])
                pe.wait_ge(vector_step, st.at("M.m31"))
                pe.wait_ge(scalar_step, st.at("M.pT31"))
                ada_reduce(2)
                st.r += 2 * KD
                pe.wait_ge(vector_step, st.at("M.ada2"))
                pe.wait_ge(vector_step, st.at("M.gate2"))
                transposes("Mo", osb, "on")
                out_product(p)

            def ada_reduce(third):
                pe.wait_ge(unit_split, st.at(f"M.acc{third}"))
                gate = {0: None, 1: 0, 2: 1}[third]
                for half in range(2):
                    if gate == half:
                        for c in range(2):
                            mm = pe.matmul(B[1 + c], ones[:, :], acc[:, half * D + c * 512:half * D + c * 512 + 512],
                                           start=True, stop=True)
                        mm.then_inc(tensor_step, st.step(f"M.rows{third}"))
                    else:
                        for k in range(KD):
                            mm = pe.matmul(B[0][:, half * KD + k:half * KD + k + 1],
                                           acc[:, half * D + k * P:half * D + k * P + P], ones[:, 0:1],
                                           start=True, stop=True)
                        mm.then_inc(tensor_step, st.step(f"M.cols{third}.{half}"))

            def hgrn(p):
                def project(c):
                    for u, e in enumerate("qfg"):
                        if c:
                            pe.wait_ge(st.sem_of(f"{p}.{e}{c - 1}.ev"), st.at(f"{p}.{e}{c - 1}.ev"))
                        stationary(B[u], f"{p}.{e}{c}", p if c == 0 and u == 0 else None)
                    if c:
                        pe.wait_ge(scalar_step, st.at(f"{p}.v{c - 1}.ev"))
                    moving([[(B[3][:, t * CH:t * CH + CH], CH)] for t in range(NT)], f"{p}.v{c}", CH, h_hi, h_lo, KD, CH)

                def recur(c):
                    pe.wait_ge(vector_step, st.at(f"{p}.k_s{c}"))
                    if c:
                        pe.wait_ge(vector_step, st.at(f"{p}.oms{c - 1}"))
                    for h in range(2):
                        for t in range(NT):
                            mm = pe.transpose(B[4][:, (2 * h + t) * P:(2 * h + t) * P + P],
                                              k_s[c % 2][:, h, t * P:t * P + P], ident[:, :])
                    mm.then_inc(tensor_step, st.step(f"{p}.kst{c}"))
                    pe.wait_ge(scalar_step, st.at(f"{p}.ksT{c}"))
                    for h in range(2):
                        for t in range(NT):
                            ts = slice(t * P, t * P + P)
                            mm = pe.matmul(B[4][:, (2 * h + t) * P:(2 * h + t) * P + P], k_r[c % 2][:, h, ts],
                                           q_r[c % 2][:, h, ts], start=True, stop=True)
                    mm.then_inc(tensor_step, st.step(f"{p}.a{c}"))
                    pe.wait_ge(vector_step, st.at(f"{p}.atm{c}"))
                    if c:
                        pe.wait_ge(vector_step, st.at(f"{p}.on{c - 1}"))
                    for h in range(2):
                        hh = 2 * c + h
                        for t in range(NT):
                            o = B[5][:, h * S + t * P:h * S + t * P + P]
                            for g in range(2):
                                i = (hh * NT + t) * 2 + g
                                if i >= 2:
                                    pe.wait_ge(vector_step, st.at(f"{p}.st{i - 2}"))
                                if g == 0:
                                    pe.wait_ge(gpsimd_step, st.at(f"{p}.vm{hh}.{t}"))
                                mm = pe.matmul(B[6 + g], ksT[:, 2 * h + t, :],
                                               vmask[t][:, g * 4:g * 4 + 4, :].rearrange("p a b -> p (a b)"),
                                               start=True, stop=True)
                                mm.then_inc(tensor_step, st.step(f"{p}.u{i}"))
                            pe.matmul(o, hv[:, t, hh * P:hh * P + P], atm[:, 2 * h + t, :], start=True, stop=False,
                                      skip_group_check=True)
                            for b in range(NHB):
                                n = t * NHB + b
                                if n == 0:
                                    continue
                                pe.wait_ge(vector_step, st.at(f"{p}.S{hh}.{n}"))
                                mm = pe.matmul(o[:, b * HB:b * HB + HB], hist[h][:, n, :],
                                               q_i[c % 2][:, h, n * HB:n * HB + HB], start=False,
                                               stop=b == NHB - 1, skip_group_check=True)
                        mm.then_inc(tensor_step, st.step(f"{p}.ho{hh}"))
                    pe.wait_ge(scalar_step, st.at(f"{p}.osq{c}"))
                    mm = pe.matmul(B[4], ones[:, :], osq.rearrange("p a b -> p (a b)"), start=True, stop=True)
                    mm.then_inc(tensor_step, st.step(f"{p}.oss{c}"))

                transposes(p, xn)
                project(0)
                for c in range(4):
                    if c < 3:
                        project(c + 1)
                    recur(c)
                out_product(p)

            def diff(p):
                transposes(p, xn)
                for u in range(8):
                    b = u % 4
                    if u >= 4:
                        pe.wait_ge(scalar_step, st.at(f"{p}.p{u - 4}.ev"))
                    stationary(B[b], f"{p}.p{u}", p if u == 0 else None)
                for u in range(8, 12):
                    pe.wait_ge(vector_step, st.at(f"{p}.p{u - 4}.ev"))
                    moving([[(B[u % 4][:, t * CH:t * CH + CH], CH)] for t in range(NT)], f"{p}.p{u}", CH,
                           h_hi, h_lo, KD, CH)

                def scores(j):
                    h, t = divmod(j, 2)
                    w = (t + 1) * P
                    for g in range(2):
                        i = 2 * j + g
                        if i >= 2:
                            pe.wait_ge(vector_step, st.at(f"{p}.m{i - 2}"))
                        mm = pe.matmul(B[g][:, 0:w], dq[:, h, t * P:t * P + P], dk[:, 2 * h + g, 0:w],
                                       start=True, stop=True)
                        mm.then_inc(tensor_step, st.step(f"{p}.s{i}"))

                def turn(j):
                    t = j % 2
                    pe.wait_ge(vector_step, st.at(f"{p}.w{j}"))
                    if j >= 2:
                        pe.wait_ge(scalar_step, st.at(f"{p}.pT{j - 2}"))
                    for k in range(t + 1):
                        mm = pe.transpose(B[2 + j % 2][:, k * P:k * P + P], dw[:, j % 2, k * P:k * P + P], ident[:, :])
                    mm.then_inc(tensor_step, st.step(f"{p}.t{j}"))

                def values(j):
                    h, t = divmod(j, 2)
                    pe.wait_ge(scalar_step, st.at(f"{p}.pT{j}"))
                    for k in range(t + 1):
                        mm = pe.matmul(Yt[:, t, h * P:h * P + P], dpT[:, j % 2, k * P:k * P + P],
                                       dv[:, k, h * P:h * P + P], start=k == 0, stop=k == t)
                    mm.then_inc(tensor_step, st.step(f"{p}.o{j}"))

                for u in range(8, 12):
                    pe.wait_ge(scalar_step, st.at(f"{p}.p{u}.ev"))
                scores(0)
                for j in range(16):
                    if j < 15:
                        scores(j + 1)
                    turn(j)
                    if j:
                        values(j - 1)
                values(15)
                transposes(f"{p}o", do, "on")
                out_product(p)

            def pooling(p):
                transposes(p, xn)
                for u in range(4):
                    stationary(B[u], f"{p}.p{u}", p if u == 0 else None)
                hi, lo = unit()
                for g in range(4):
                    pe.wait_ge(vector_step, st.at(f"{p}.pt{g}"))
                    for c in range(2):
                        for k in range(2):
                            s = slice((2 * g + k) * CH + c * P, (2 * g + k) * CH + c * P + P)
                            mm = mm3(B[4 + g][:, c * S:c * S + S], hi[:, s], lo[:, s], h_hi[:, 2 * g + k, :],
                                     h_lo[:, 2 * g + k, :], k == 0, k == 1)
                    if g < 3:
                        mm.then_inc(tensor_step, st.step(f"{p}o.tr{g}"))
                mm.then_inc(unit_multiplied, st.step(f"{p}o.tr3", unit_multiplied))
                out_product(p)

            def bias_rows():
                pe.wait_ge(gpsimd_step, st.at("t5.lhs"))
                for h in range(4):
                    mm = pe.matmul(B[h][:, 0:T5_W], t5_lhs[0:33, h * P:h * P + P], bucket[0:33, :],
                                   start=True, stop=True)
                mm.then_inc(tensor_step, st.step("t5.rows"))

            def columns(name, n, b=0):
                pe.wait_ge(st.sem_of(f"{name}.loaded"), st.at(f"{name}.loaded"))
                st.apart()
                mm = pe.transpose(B[b][:, 0:n], rows[0:n, :], ident[0:n, 0:n])
                mm.then_inc(tensor_step, st.step(f"{name}.T"))

            pe.wait_ge(inputs_loaded, st.at("const.loaded"))
            bias_rows()
            pe.wait_ge(scalar_step, st.at("t5.ev"))
            columns("c", 8)
            with st.loop("layers", LAYERS, LAYER_UNITS):
                columns("L", 27, 7)
                st.r += KD
                ada_reduce(0)
                mixer1()
                ffn("F")
                pe.wait_ge(vector_step, st.at("F.x1"))
            columns("V", 96, 1)
            columns("W", 43, 2)
            for i in range(4):
                ffn(f"{i}a")
                (hgrn, diff, pooling)[i % 3](f"{i}m")
                ffn(f"{i}b")

        @block.scalar
        def _(act):
            st = steps(act, scalar_step)

            def hi(n):
                act.wait_ge(unit_loaded[st.r % RING], st.units(16 * (st.r // RING + 1), 0, RING))
                act.wait_ge(unit_multiplied, st.units(st.n + 1, 1))
                act.activation(w_hi[st.n % RING][:, 0:n], raw[st.r % RING][:, 0:n], ACT.Copy).then_inc(unit_rounded, 1)
                st.r += 1
                st.n += 1

            def copy(out, in_, scale=1.0):
                return act.activation(out, in_, ACT.Copy, scale=scale)

            def square(name, i, src):
                st.apart()
                act.drain()
                act.activation(junk[:, 0:src.shape[-1]], src, ACT.Square, accum_out=stat[:, 0, i:i + 1]).then_inc(scalar_step, st.step(name))

            def pre(p, prev):
                for t in range(NT):
                    act.wait_ge(vector_step, st.at(f"{prev}{t}"))
                    square(f"{p}.sq{t}", t, x[:, t, :])
                to_h(p)

            def to_h(p, a=None, b=None, b0=0):
                a, b = gains(p) if a is None else (a, b)
                for g in range(4):
                    act.wait_ge(st.sem_of(f"{p}.tr{g}"), st.at(f"{p}.tr{g}"))
                    for k in (2 * g, 2 * g + 1):
                        i = act.activation(h_hi[:, k, :], B[b0 + g][:, (k % 2) * S:(k % 2) * S + S], ACT.Identity,
                                           scale=a(k), bias=b(k) if b else 0.0)
                    i.then_inc(scalar_step, st.step(f"{p}.hh{g}"))

            def post_norm(p):
                for t in range(NT):
                    act.wait_ge(st.sem_of(f"{p}.y{t}"), st.at(f"{p}.y{t}"))
                    square(f"{p}.psq{t}", 4 + t, Yt[:, t, :])

            def ffn(p, prev, lead):
                def body(tag, prev, before=True, after=True):
                    if before:
                        hi(2 * D)
                    if after:
                        hi(KD * CH)
                    act.wait_ge(unit_multiplied, st.at(f"{p}.{tag}.gate"))
                    act.activation(tmp[:, 0:2 * S], B[0], ACT.Silu).then_inc(scalar_step, st.step(f"{p}.{tag}.silu"))
                    if after:
                        hi(KD * CH)
                    act.wait_ge(vector_step, st.at(f"{p}.{tag}.mul"))
                    if before:
                        act.wait_ge(unit_multiplied, st.at(f"{p}.{tag}.down"))
                    act.activation(a_hi[:, 0:2, :].rearrange("p a b -> p (a b)"), tmp[:, 2 * S:4 * S], ACT.Copy).then_inc(scalar_step, st.step(f"{p}.{tag}.ahi"))

                pre(p, prev)
                body("first", None, before=False)
                body("second", "first")
                with st.loop(p, NCH - 3, STEP_UNITS):
                    body("loop", "loop")
                body("last", "loop", after=False)
                hi(2 * D)
                for n in lead:
                    hi(n)
                post_norm(p)

            def lead_out():
                for _ in range(3):
                    hi(2 * D)

            def rest_out(p, lead):
                hi(2 * D)
                for n in lead:
                    hi(n)
                post_norm(p)

            MLP = [KD * CH] * 2

            def mixer1():
                p = "M"
                sizes = [KD * CH, KD * 160, KD * (CH + 4)] + [KD * CH] * 5 + [2 * 768, 512, 512]
                hi(sizes[0])
                hi(sizes[1])
                pre(p, "x.ready")
                hi(sizes[2])
                act.wait_ge(unit_multiplied, st.at("M.c_q"))
                copy(lat[:, :, 0:CH], shape3(B[0], 2)).then_inc(scalar_step, st.step("M.c_q.ev"))
                hi(sizes[3])
                act.wait_ge(unit_multiplied, st.at("M.c_kv"))
                copy(lat[:, :, CH:CH + 160], shape3(B[1][:, 0:320], 2)).then_inc(scalar_step, st.step("M.c_kv.ev"))
                act.wait_ge(scalar_step, st.at("M.c_kv.ev"))
                for t in range(NT):
                    square(f"M.sqq{t}", 2 * t, lat[:, t, 0:CH])
                    square(f"M.sqk{t}", 2 * t + 1, lat[:, t, CH:CH + P])
                hi(sizes[4])
                act.wait_ge(unit_multiplied, st.at("M.v_f"))
                for t in range(NT):
                    copy(vfm[:, t, 0:CH], B[2 + t][:, 0:CH])
                    copy(lat[:, t, 416:420], B[2 + t][:, CH:CH + 4]).then_inc(scalar_step, st.step(f"M.v_f.ev"))
                hi(sizes[5])
                act.wait_ge(gpsimd_step, st.at("M.z"))
                act.activation(ft[:, 1], ft[:, 0], ACT.Abs).then_inc(scalar_step, st.step("M.absz"))
                act.wait_ge(scalar_step, st.at("M.absz"))
                act.activation(ft[:, 1], ft[:, 1], ACT.Exp, scale=-1.0).then_inc(scalar_step, st.step("M.expz"))
                act.wait_ge(gpsimd_step, st.at("M.onez"))
                act.activation(ft[:, 1], ft[:, 1], ACT.Ln).then_inc(scalar_step, st.step("M.lnz"))
                act.wait_ge(tensor_step, st.at("M.latT"))
                for k in range(3):
                    i = act.activation(a_hi[:, k, :], B[4 + k // 2][:, (k % 2) * S:(k % 2) * S + S], ACT.Copy,
                                       scale=col[:, C_QLAT + k:C_QLAT + k + 1])
                i.then_inc(scalar_step, st.step("M.latT.hh"))
                act.wait_ge(unit_multiplied, st.at("M.q_f"))
                copy(qf[:, :, :], shape3(B[0], 2), scale=HD ** -0.5).then_inc(scalar_step, st.step("M.q_f.ev"))
                hi(sizes[6])
                act.wait_ge(tensor_step, st.at("M.F0"))
                for h in range(2):
                    copy(FQ[0:2, 2 * h:2 * h + 2, :], shape3(B[6 + h][0:2, :], 2)).then_inc(scalar_step, st.step("M.FQ"))
                hi(sizes[7])
                act.wait_ge(tensor_step, st.at("M.F1"))
                for h in range(2):
                    copy(FK[0:2, h, :, :], shape3(B[6 + h][0:2, :], 2)).then_inc(scalar_step, st.step("M.FK"))
                act.wait_ge(unit_multiplied, st.at("M.q_m"))
                copy(qm[:, :, :], shape3(B[2], 2), scale=HD ** -0.5).then_inc(scalar_step, st.step("M.q_m.ev"))
                hi(sizes[8])
                hi(sizes[9])
                act.wait_ge(unit_multiplied, st.at("M.v_m"))
                copy(vfm[:, :, CH:2 * CH], shape3(B[0], 2)).then_inc(scalar_step, st.step("M.v_m.ev"))
                hi(sizes[10])
                act.wait_ge(unit_multiplied, st.at("M.uq"))
                q0 = qlat[:, 0, :, :].rearrange("p h d -> p (h d)")
                copy(q0[:, 0:512], B[1])
                copy(q0[:, 512:768], B[2][:, 0:256]).then_inc(scalar_step, st.step("M.uq.ev"))

                def attend(js):
                    def evac(j):
                        _, _, t, s = js[j]
                        act.wait_ge(tensor_step, st.at(f"M.t{s}"))
                        if s >= 2:
                            act.wait_ge(tensor_step, st.at(f"M.o{s - 2}"))
                        copy(pT[:, s % 2, 0:(t + 1) * P], B[2 + s % 2][:, 0:(t + 1) * P]).then_inc(scalar_step, st.step(f"M.pT{s}"))

                    for j in range(len(js)):
                        _, _, t, s = js[j]
                        w = (t + 1) * P
                        act.wait_ge(vector_step, st.at(f"M.m{s}"))
                        if s >= 2:
                            act.wait_ge(tensor_step, st.at(f"M.t{s - 2}"))
                        act.activation(pb[:, s % 2, 0:w], ssb[:, s % 2, 0:w], ACT.Exp, scale=-1.0,
                                               bias=stats[:, 0, s:s + 1], accum_out=stats[:, 1, s:s + 1]).then_inc(scalar_step, st.step(f"M.e{s}"))
                        if j:
                            evac(j - 1)
                    evac(len(js) - 1)

                jobs = attention_jobs()
                attend(jobs[:16])
                for n in range(0, 8, 2):
                    act.wait_ge(tensor_step, st.at(f"M.ct{n}"))
                    dst = (qcT, kcT)[n // 4]
                    copy(dst[0:MLA_QK, (n % 4) * 2:(n % 4) * 2 + 2, :], shape3(B[n % 4][0:MLA_QK, :], 2)).then_inc(scalar_step, st.step(f"M.cT{n}"))
                attend(jobs[16:])
                st.r += 2 * KD
                lead_out()
                for t in range(NT):
                    act.wait_ge(vector_step, st.at(f"M.ob1.{t}"))
                    for g, (a, b) in enumerate(((0, 256), (256, 512), (512, 1024))):
                        square(f"M.osq{t}" if g == 2 else f"M.osq{t}.{g}", 3 * t + g, osb[:, t, a:b])
                to_h("Mo", lambda k: col[:, C_GROUP + k:C_GROUP + k + 1])
                rest_out(p, MLP)

            def hgrn(p, prev):
                def project(c):
                    last = c == 3
                    act.wait_ge(unit_multiplied, st.at(f"{p}.q{c}"))
                    if c:
                        act.wait_ge(vector_step, st.at(f"{p}.k_s{c - 1}"))
                    copy(hq[:, :, :], shape3(B[0], 2)).then_inc(scalar_step, st.step(f"{p}.q{c}.ev"))
                    hi(KD * CH)
                    act.wait_ge(unit_multiplied, st.at(f"{p}.f{c}"))
                    act.activation(hf.rearrange("p a b -> p (a b)"), B[1], ACT.Sigmoid).then_inc(scalar_step, st.step(f"{p}.f{c}.ev"))
                    hi(KD * CH)
                    act.wait_ge(unit_multiplied, st.at(f"{p}.g{c}"))
                    act.activation(hg[:, 2 * c:2 * c + 2, :], shape3(B[2], 2), ACT.Sigmoid).then_inc(scalar_step, st.step(f"{p}.g{c}.sig"))
                    if not last:
                        hi(KD * CH)
                    act.wait_ge(unit_multiplied, st.at(f"{p}.v{c}"))
                    copy(hv[:, :, c * CH:c * CH + CH], shape3(B[3], 2)).then_inc(scalar_step, st.step(f"{p}.v{c}.ev"))
                    if not last:
                        hi(KD * CH)

                def gates(c):
                    f = lambda v: v.rearrange("p a b -> p (a b)")
                    act.wait_ge(vector_step, st.at(f"{p}.k{c}"))
                    if c:
                        act.wait_ge(vector_step, st.at(f"{p}.dl{c - 1}"))
                    act.activation(f(hl), f(hf), ACT.Ln).then_inc(scalar_step, st.step(f"{p}.lf{c}"))
                    act.wait_ge(vector_step, st.at(f"{p}.dl{c}"))
                    if c >= 2:
                        act.wait_ge(tensor_step, st.at(f"{p}.oss{c - 2}"))
                    act.activation(f(q_r[c % 2]), f(hd), ACT.Exp)
                    act.activation(f(k_r[c % 2]), f(hd), ACT.Exp, scale=-1.0)
                    act.activation(f(e_b[c % 2]), f(hb), ACT.Exp)
                    act.activation(f(k_s[c % 2]), f(hl), ACT.Exp).then_inc(scalar_step, st.step(f"{p}.e{c}"))

                def recur(c):
                    act.wait_ge(tensor_step, st.at(f"{p}.kst{c}"))
                    copy(ksT.rearrange("p a b -> p (a b)"), B[4]).then_inc(scalar_step, st.step(f"{p}.ksT{c}"))
                    act.wait_ge(tensor_step, st.at(f"{p}.ho{2 * c + 1}"))
                    act.activation(osq.rearrange("p a b -> p (a b)"), B[5], ACT.Square).then_inc(scalar_step, st.step(f"{p}.osq{c}"))

                pre(p, prev)
                project(0)
                gates(0)
                project(1)
                recur(0)
                gates(1)
                project(2)
                recur(1)
                gates(2)
                project(3)
                recur(2)
                gates(3)
                recur(3)
                for g in range(4):
                    act.wait_ge(vector_step, st.at(f"{p}.on{g}"))
                    copy(h_hi[:, 2 * g:2 * g + 2, :], ho[:, 2 * g:2 * g + 2, :]).then_inc(scalar_step, st.step(f"{p}o.hh{g}"))
                lead_out()
                rest_out(p, MLP)

            def diff(p, prev):
                pre(p, prev)
                for u in range(12):
                    if u < 10:
                        hi(KD * CH)
                    act.wait_ge(unit_multiplied, st.at(f"{p}.p{u}"))
                    if u < 4:
                        copy(dq[:, 2 * u:2 * u + 2, :], shape3(B[u % 4], 2), scale=HD ** -0.5).then_inc(scalar_step, st.step(f"{p}.p{u}.ev"))
                    elif u >= 8:
                        c = (u - 8) * CH
                        copy(dv[:, :, c:c + CH], shape3(B[u % 4], 2)).then_inc(scalar_step, st.step(f"{p}.p{u}.ev"))
                act.wait_ge(vector_step, st.at(f"{p}.lamsum"))
                act.activation(lam2[:, 2:4], lam2[:, 0:2], ACT.Exp).then_inc(scalar_step, st.step(f"{p}.lamexp"))

                def evac(j):
                    t = j % 2
                    act.wait_ge(tensor_step, st.at(f"{p}.t{j}"))
                    if j >= 2:
                        act.wait_ge(tensor_step, st.at(f"{p}.o{j - 2}"))
                    copy(dpT[:, j % 2, 0:(t + 1) * P], B[2 + j % 2][:, 0:(t + 1) * P]).then_inc(scalar_step, st.step(f"{p}.pT{j}"))

                for j in range(16):
                    w = (j % 2 + 1) * P
                    for i in (2 * j, 2 * j + 1):
                        act.wait_ge(vector_step, st.at(f"{p}.m{i}"))
                        if j >= 2:
                            act.wait_ge(vector_step, st.at(f"{p}.w{j - 2}"))
                        act.activation(dp[:, i % 4, 0:w], dss[:, i % 4, 0:w], ACT.Exp, scale=-1.0,
                                               bias=dstat[:, 0, i:i + 1], accum_out=dstat[:, 1, i:i + 1]).then_inc(scalar_step, st.step(f"{p}.e{i}"))
                    if j:
                        evac(j - 1)
                evac(15)
                lead_out()
                for t in range(NT):
                    act.wait_ge(tensor_step, st.at(f"{p}.o{14 + t}"))
                    act.activation(do[:, t, :], Yt[:, t, :], ACT.Square).then_inc(scalar_step, st.step(f"{p}.osq{t}"))
                to_h(f"{p}o", lambda k: col[:, C_SUBS:C_SUBS + 1])
                rest_out(p, MLP)

            def pooling(p, prev):
                pre(p, prev)
                for u in range(4):
                    hi(KD * CH)
                    act.wait_ge(unit_multiplied, st.at(f"{p}.p{u}"))
                    copy(pu[:, 2 * u:2 * u + 2, :], shape3(B[u], 2)).then_inc(scalar_step, st.step(f"{p}.p{u}.ev"))
                for g in range(4):
                    act.wait_ge(vector_step, st.at(f"{p}.pp{g}"))
                    copy(h_hi[:, 2 * g:2 * g + 2, :], ppT[:, 2 * g:2 * g + 2, :]).then_inc(scalar_step, st.step(f"{p}.pth{g}"))
                to_h(f"{p}o", lambda k: col[:, C_PSCALE + k:C_PSCALE + k + 1], None, 4)
                hi(2 * D)
                hi(2 * D)
                rest_out(p, MLP)

            act.wait_ge(tensor_step, st.at("t5.rows"))
            for h in range(4):
                copy(t5_rows[:, h, :], B[h][:, 0:T5_W]).then_inc(scalar_step, st.step("t5.ev"))
            act.wait_ge(tensor_step, st.at("c.T"))
            act.activation(col[:, C_C:C_C + KD], B[0][:, 0:KD], ACT.Silu).then_inc(scalar_step, st.step("c.col"))
            with st.loop("layers", LAYERS, LAYER_UNITS):
                act.wait_ge(tensor_step, st.at("L.T"))
                copy(col[:, 0:27], B[7][:, 0:27]).then_inc(scalar_step, st.step("L.col"))
                st.r += KD
                mixer1()
                ffn("F", "M.x", ())
                act.wait_ge(vector_step, st.at("F.x1"))
            for n in MLP:
                hi(n)
            act.wait_ge(tensor_step, st.at("V.T"))
            copy(col[:, 0:96], B[1][:, 0:96]).then_inc(scalar_step, st.step("V.col"))
            act.wait_ge(tensor_step, st.at("W.T"))
            copy(col[:, C_LB:C_LB + 43], B[2][:, 0:43]).then_inc(scalar_step, st.step("W.col"))
            act.wait_ge(vector_step, st.at("lb.in"))
            act.activation(col[:, C_LB:C_LB + 32], col[:, C_LB:C_LB + 32], ACT.Exp).then_inc(scalar_step, st.step("lb.exp"))
            prev = "x.ready"
            for i in range(4):
                ffn(f"{i}a", prev, MLP)
                (hgrn, diff, pooling)[i % 3](f"{i}m", f"{i}a.x")
                ffn(f"{i}b", f"{i}m.x", MLP if i < 3 else ())
                prev = f"{i}b.x"

        @block.vector
        def _(dve):
            st = steps(dve, vector_step, {unit_split.name: RING})
            dve.sem_inc(unit_split, RING)
            flat = lambda v: v.rearrange("p a b -> p (a b)")

            def lo(n):
                dve.wait_ge(unit_rounded, st.units(st.n + 1, 1))
                s = st.n % RING
                dve.tensor_tensor(w_lo[s][:, 0:n], raw[st.r % RING][:, 0:n], w_hi[s][:, 0:n].bitcast(F32),
                                          ALU.subtract).then_inc(unit_split, st.step("", unit_split))
                st.r += 1
                st.n += 1

            def ts(o, i, a, b, op0=ALU.mult, op1=ALU.add):
                return dve.tensor_scalar(o, i, a, b, op0, op1) if b is not None else \
                    dve.tensor_scalar(o, i, a, None, op0)

            def tt(o, a, b, op):
                return dve.tensor_tensor(o, a, b, op)

            def pre(p):
                for t in range(NT):
                    dve.wait_ge(gpsimd_step, st.at(f"{p}.rs{t}"))
                    ts(xn[:, t, :], x[:, t, :], stat[:, 2, t:t + 1], None).then_inc(vector_step, st.step(f"{p}.xn{t}"))
                to_h(p)

            def to_h(p, a=None, b=None, b0=0):
                a, b = gains(p) if a is None else (a, b)
                for g in range(4):
                    dve.wait_ge(scalar_step, st.at(f"{p}.hh{g}"))
                    for k in (2 * g, 2 * g + 1):
                        ps = B[b0 + g][:, (k % 2) * S:(k % 2) * S + S]
                        if b:
                            ts(tmp[:, (k % 4) * S:(k % 4) * S + S], ps, a(k), b(k))
                    if b:
                        dve.drain()
                    for k in (2 * g, 2 * g + 1):
                        ps = B[b0 + g][:, (k % 2) * S:(k % 2) * S + S]
                        h = h_hi[:, k, :].bitcast(F32)
                        if b:
                            i = dve.tensor_tensor(h_lo[:, k, :], tmp[:, (k % 4) * S:(k % 4) * S + S], h, ALU.subtract)
                        else:
                            i = dve.scalar_tensor_tensor(h_lo[:, k, :], ps, a(k), h, ALU.mult, ALU.subtract)
                    i.then_inc(vector_step, st.step(f"{p}.h{g}"))

            def post_norm(p, n, factor):
                for t in range(NT):
                    dve.wait_ge(gpsimd_step, st.at(f"{p}.prs{t}"))
                    dve.wait_ge(st.sem_of(f"{p}.post"), st.at(f"{p}.post"))
                    if t:
                        dve.wait_ge(vector_step, st.at(f"{p}.x0"))
                    dve.scalar_tensor_tensor(tmp[:, :], Yt[:, t, :], stat[:, 2, 4 + t:5 + t], post[n][:, :],
                                             ALU.mult, ALU.mult)
                    dve.drain()
                    dve.scalar_tensor_tensor(x[:, t, :], tmp[:, :], factor, x[:, t, :], ALU.mult, ALU.add).then_inc(vector_step, st.step(f"{p}.x{t}"))

            def ffn(p, n, factor, lead):
                def body(tag, prev, before=True, after=True):
                    if before:
                        lo(2 * D)
                    if after:
                        lo(KD * CH)
                    if before:
                        dve.wait_ge(vector_step, st.at(f"{p}.{prev}.act", int(tag == "loop")))
                    dve.wait_ge(scalar_step, st.at(f"{p}.{tag}.silu"))
                    dve.wait_ge(unit_multiplied, st.at(f"{p}.{tag}.up"))
                    tt(tmp[:, 2 * S:4 * S], tmp[:, 0:2 * S], B[1], ALU.mult).then_inc(vector_step, st.step(f"{p}.{tag}.mul"))
                    if after:
                        lo(KD * CH)
                    dve.wait_ge(scalar_step, st.at(f"{p}.{tag}.ahi"))
                    tt(flat(a_lo[:, 0:2, :]), tmp[:, 2 * S:4 * S], flat(a_hi[:, 0:2, :].bitcast(F32)), ALU.subtract).then_inc(vector_step, st.step(f"{p}.{tag}.act"))

                pre(p)
                body("first", None, before=False)
                body("second", "first")
                with st.loop(p, NCH - 3, STEP_UNITS):
                    body("loop", "loop")
                body("last", "loop", after=False)
                lo(2 * D)
                for w in lead:
                    lo(w)
                post_norm(p, n, factor)

            def lead_out():
                for _ in range(3):
                    lo(2 * D)

            def rest_out(p, n, factor, lead):
                lo(2 * D)
                for w in lead:
                    lo(w)
                post_norm(p, n, factor)

            MLP = [KD * CH] * 2

            def mac(third, k):
                if k == 0:
                    dve.wait_ge(bias_loaded, st.at(f"M.bias{third}"))
                dve.wait_ge(unit_loaded[st.r % RING], st.units(16 * (st.r // RING + 1), 0, RING))
                dve.wait_ge(unit_split, st.units(st.r + RING, 0))
                dve.scalar_tensor_tensor(acc, raw[st.r % RING][:, 0:ADA_W], col[:, C_C + k:C_C + k + 1], acc,
                                                 ALU.mult, ALU.add).then_inc(unit_split, st.step(f"M.acc{third}", unit_split))
                st.r += 1

            def modulation(third):
                cb = B[0]
                if third == 0:
                    dve.wait_ge(scalar_step, st.at("L.col"))
                    dve.wait_ge(tensor_step, st.at("M.cols0.1"))
                    ts(col[:, C_MIXB:C_MIXB + KD], cb[:, 0:KD], 1.0, None)
                    dve.scalar_tensor_tensor(col[:, C_MIXA:C_MIXA + KD], cb[:, KD:2 * KD], 1.0,
                                                     col[:, C_MIX:C_MIX + KD], ALU.add, ALU.mult).then_inc(vector_step, st.step("M.ada0"))
                    return
                if third == 1:
                    dve.wait_ge(tensor_step, st.at("M.cols1.1"))
                    ts(col[:, C_FFNB:C_FFNB + KD], cb[:, KD:2 * KD], 1.0, None).then_inc(vector_step, st.step("M.ada1"))
                else:
                    dve.wait_ge(tensor_step, st.at("M.cols2.0"))
                    dve.scalar_tensor_tensor(col[:, C_FFNA:C_FFNA + KD], cb[:, 0:KD], 1.0,
                                                     col[:, C_FFN:C_FFN + KD], ALU.add, ALU.mult).then_inc(vector_step, st.step("M.ada2"))
                dve.wait_ge(tensor_step, st.at(f"M.rows{third}"))
                dve.wait_ge(post_gain_loaded[0], st.at("L.post"))
                g = post[third - 1]
                for c in range(2):
                    tt(g[:, c * 512:c * 512 + 512], g[:, c * 512:c * 512 + 512], B[1 + c], ALU.mult).then_inc(vector_step, st.step(f"M.gate{third}"))
                st.alias("MF"[third - 1] + ".post", f"M.gate{third}")

            def mixer1():
                sizes = [KD * CH, KD * 160, KD * (CH + 4)] + [KD * CH] * 5 + [2 * 768, 512, 512]
                lo(sizes[0])
                lo(sizes[1])
                pre("M")
                lo(sizes[2])
                lo(sizes[3])
                dve.wait_ge(gpsimd_step, st.at("M.rsl"))
                for t in range(NT):
                    ts(lat[:, t, 0:CH], lat[:, t, 0:CH], stat[:, 2, 2 * t:2 * t + 1], None)
                    ts(lat[:, t, CH:CH + P], lat[:, t, CH:CH + P], stat[:, 2, 2 * t + 1:2 * t + 2], None).then_inc(vector_step, st.step(f"M.latn{t}"))
                lo(sizes[4])
                lo(sizes[5])
                dve.wait_ge(scalar_step, st.at("M.latT.hh"))
                for k in range(3):
                    i = dve.scalar_tensor_tensor(a_lo[:, k, :], B[4 + k // 2][:, (k % 2) * S:(k % 2) * S + S],
                                                 col[:, C_QLAT + k:C_QLAT + k + 1], a_hi[:, k, :].bitcast(F32),
                                                 ALU.mult, ALU.subtract)
                i.then_inc(vector_step, st.step("M.latT.h"))
                lo(sizes[6])
                heads = lambda dst, b, name: (
                    ts(dst[0:HD, 0:4:2, :], shape3(b[0:HD, :], 2), 1.0, None),
                    ts(dst[HD:P, 1:4:2, :], shape3(b[HD:P, :], 2), 1.0, None).then_inc(vector_step, st.step(name)))
                dve.wait_ge(unit_multiplied, st.at("M.k_f"))
                heads(kf, B[1], "M.k_f.ev")
                lo(sizes[7])
                lo(sizes[8])
                dve.wait_ge(unit_multiplied, st.at("M.k_m"))
                heads(km, B[3], "M.k_m.ev")
                lo(sizes[9])
                lo(sizes[10])
                dve.wait_ge(unit_multiplied, st.at("M.uq"))
                q1 = qlat[:, 1, :, :].rearrange("p h d -> p (h d)")
                ts(q1[:, 0:512], B[3], 1.0, None)
                ts(q1[:, 512:768], B[6][:, 0:256], 1.0, None).then_inc(vector_step, st.step("M.uq.ev1"))
                for c in range(2):
                    dve.wait_ge(unit_multiplied, st.at(f"M.ukv{c}"))
                    for t in range(NT):
                        v = B[[(0, 7), (4, 5)][c][t]].rearrange("p (h d) -> p h d", h=4)
                        ts(klat[:, t, 4 * c:4 * c + 4, 0:HD], v[:, :, 0:HD], 1.0, None)
                        ts(vc[:, t, c * CH:c * CH + CH].rearrange("p (h d) -> p h d", h=4), v[:, :, HD:P], 1.0, None).then_inc(vector_step, st.step(f"M.ukv{c}.ev"))

                def attend(js, third):
                    for j, (kind, h, t, s) in enumerate(js):
                        w = (t + 1) * P
                        bias = t5_bias[:, h, S - w:S] if kind == "moba" else causal[:, S - w:S]
                        dve.wait_ge(tensor_step, st.at(f"M.s{s}"))
                        if s >= 2:
                            dve.wait_ge(scalar_step, st.at(f"M.e{s - 2}"))
                        st.apart()
                        dve.tensor_tensor_reduce(ssb[:, s % 2, 0:w], B[s % 2][:, 0:w], bias,
                                                         -(MLA_QK ** -0.5) if kind == "mla" else -1.0, BIG,
                                                         ALU.add, ALU.min, stats[:, 0, s:s + 1]).then_inc(vector_step, st.step(f"M.m{s}"))
                        if j % 2:
                            mac(third, j // 2)
                    h0 = js[0][3]
                    dve.wait_ge(scalar_step, st.at(f"M.e{js[-1][3]}"))
                    dve.reciprocal(stats[:, 2, h0:h0 + 16], stats[:, 1, h0:h0 + 16]).then_inc(vector_step, st.step(f"M.ri{h0}"))
                    dve.wait_ge(tensor_step, st.at(f"M.o{js[-1][3]}"))
                    dve.wait_ge(vector_step, st.at(f"M.ri{h0}"))
                    half = h0 // 16
                    dve.wait_ge(gpsimd_step, st.at("M.rope"))
                    for t in range(NT):
                        r = stats[:, 2, h0:h0 + 16].rearrange("p (h t) -> p h t", t=NT)[:, :, t:t + 1]
                        cs_ = slice(half * 512, half * 512 + 512)
                        tt(osb[:, t, cs_].rearrange("p (h d) -> p h d", h=8), Yt[:, t, cs_].rearrange("p (h d) -> p h d", h=8), r.to_broadcast([P, 8, HD]), ALU.mult).then_inc(vector_step, st.step(f"M.ob{half}.{t}"))

                jobs = attention_jobs()
                attend(jobs[:16], 1)
                modulation(1)
                for n in range(1, 8, 2):
                    dve.wait_ge(tensor_step, st.at(f"M.ct{n}"))
                    dst = (qcT, kcT)[n // 4]
                    ts(dst[0:MLA_QK, (n % 4) * 2:(n % 4) * 2 + 2, :], shape3(B[n % 4][0:MLA_QK, :], 2), 1.0, None).then_inc(vector_step, st.step(f"M.cT{n}"))
                attend(jobs[16:], 2)
                modulation(2)
                lead_out()
                for t in range(NT):
                    dve.wait_ge(gpsimd_step, st.at(f"M.ors{t}"))
                    for g, (a, b) in enumerate(((0, 256), (256, 512), (512, 1024))):
                        ts(osb[:, t, a:b], osb[:, t, a:b], stat[:, 2, 3 * t + g:3 * t + g + 1], None).then_inc(vector_step, st.step(f"Mo.on{t}"))
                to_h("Mo", lambda k: col[:, C_GROUP + k:C_GROUP + k + 1])
                rest_out("M", 0, 1.0, MLP)

            def hgrn(p, n):
                layer = int(p[0]) // 3

                def project(c):
                    lo(KD * CH)
                    dve.wait_ge(scalar_step, st.at(f"{p}.f{c}.ev"))
                    for h in range(2):
                        k = 2 * c + h + 8 * layer
                        ts(hf[:, h, :], hf[:, h, :], col[:, C_OML + k:C_OML + k + 1], col[:, C_LBV + k:C_LBV + k + 1]).then_inc(vector_step, st.step(f"{p}.f{c}.{h}"))
                    lo(KD * CH)
                    dve.wait_ge(vector_step, st.at(f"{p}.f{c}.1"))
                    ts(flat(hk), flat(hf), -1.0, 1.0).then_inc(vector_step, st.step(f"{p}.k{c}"))
                    dve.wait_ge(scalar_step, st.at(f"{p}.g{c}.sig"))
                    tt(hg[:, 2 * c:2 * c + 2, :], hg[:, 2 * c:2 * c + 2, :], shape3(B[2], 2), ALU.mult).then_inc(vector_step, st.step(f"{p}.g{c}.ev"))
                    if c < 3:
                        lo(KD * CH)
                        lo(KD * CH)

                def gates(c):
                    blocks = lambda v: flat(v).rearrange("p (b i) -> p b i", i=HB)
                    dve.wait_ge(scalar_step, st.at(f"{p}.lf{c}"))
                    dve.tensor_tensor_scan(flat(hb), scan_mask, flat(hl), 0.0, ALU.mult, ALU.add).then_inc(vector_step, st.step(f"{p}.b{c}"))
                    dve.wait_ge(vector_step, st.at(f"{p}.b{c}"))
                    full = [P, 2 * S // HB, HB]
                    tt(blocks(hd), blocks(hb), blocks(hb)[:, :, HB // 2:HB // 2 + 1].to_broadcast(full), ALU.subtract)
                    tt(blocks(hl), blocks(hb)[:, :, HB - 1:HB].to_broadcast(full), blocks(hb), ALU.subtract).then_inc(vector_step, st.step(f"{p}.dl{c}"))
                    dve.wait_ge(scalar_step, st.at(f"{p}.e{c}"))
                    i = c % 2
                    tt(flat(q_r[i]), flat(q_r[i]), flat(hq), ALU.mult)
                    tt(flat(k_r[i]), flat(k_r[i]), flat(hk), ALU.mult)
                    tt(flat(q_i[i]), flat(e_b[i]), flat(hq), ALU.mult)
                    tt(flat(k_s[i]), flat(k_s[i]), flat(hk), ALU.mult).then_inc(vector_step, st.step(f"{p}.k_s{c}"))

                def recur(c):
                    dve.wait_ge(tensor_step, st.at(f"{p}.a{c}"))
                    dve.copy_predicated(flat(atm), intra.bitcast(U32), B[4]).then_inc(vector_step, st.step(f"{p}.atm{c}"))
                    for h in range(2):
                        hh = 2 * c + h
                        if hh >= 2:
                            dve.wait_ge(tensor_step, st.at(f"{p}.ho{hh - 2}"))
                        for nb in range(2 * NHB - 1):
                            i = hh * 4 + nb // 4
                            if nb % 4 == 0:
                                dve.wait_ge(tensor_step, st.at(f"{p}.u{i}"))
                            u = B[6 + i % 2][:, (nb % 4) * P:(nb % 4) * P + P]
                            if nb == 0:
                                ts(hist[h][:, 1, :], u, 1.0, None).then_inc(vector_step, st.step(f"{p}.S{hh}.1"))
                            else:
                                dve.wait_ge(vector_step, st.at(f"{p}.S{hh}.{nb}"))
                                dve.scalar_tensor_tensor(
                                    hist[h][:, nb + 1, :], hist[h][:, nb, :],
                                    e_b[c % 2][:, h, nb * HB + HB - 1:nb * HB + HB], u, ALU.mult, ALU.add).then_inc(vector_step, st.step(f"{p}.S{hh}.{nb + 1}"))
                            if nb % 4 == 3 or nb == 2 * NHB - 2:
                                st.alias(f"{p}.st{i}", f"{p}.S{hh}.{nb + 1}")
                    dve.wait_ge(tensor_step, st.at(f"{p}.oss{c}"))
                    ts(flat(oms), B[4], 1.0 / P, EPS).then_inc(vector_step, st.step(f"{p}.oms{c}"))
                    dve.wait_ge(gpsimd_step, st.at(f"{p}.orr{c}"))
                    tt(flat(oms), flat(oms), B[5], ALU.mult)
                    dve.drain()
                    gn = col[:, C_GN + layer:C_GN + layer + 1]
                    dve.scalar_tensor_tensor(ho[:, 2 * c:2 * c + 2, :], oms, gn, hg[:, 2 * c:2 * c + 2, :],
                                                     ALU.mult, ALU.mult).then_inc(vector_step, st.step(f"{p}.on{c}"))

                pre(p)
                dve.memset(flat(atm), 0.0)
                dve.wait_ge(vectors_loaded, st.at(f"{p}.const"))
                project(0)
                gates(0)
                project(1)
                recur(0)
                gates(1)
                project(2)
                recur(1)
                gates(2)
                project(3)
                recur(2)
                gates(3)
                recur(3)
                for g in range(4):
                    dve.wait_ge(scalar_step, st.at(f"{p}o.hh{g}"))
                    tt(h_lo[:, 2 * g:2 * g + 2, :], ho[:, 2 * g:2 * g + 2, :], h_hi[:, 2 * g:2 * g + 2, :].bitcast(F32), ALU.subtract).then_inc(vector_step, st.step(f"{p}o.h{g}"))
                lead_out()
                rest_out(p, n, 1.0, MLP)

            def diff(p, n):
                pre(p)
                dve.wait_ge(vectors_loaded, st.at(f"{p}.const"))
                for h in range(DIFF_H):
                    ts(dbias[:, h, :], cdist, -(2.0 ** (-8.0 * (h + 1) / DIFF_H)), None)
                for g in range(2):
                    ins = dve.tensor_tensor_reduce(dw[:, g, 0:HD], lamrow[:, 2 * g, :], lamrow[:, 2 * g + 1, :], 1.0, 0.0,
                                             ALU.mult, ALU.add, lam2[:, g:g + 1])
                    if g:
                        ins.then_inc(vector_step, st.step(f"{p}.lamsum"))
                dve.wait_ge(gpsimd_step, st.at(f"{p}.zero"))
                for u in range(12):
                    if u < 10:
                        lo(KD * CH)
                    if 4 <= u < 8:
                        c = 4 * (u - 4)
                        dve.wait_ge(unit_multiplied, st.at(f"{p}.p{u}"))
                        ts(dk[0:HD, c:c + 4:2, :], shape3(B[u % 4][0:HD, :], 2), 1.0, None)
                        ts(dk[HD:P, c + 1:c + 4:2, :], shape3(B[u % 4][HD:P, :], 2), 1.0, None).then_inc(vector_step, st.step(f"{p}.p{u}.ev"))
                lam_init = 0.8 - 0.6 * float(np.exp(-0.3 * DIFF_LAYER))
                dve.wait_ge(scalar_step, st.at(f"{p}.lamexp"))
                tt(lam2[:, 4:5], lam2[:, 3:4], lam2[:, 2:3], ALU.subtract)
                ts(col[:, C_SUBS:C_SUBS + 1], col[:, C_SUBLN:C_SUBLN + 1], 1.0 - lam_init, None)
                dve.drain()
                ts(lam2[:, 5:6], lam2[:, 4:5], -lam_init, None, ALU.add)

                def scores(j):
                    h, t = divmod(j, 2)
                    w = (t + 1) * P
                    for i in (2 * j, 2 * j + 1):
                        dve.wait_ge(tensor_step, st.at(f"{p}.s{i}"))
                        if i >= 4:
                            dve.wait_ge(scalar_step, st.at(f"{p}.e{i - 4}"))
                        dve.tensor_tensor_reduce(dss[:, i % 4, 0:w], B[i % 2][:, 0:w], dbias[:, h, S - w:S],
                                                         -1.0, BIG, ALU.add, ALU.min, dstat[:, 0, i:i + 1]).then_inc(vector_step, st.step(f"{p}.m{i}"))

                def combine(j):
                    w = (j % 2 + 1) * P
                    i = 2 * j
                    dve.wait_ge(scalar_step, st.at(f"{p}.e{i + 1}"))
                    if j >= 2:
                        dve.wait_ge(tensor_step, st.at(f"{p}.t{j - 2}"))
                    dve.reciprocal(dstat[:, 2, i:i + 2], dstat[:, 1, i:i + 2])
                    dve.drain()
                    ts(dt1[:, j % 2, 0:w], dp[:, (i + 1) % 4, 0:w], dstat[:, 2, i + 1:i + 2], lam2[:, 5:6],
                       ALU.mult, ALU.mult)
                    dve.drain()
                    dve.scalar_tensor_tensor(dw[:, j % 2, 0:w], dp[:, i % 4, 0:w], dstat[:, 2, i:i + 1],
                                                     dt1[:, j % 2, 0:w], ALU.mult, ALU.add).then_inc(vector_step, st.step(f"{p}.w{j}"))

                scores(0)
                for j in range(16):
                    if j < 15:
                        scores(j + 1)
                    combine(j)
                lead_out()
                for t in range(NT):
                    dve.wait_ge(scalar_step, st.at(f"{p}.osq{t}"))
                    dve.tensor_reduce(dstat[:, 3, 8 * t:8 * t + 8],
                                              do[:, t, :].rearrange("p (h d) -> p h d", h=DIFF_H), AXX, ALU.add).then_inc(vector_step, st.step(f"{p}.oss{t}"))
                for t in range(NT):
                    dve.wait_ge(gpsimd_step, st.at(f"{p}.ors{t}"))
                    r = dstat[:, 3, 16 + 8 * t:24 + 8 * t].unsqueeze(2)
                    tt(do[:, t, :].rearrange("p (h d) -> p h d", h=DIFF_H), Yt[:, t, :].rearrange("p (h d) -> p h d", h=DIFF_H), r.to_broadcast([P, DIFF_H, P]), ALU.mult).then_inc(vector_step, st.step(f"{p}o.on{t}"))
                to_h(f"{p}o", lambda k: col[:, C_SUBS:C_SUBS + 1])
                rest_out(p, n, 1.0, MLP)

            def pooling(p, n):
                pre(p)
                dve.wait_ge(vectors_loaded, st.at(f"{p}.const"))
                for g, w in enumerate(POOL_WINDOWS):
                    lo(KD * CH)
                    dve.wait_ge(scalar_step, st.at(f"{p}.p{g}.ev"))
                    if g:
                        dve.wait_ge(vector_step, st.at(f"{p}.pp{g - 1}"))
                    u = cur = pu[:, 2 * g:2 * g + 2, :]
                    d, i = 1, 0
                    while d < w:
                        nxt = ps_a[i % 2]
                        tt(nxt[:, :, d:S], cur[:, :, d:S], cur[:, :, 0:S - d], ALU.add)
                        ts(nxt[:, :, 0:d], cur[:, :, 0:d], 1.0, None)
                        dve.drain()
                        cur, d, i = nxt, 2 * d, i + 1
                    nxt = ps_a[i % 2]
                    tt(nxt, cur, counts[:, g:g + 1, :].to_broadcast([P, 2, S]), ALU.mult)
                    dve.drain()
                    tt(ppT[:, 2 * g:2 * g + 2, :], nxt, u, ALU.subtract).then_inc(vector_step, st.step(f"{p}.pp{g}"))
                for g in range(4):
                    dve.wait_ge(scalar_step, st.at(f"{p}.pth{g}"))
                    tt(h_lo[:, 2 * g:2 * g + 2, :], ppT[:, 2 * g:2 * g + 2, :], h_hi[:, 2 * g:2 * g + 2, :].bitcast(F32), ALU.subtract).then_inc(vector_step, st.step(f"{p}.pt{g}"))
                to_h(f"{p}o", lambda k: col[:, C_PSCALE + k:C_PSCALE + k + 1], None, 4)
                lo(2 * D)
                lo(2 * D)
                rest_out(p, n, 1.0, MLP)

            def lower_bounds():
                lb = lambda i: col[:, C_LB + 8 * i:C_LB + 8 * i + 8]
                mx, sm = xn[:, 0, 0:8], xn[:, 0, 8:16]
                dve.wait_ge(scalar_step, st.at("W.col"))
                tt(mx, lb(0), lb(1), ALU.max)
                for i in (2, 3):
                    dve.drain()
                    tt(mx, mx, lb(i), ALU.max)
                dve.drain()
                for i in range(4):
                    tt(lb(i), lb(i), mx, ALU.subtract).then_inc(vector_step, st.step("lb.in"))
                dve.wait_ge(scalar_step, st.at("lb.exp"))
                tt(sm, lb(0), lb(1), ALU.add)
                for i in (2, 3):
                    dve.drain()
                    tt(sm, sm, lb(i), ALU.add)
                dve.drain()
                dve.reciprocal(mx, sm)
                dve.drain()
                for i in range(4):
                    tt(lb(i), lb(i), mx, ALU.mult)
                dve.drain()
                tt(sm, lb(0), lb(1), ALU.add)
                dve.drain()
                tt(sm, sm, lb(2), ALU.add)
                dve.drain()
                tt(sm, sm, lb(3), ALU.add)
                dve.drain()
                v = lambda i: col[:, C_LBV + 8 * i:C_LBV + 8 * i + 8]
                tt(v(0), lb(0), lb(0), ALU.subtract)
                tt(v(1), sm, lb(0), ALU.subtract)
                dve.drain()
                ts(col[:, C_OML:C_OML + 16], col[:, C_LBV:C_LBV + 16], -1.0, 1.0)

            dve.wait_ge(inputs_loaded, st.at("const.loaded"))
            dve.wait_ge(scalar_step, st.at("c.col"))
            ts(x[:, 1, 0:1], x[:, 1, 0:1], 1.0, None).then_inc(vector_step, st.step("x.ready0"))
            st.alias("x.ready1", "x.ready0")
            with st.loop("layers", LAYERS, LAYER_UNITS):
                for k in range(KD):
                    mac(0, k)
                modulation(0)
                mixer1()
                ffn("F", 1, 1.0, ())
            lower_bounds()
            for n in MLP:
                lo(n)
            s = 0
            for i in range(4):
                ffn(f"{i}a", s % 2, 0.5, MLP)
                (hgrn, diff, pooling)[i % 3](f"{i}m", (s + 1) % 2)
                ffn(f"{i}b", (s + 2) % 2, 0.5, MLP if i < 3 else ())
                s += 3

        @block.gpsimd
        def _(pool):
            st = steps(pool, gpsimd_step)

            def rms(name, after, i0, i1, n, i2=1):
                pool.wait_ge(scalar_step, st.at(after))
                st.apart()
                a = slice(i0, i1, i2)
                pool.tensor_scalar(stat[:, 1, a], stat[:, 0, a], 1.0 / n, EPS, ALU.mult, ALU.add).then_inc(gpsimd_step, st.step(f"{name}.ms"))
                pool.wait_ge(gpsimd_step, st.at(f"{name}.ms"))
                st.apart()
                pool.tensor_tensor(stat[:, 2, a], stat[:, 1, a], half_power[:, 0:(i1 - i0 + i2 - 1) // i2],
                                           ALU.pow).then_inc(gpsimd_step, st.step(name))

            def pre(p):
                for t in range(NT):
                    rms(f"{p}.rs{t}", f"{p}.sq{t}", t, t + 1, D)

            def post_norm(p):
                for t in range(NT):
                    rms(f"{p}.prs{t}", f"{p}.psq{t}", 4 + t, 5 + t, D)

            def acc_bias(third, l):
                if third:
                    pool.wait_ge(tensor_step, st.at({1: "M.cols0.1", 2: "M.cols1.1"}[third]))
                    st.apart()
                pool.memset(acc, 0.0).then_inc(gpsimd_step, st.step(f"M.zero{third}"))
                pool.wait_ge(gpsimd_step, st.at(f"M.zero{third}"))
                st.apart()
                pool.dma_start(acc[0:1, :], A["b_ada"][bass.ds(l, 1), third * ADA_W:third * ADA_W + ADA_W])\
                    .then_inc(bias_loaded, st.step(f"M.bias{third}", bias_loaded, 16))

            def vec(t, l):
                return t[bass.ds(l, 1), :].rearrange("a (k p) -> (a k) p", p=P)

            def mixer1(l):
                pre("M")
                acc_bias(1, l)
                for n, i0, w in (("q", 0, CH), ("k", 1, P)):
                    pool.wait_ge(scalar_step, st.at("M.sqk1"))
                    st.apart()
                    pool.tensor_scalar(stat[:, 1, i0:4:2], stat[:, 0, i0:4:2], 1.0 / w, EPS, ALU.mult, ALU.add).then_inc(gpsimd_step, st.step(f"M.lms{n}"))
                pool.wait_ge(gpsimd_step, st.at("M.lmsk"))
                st.apart()
                pool.tensor_tensor(stat[:, 2, 0:4], stat[:, 1, 0:4], half_power[:, 0:4], ALU.pow).then_inc(gpsimd_step, st.step("M.rsl"))
                pool.wait_ge(scalar_step, st.at("M.v_f.ev"))
                st.apart()
                pool.wait_ge(vectors_loaded, st.at("L.loaded"))
                st.apart()
                pool.tensor_tensor(ft[:, 0], lat[:, :, 416:420], bforget.unsqueeze(1).to_broadcast([P, NT, 4]),
                                           ALU.add).then_inc(gpsimd_step, st.step("M.z"))
                pool.wait_ge(scalar_step, st.at("M.expz"))
                st.apart()
                pool.tensor_scalar(ft[:, 1], ft[:, 1], 1.0, None, ALU.add).then_inc(gpsimd_step, st.step("M.onez"))
                pool.tensor_scalar(ft[:, 0], ft[:, 0], 0.0, None, ALU.min).then_inc(gpsimd_step, st.step("M.minz"))
                pool.wait_ge(scalar_step, st.at("M.lnz"))
                st.apart()
                pool.wait_ge(gpsimd_step, st.at("M.minz"))
                st.apart()
                pool.tensor_tensor(logf, ft[:, 0], ft[:, 1], ALU.subtract).then_inc(gpsimd_step, st.step("M.lf"))
                pool.wait_ge(gpsimd_step, st.at("M.lf"))
                st.apart()
                pool.tensor_copy(fa[:, :, :, 0], logf)
                pool.tensor_scalar(fb[:, :, :, 1], logf, -1.0, None, ALU.mult).then_inc(gpsimd_step, st.step("M.logf"))
                for e in ("uq.ev", "uq.ev1", "ukv1.ev"):
                    pool.wait_ge(st.sem_of(f"M.{e}"), st.at(f"M.{e}"))
                    st.apart()
                half = ROPE // 2
                for tag, v, heads in (("q", qlat, MLA_H), ("k", None, 1)):
                    if v is None:
                        x1 = lat[:, :, 384:384 + half]
                        x2 = lat[:, :, 384 + half:384 + ROPE]
                        o1, o2 = krot[:, :, 0:half], krot[:, :, half:ROPE]
                        c_, s_ = cs[:, 0], cs[:, 1]
                        r = [m_[:, 0:NT * half].rearrange("p (t d) -> p t d", t=NT) for m_ in rot]
                    else:
                        x1, x2 = v[:, :, :, HD:HD + half], v[:, :, :, HD + half:]
                        o1, o2 = x1, x2
                        c_, s_ = (cs[:, i].unsqueeze(2).to_broadcast([P, NT, heads, half]) for i in range(2))
                        r = [m_.rearrange("p (t h d) -> p t h d", t=NT, h=heads) for m_ in rot]
                    for i, (a, b) in enumerate(((x1, c_), (x2, s_), (x2, c_), (x1, s_))):
                        pool.tensor_tensor(r[i], a, b, ALU.mult).then_inc(gpsimd_step, st.step(f"M.r{tag}{i}"))
                    pool.wait_ge(gpsimd_step, st.at(f"M.r{tag}3"))
                    st.apart()
                    pool.tensor_tensor(o1, r[0], r[1], ALU.subtract)
                    pool.tensor_tensor(o2, r[2], r[3], ALU.add).then_inc(gpsimd_step, st.step(f"M.r{tag}"))
                    pool.wait_ge(gpsimd_step, st.at(f"M.r{tag}"))
                    st.apart()
                for t in range(NT):
                    i = pool.tensor_copy(klat[:, t, :, HD:], krot[:, t, :].unsqueeze(1).to_broadcast([P, MLA_H, ROPE]))
                i.then_inc(gpsimd_step, st.step("M.rope"))
                acc_bias(2, l)
                for t in range(NT):
                    pool.wait_ge(scalar_step, st.at(f"M.osq{t}"))
                    st.apart()
                    for g, w in enumerate((256, 256, 512)):
                        i = 3 * t + g
                        pool.tensor_scalar(stat[:, 1, i:i + 1], stat[:, 0, i:i + 1], 1.0 / w, EPS, ALU.mult,
                                                   ALU.add).then_inc(gpsimd_step, st.step(f"M.oms{t}.{g}"))
                    pool.wait_ge(gpsimd_step, st.at(f"M.oms{t}.2"))
                    st.apart()
                    pool.tensor_tensor(stat[:, 2, 3 * t:3 * t + 3], stat[:, 1, 3 * t:3 * t + 3],
                                               half_power[:, 0:3], ALU.pow).then_inc(gpsimd_step, st.step(f"M.ors{t}"))
                post_norm("M")

            def ffn(p):
                pre(p)
                post_norm(p)

            def hgrn(p):
                pre(p)
                for c in range(4):
                    pool.wait_ge(scalar_step, st.at(f"{p}.v{c}.ev"))
                    pool.wait_ge(vectors_loaded, st.at(f"{p}.const"))
                    for h in (2 * c, 2 * c + 1):
                        for t in range(NT):
                            if h:
                                pool.wait_ge(tensor_step, st.at(f"{p}.u{(h - 1) * 4 + 2 * t + 1}"))
                            full = [P, NHB, P]
                            pool.tensor_tensor(vmask[t], hv[:, t, h * P:h * P + P].unsqueeze(1).to_broadcast(full),
                                                       blockm.unsqueeze(2).to_broadcast(full), ALU.mult).then_inc(gpsimd_step, st.step(f"{p}.vm{h}.{t}"))
                    pool.wait_ge(vector_step, st.at(f"{p}.oms{c}"))
                    v = oms.rearrange("p a b -> p (a b)")
                    pool.tensor_tensor(v, v, half_power[:, 0:1].to_broadcast([P, 2 * S]), ALU.pow).then_inc(gpsimd_step, st.step(f"{p}.orr{c}"))
                post_norm(p)

            def diff(p):
                pre(p)
                for t in range(NT):
                    pool.wait_ge(vector_step, st.at(f"{p}.oss{t}"))
                    a, b = dstat[:, 3, 8 * t:8 * t + 8], dstat[:, 3, 16 + 8 * t:24 + 8 * t]
                    pool.tensor_scalar(b, a, 1.0 / P, EPS, ALU.mult, ALU.add).then_inc(gpsimd_step, st.step(f"{p}.oms{t}"))
                    pool.wait_ge(gpsimd_step, st.at(f"{p}.oms{t}"))
                    pool.tensor_tensor(b, b, half_power[:, 0:8], ALU.pow).then_inc(gpsimd_step, st.step(f"{p}.ors{t}"))
                post_norm(p)

            def pooling(p):
                pre(p)
                post_norm(p)

            def constants_for(i):
                pool.wait_ge(vector_step, st.at("F.x1" if i == 0 else f"{i - 1}m.x1"))
                p = f"{i}m"
                if i % 3 == 0:
                    pool.dma_start(scan_mask, A["K_scan"])\
                        .then_inc(vectors_loaded, st.step(f"{p}.c0", vectors_loaded, 16))
                    pool.dma_start(intra, A["K_intra"])\
                        .then_inc(vectors_loaded, st.step(f"{p}.c1", vectors_loaded, 16))
                    pool.dma_start(blockm, A["K_block"])\
                        .then_inc(vectors_loaded, st.step(f"{p}.const", vectors_loaded, 16))
                elif i == 1:
                    pool.dma_start(cdist, A["K_chunk_dist"])\
                        .then_inc(vectors_loaded, st.step(f"{p}.c0", vectors_loaded, 16))
                    pool.dma_start(lamrow.rearrange("p a b -> p (a b)"), A["diff_lambda_2"].rearrange("a b c -> a (b c)").to_broadcast([P, 4 * HD]))\
                        .then_inc(vectors_loaded, st.step(f"{p}.const", vectors_loaded, 16))
                    pool.memset(dk, 0.0).then_inc(gpsimd_step, st.step(f"{p}.zero"))
                else:
                    pool.dma_start(counts.rearrange("p a b -> p (a b)"), A["K_counts"])\
                        .then_inc(vectors_loaded, st.step(f"{p}.const", vectors_loaded, 16))

            pool.memset(half_power[:, :], -0.5).then_inc(gpsimd_step, st.step("half"))
            pool.memset(ones[:, :], 1.0)
            pool.memset(kf, 0.0)
            pool.memset(km, 0.0)
            for n, (dst, src) in enumerate((
                    (ident[:, :], A["K_ident"]), (tri.rearrange("p a b -> p (a b)"), A["K_tri"]),
                    (causal, A["K_causal"]), (bucket, A["K_bucket"]), (firstc, A["K_first"]),
                    (cs[:, 0].rearrange("p a b -> p (a b)"), A["K_cos"]),
                    (cs[:, 1].rearrange("p a b -> p (a b)"), A["K_sin"]),
                    (lat[0:32, 0, 0:4], A["t5_table"]),
                    (rows[0:8, :], A["c"].rearrange("a (k p) -> (a k) p", p=P)),
                    (x[:, 0, :], A["x"][0, 0:P, :]), (x[:, 1, :], A["x"][0, P:S, :]))):
                pool.dma_start(dst, src)\
                    .then_inc(inputs_loaded, st.step("const.loaded", inputs_loaded, 16))
            st.alias("c.loaded", "const.loaded")
            pool.wait_ge(inputs_loaded, st.at("const.loaded"))
            pool.tensor_copy(t5_lhs[0:32, :].rearrange("p (h n) -> p h n", h=4),
                                     lat[0:32, 0, 0:4].unsqueeze(2).to_broadcast([32, 4, P])).then_inc(gpsimd_step, st.step("t5.tab"))
            for t in range(NT):
                pool.tensor_copy(fa[:, t, :, 1], firstc[:, t:t + 1].to_broadcast([P, 4]))
                pool.tensor_copy(fb[:, t, :, 0], firstc[:, t:t + 1].to_broadcast([P, 4]))
            pool.memset(ft[:, 0], 0.0).then_inc(gpsimd_step, st.step("t5.first"))
            pool.wait_ge(gpsimd_step, st.at("t5.first"))
            pool.memset(t5_lhs[32:33, :], NEG).then_inc(gpsimd_step, st.step("t5.lhs"))
            pool.wait_ge(scalar_step, st.at("t5.ev"))
            pool.dma_start(skew.rearrange("h (p j) -> p h j", j=T5_W + 1)[:, :, 0:T5_W], t5_rows)\
                .then_inc(t5_moved, st.step("t5.out", t5_moved, 16))
            pool.wait_ge(t5_moved, st.at("t5.out"))
            pool.dma_start(t5_bias, skew[:, 0:P * T5_W].rearrange("h (p j) -> p h j", j=T5_W)[:, :, P - 1:P - 1 + S])\
                .then_inc(t5_moved, st.step("t5.bias", t5_moved, 16))
            pool.wait_ge(t5_moved, st.at("t5.bias"))
            pool.wait_ge(tensor_step, st.at("c.T"))
            with st.loop("layers", LAYERS, LAYER_UNITS) as l:
                for i, (v, r, k) in enumerate((("g_mix_pre", 0, 8), ("g_ffn_pre", 8, 8), ("g_group", 16, 8),
                                               ("g_q_lat", 24, 2), ("g_kv_lat", 26, 1))):
                    pool.dma_start(rows[r:r + k, :], vec(A[v], l))\
                        .then_inc(vectors_loaded, st.step(f"L.{v}", vectors_loaded, 16))
                pool.dma_start(bforget, A["b_forget"][bass.ds(l, 1), :].to_broadcast([P, 4]))\
                    .then_inc(vectors_loaded, st.step("L.loaded", vectors_loaded, 16))
                pool.dma_start(post[0][:, :], A["g_mix_post"][bass.ds(l, 1), :].to_broadcast([P, D]))\
                    .then_inc(post_gain_loaded[0], st.step("L.post0", post_gain_loaded[0], 16))
                pool.dma_start(post[1][:, :], A["g_ffn_post"][bass.ds(l, 1), :].to_broadcast([P, D]))\
                    .then_inc(post_gain_loaded[0], st.step("L.post", post_gain_loaded[0], 16))
                acc_bias(0, l)
                mixer1(l)
                ffn("F")
                pool.wait_ge(vector_step, st.at("F.x1"))
                st.apart()
                st.r, st.n = st.r + LAYER_UNITS[0], st.n + LAYER_UNITS[1]
            for i in range(4):
                for j in range(3):
                    pool.dma_start(rows[(3 * i + j) * 8:(3 * i + j) * 8 + 8, :], A["norm_gains_2"][i, 2 * j:2 * j + 1, :].rearrange("a (k p) -> (a k) p", p=P))\
                        .then_inc(vectors_loaded, st.step("V.loaded", vectors_loaded, 16))
            names = [f"{i}{c}" for i in range(4) for c in "amb"]

            def post_gain(s):
                i, j = divmod(s, 3)
                if s >= 2:
                    pool.wait_ge(vector_step, st.at(f"{names[s - 2]}.x1"))
                pool.dma_start(post[s % 2][:, :], A["norm_gains_2"][i, 2 * j + 1:2 * j + 2, :].to_broadcast([P, D]))\
                    .then_inc(post_gain_loaded[s % 2], st.step(f"{names[s]}.post", post_gain_loaded[s % 2], 16))

            post_gain(0)
            post_gain(1)
            pool.wait_ge(tensor_step, st.at("V.T"))
            for v, r, k in (("hgrn_lb_raw_2", 0, 32), ("hgrn_gnorm_2", 32, 2), ("diff_subln_2", 34, 1),
                            ("pool_scale_2", 35, 8)):
                pool.dma_start(rows[r:r + k, :], A[v].rearrange("a (k p) -> (a k) p", p=P))\
                    .then_inc(vectors_loaded, st.step("W.loaded", vectors_loaded, 16))
            pool.wait_ge(vectors_loaded, st.at("W.loaded"))
            constants_for(0)
            for s, p in enumerate(names):
                {"a": ffn, "b": ffn, "m": (hgrn, diff, pooling)[int(p[0]) % 3]}[p[1]](p)
                if s + 2 < len(names):
                    post_gain(s + 2)
                if p[1] == "m" and p != "3m":
                    constants_for(int(p[0]) + 1)


_OUT = (1, S, D)


def kernel(**inputs):
    import concourse.bacc as _bacc
    from concourse.bass_utils import run_bass_kernel_spmd as _run

    arrays = {f"in_{k}": np.ascontiguousarray(v) for k, v in inputs.items()}
    arrays.update({f"in_K_{k}": v for k, v in constants().items()})

    def build(table, per, trips):
        nc = _bacc.Bacc("TRN2", target_bir_lowering=False, num_devices=1)
        A = {k[3:]: nc.dram_tensor(k, a.shape, mybir.dt.from_np(a.dtype), kind="ExternalInput").ap()
             for k, a in arrays.items()}
        out = nc.dram_tensor("out_0", _OUT, F32, kind="ExternalOutput").ap()
        program(nc, A, out, table, per, trips)
        return nc

    table, per, trips = {}, {}, {}
    build(table, per, trips)
    nc = build(table, per, trips)
    r = _run(nc, [arrays], core_ids=[0])
    return r.results[0]["out_0"]
```

```python
from contextlib import ExitStack, contextmanager

import numpy as np

import concourse.bass as bass
from concourse import mybir

F32 = mybir.dt.float32
F32R = mybir.dt.float32r
U32 = mybir.dt.uint32
ALU = mybir.AluOpType
ACT = mybir.ActivationFunctionType
AXX = mybir.AxisListType.X

P = 128
S = 256
NT = S // P
D = 1024
KD = D // P
LAYERS = 2
FF = 2816
CH = 256
NCH = FF // CH
UNIT = 2080
RING = 3
EPS = 1e-6
NEG = -1e30
BIG = 3e38
HD = 64
IN_W = 1956
FOX_Q, FOX_K, FOX_V, MOBA_Q, MOBA_K, MOBA_V, C_Q, C_KV = 0, 256, 512, 772, 1028, 1284, 1540, 1796
ROPE = 32
MLA_QK = HD + ROPE
MLA_H = 8
HB = 16
NHB = P // HB
ADA_W = 2 * D
T5_W = 384
POOL_WINDOWS = (2, 4, 8, 16)
DIFF_LAYER, DIFF_H = 1, 8

LAYER_UNITS = (3 * KD + 15 + 3 * NCH, 15 + 3 * NCH)
STEP_UNITS = (3, 3)


def constants():
    p = np.arange(P)
    f = np.float32
    c = {}
    c["ident"] = np.eye(P, dtype=f)
    c["tri"] = np.stack([(t * P + p[:, None] <= np.arange(S)[None]) for t in range(NT)], 1).astype(f).reshape(P, -1)
    dist = P + p[:, None] - np.arange(S)[None]
    c["causal"] = np.where(dist >= 0, 0, NEG).astype(f)
    chunk = (np.arange(S)[None] // 64) <= ((P + p[:, None]) // 64)
    c["chunk_dist"] = np.where(chunk, np.abs(dist), 1e33).astype(f)
    half = ROPE // 2
    inv = (f(1.0) / (f(10000.0) ** (np.arange(half, dtype=f) / f(half)))).astype(f)
    ang = np.arange(S, dtype=f)[:, None] * inv[None]
    for n, fn in (("cos", np.cos), ("sin", np.sin)):
        c[n] = fn(ang).astype(f).reshape(NT, P, half).transpose(1, 0, 2).reshape(P, -1)
    d = (S - 1) - np.arange(T5_W)
    n = np.maximum(d, 0)
    large = 16 + (np.log(np.maximum(n, 16).astype(f) / f(16)) / f(np.log(8.0)) * f(16)).astype(np.int32)
    bucket = np.where(n < 16, n, np.minimum(large, 31))
    hot = np.zeros((P, T5_W), f)
    hot[np.where(d >= 0, bucket, 32), np.arange(T5_W)] = 1
    c["bucket"] = hot
    c["first"] = np.stack([p == 0, p < 0], 1).astype(f)
    c["scan"] = np.tile((np.arange(2 * S) % HB != 0).astype(f), (P, 1))
    c["block"] = (p[:, None] // HB == np.arange(NHB)[None]).astype(f)
    s, t = p[:, None], p[None]
    c["intra"] = np.tile(((s <= t) & (s // HB == t // HB)), (1, 4)).astype(f)
    c["counts"] = np.tile(np.concatenate([1.0 / np.minimum(np.arange(S) + 1, w) for w in POOL_WINDOWS]), (P, 1)).astype(f)
    return c


class Steps:

    def __init__(self, eng, own, apart, table, per, trips, start=()):
        self.eng, self.own, self.nobody, self.table, self.per, self.trips = eng, own, apart, table, per, trips
        self.count = dict(start)
        self.loops = []
        self.r = self.n = 0

    def step(self, name, sem=None, by=1):
        sem = sem or self.own
        key = sem.name
        self.count[key] = self.count.get(key, 0) + by
        if name:
            self.table[name] = (sem, self.count[key], tuple(i for i, _, _ in self.loops))
        return by

    def alias(self, other, name):
        self.table[other] = self.table[name]

    def sem_of(self, name):
        return self.table[name][0] if name in self.table else self.own

    def at(self, name, back=0):
        if name not in self.table:
            return 1
        sem, value, where = self.table[name]
        mine = {i: reg for i, reg, _ in self.loops}
        for i in where:
            if i not in mine:
                value += (self.trips[i] - 1) * self.per.get((i, sem.name), 0)
        if back:
            value -= back * self.per.get((self.loops[-1][0], sem.name), 0)
        for i in where:
            if i in mine:
                value = mine[i] * self.per.get((i, sem.name), 0) + value
        return value

    def units(self, value, which, ring=None):
        for i, reg, units in self.loops:
            value = reg * (16 * units[which] // ring if ring else units[which]) + value
        return value

    def apart(self):
        if self.loops:
            self.eng.sem_inc(self.nobody, 1)

    @contextmanager
    def loop(self, name, turns, units):
        self.trips[name] = turns
        before, r, n = dict(self.count), self.r, self.n
        with self.eng.Fori(0, turns) as i:
            self.loops.append((name, i, units))
            yield i
            self.loops.pop()
        assert (self.r - r, self.n - n) == units
        self.r, self.n = r + turns * units[0], n + turns * units[1]
        for key, c in self.count.items():
            one = c - before.get(key, 0)
            self.per[name, key] = one
            self.count[key] = c + (turns - 1) * one


def program(nc, A, out, table, per, trips):
    ctx = ExitStack()
    with ctx:
        def sb(name, shape, dt=F32):
            return ctx.enter_context(nc.sbuf_tensor(name, shape, dt))

        x = sb("x", [P, NT, D])
        xn = sb("xn", [P, NT, D])
        tmp = sb("tmp", [P, D])
        junk = sb("junk", [P, D], mybir.dt.bfloat16)
        raw = [sb(f"raw{i}", [P, UNIT]) for i in range(RING)]
        w_hi = [sb(f"w_hi{i}", [P, UNIT], F32R) for i in range(RING)]
        w_lo = [sb(f"w_lo{i}", [P, UNIT], F32R) for i in range(RING)]
        h_hi = sb("h_hi", [P, KD, S], F32R)
        h_lo = sb("h_lo", [P, KD, S], F32R)
        a_hi = sb("a_hi", [P, 3, S], F32R)
        a_lo = sb("a_lo", [P, 3, S], F32R)
        ident = sb("ident", [P, P])
        ones = sb("ones", [P, P])
        stat = sb("stat", [P, 4, 8])
        half_power = sb("half_power", [P, 8])
        post = [sb(f"post{i}", [P, D]) for i in range(2)]
        rows = sb("rows", [P, P])
        col = sb("col", [P, 246])
        M = sb("M", [P, 19850])
        at = [0]

        def m(shape):
            n = int(np.prod(shape))
            v = M[:, at[0]:at[0] + n]
            at[0] += n
            assert at[0] <= M.shape[1], at[0]
            names = "abcd"[:len(shape)]
            if len(shape) == 1:
                return v
            return v.rearrange(f"p ({' '.join(names)}) -> p {' '.join(names)}", **dict(zip(names[1:], shape[1:])))

        C_MIX, C_FFN, C_GROUP, C_QLAT, C_KVLAT, C_C = 0, 8, 16, 24, 26, 27
        C_MIXA, C_MIXB, C_FFNA, C_FFNB = 40, 48, 56, 64
        C_SUB = 72
        C_LB, C_GN, C_SUBLN, C_PSCALE, C_LBV, C_OML, C_SUBS = 168, 200, 202, 203, 212, 228, 244

        B = [ctx.enter_context(nc.psum_tensor(f"B{i}", [P, 512], F32)) for i in range(4)]
        Yt = ctx.enter_context(nc.psum_tensor("Y", [P, NT, D], F32))
        B += [Yt[:, i // 2, (i % 2) * 512:(i % 2) * 512 + 512] for i in range(4)]
        B = [b[:, :] for b in B]

        def sem(name):
            return ctx.enter_context(nc.semaphore(name))

        tensor_step, scalar_step = sem("tensor_step"), sem("scalar_step")
        vector_step, gpsimd_step = sem("vector_step"), sem("gpsimd_step")
        unit_loaded = [sem(f"unit_loaded{i}") for i in range(RING)]
        unit_rounded = sem("unit_rounded")
        unit_split = sem("unit_split")
        unit_multiplied = sem("unit_multiplied")
        c_loaded, inputs_loaded, gains_loaded = sem("c_loaded"), sem("inputs_loaded"), sem("gains_loaded")
        vectors_loaded, bias_loaded = sem("vectors_loaded"), sem("bias_loaded")
        post_gain_loaded = [sem(f"post_gain_loaded{i}") for i in range(2)]
        t5_moved, output_stored = sem("t5_moved"), sem("output_stored")
        nobody_waits = sem("nobody_waits")

        def steps(eng, own, start=()):
            return Steps(eng, own, nobody_waits, table, per, trips, start)

        skew = nc.dram_tensor("skew", (4, P * (T5_W + 1)), F32, kind="Internal").ap()

        block = ctx.enter_context(nc.Block())

        def shape3(v, k):
            return v.rearrange("p (k n) -> p k n", k=k)

        acc = m([ADA_W])
        tri = m([NT, S])
        causal = m([S])
        cs = m([2, NT, ROPE // 2])
        bforget = m([4])
        firstc = m([2])
        t5_bias = m([4, S])
        qf, kf, qm, km = m([2, S]), m([4, S]), m([2, S]), m([4, S])
        vfm = m([NT, 512])
        lat = m([NT, 420])
        logf = m([NT, 4]); fa = m([NT, 4, 2]); fb = m([NT, 4, 2]); ft = m([2, NT, 4])
        FQ = tmp[:, :].rearrange("p (h s) -> p h s", h=4)
        FK = xn[:, :, 0:512].rearrange("p t (h s) -> p t h s", h=2)
        qlat = m([NT, MLA_H, MLA_QK]); klat = m([NT, MLA_H, MLA_QK]); vc = m([NT, 512])
        rot = [xn[:, i // 2, 512 + (i % 2) * 256:768 + (i % 2) * 256] for i in range(4)]
        krot = m([NT, ROPE])
        qcT, kcT = m([MLA_H, S]), m([MLA_H, S])
        bucket = kcT[:, 0:2, :].rearrange("p a b -> p (a b)")[:, 0:T5_W]
        t5_lhs = qf.rearrange("p a b -> p (a b)")
        t5_rows = klat.rearrange("p a b c -> p (a b c)").rearrange("p (h j) -> p h j", h=4)
        ssb, pb, pT = m([2, S]), m([2, S]), m([2, S])
        stats = m([4, 32])
        osb = xn
        at[0] = 0
        scan_mask = m([2 * S]); intra = m([4 * P]); blockm = m([NHB])
        hv, hg = m([NT, D]), m([KD, S])
        hq, hf, hk, hl = (m([2, S]) for _ in range(4))
        hb = hf
        osq, hd = (tmp[:, i * 512:i * 512 + 512].rearrange("p (a b) -> p a b", a=2) for i in range(2))
        diag = osq.rearrange("p a b -> p (a b)")
        hstat = m([8])
        q_r, k_r, q_i, k_s, e_b = ([m([2, S]) for _ in range(2)] for _ in range(5))
        ksT, atm = m([4, P]), m([4, P])
        vmask = [m([NHB, P]) for _ in range(2)]
        hist = [m([2 * NHB, P]) for _ in range(2)]
        ho = xn[:, :, :].rearrange("p t n -> p (t n)").rearrange("p (h s) -> p h s", h=KD)
        at[0] = 0
        dbias = m([DIFF_H, S])
        cdist = m([S])
        dq, dk = m([DIFF_H, S]), m([2 * DIFF_H, S])
        dv = m([NT, D])
        dss, dp = m([4, S]), m([4, S])
        dt1, dw = m([2, S]), m([2, S])
        dpT = m([2, S])
        dstat = m([4, 32])
        lamrow = m([4, HD])
        lam2 = m([16])
        do = xn
        at[0] = 0
        counts = m([4, S])
        pu = m([KD, S])
        ps_a = [m([2, S]) for _ in range(2)]
        ppT = m([KD, S])

        rows_c, rows_v, rows_w = (xn[:, 0, i * P:i * P + P] for i in range(3))

        def cols(w, c0, n):
            return w[:, c0:c0 + n].rearrange("(k p) n -> p k n", p=P)

        def wrows(w, r0, k):
            return w[r0:r0 + k * P, :].rearrange("(k p) n -> p k n", p=P)

        hgrn_units = [(g * D + c * CH) for c in range(4) for g in (0, 1, 3, 2)]

        def gains(p):
            if p in "MF":
                a, b = {"M": (C_MIXA, C_MIXB), "F": (C_FFNA, C_FFNB)}[p]
                return (lambda k: col[:, a + k:a + k + 1]), (lambda k: col[:, b + k:b + k + 1])
            c = C_SUB + (3 * int(p[0]) + "amb".index(p[1])) * KD
            return (lambda k: col[:, c + k:c + k + 1]), None

        names = [f"{i}{c}" for i in range(4) for c in "amb"]

        def other(l):
            return LAYERS - 1 - l

        def attention_jobs():
            js = [(kind, h, t) for kind, n in (("fox", 4), ("moba", 4), ("mla", MLA_H)) for h in range(n)
                  for t in range(NT)]
            return [(*j, s) for s, j in enumerate(js)]

        @block.sync
        def _(sp):
            st = steps(sp, output_stored)

            def load(src, k=KD):
                slot = st.r % RING
                sp.wait_ge(unit_split, st.units(st.r + 1, 0))
                st.apart()
                n = src.shape[-1]
                sp.dma_start(shape3(raw[slot][:, 0:k * n], k) if k > 1 else raw[slot][:, 0:n], src)\
                    .then_inc(unit_loaded[slot], 16)
                st.r += 1
                st.n += 1

            def layer(t, l):
                return t[bass.ds(l, 1), :, :].rearrange("a k n -> (a k) n")

            def ada_unit(w, third, k):
                load(w[k * P:k * P + P, third * ADA_W:third * ADA_W + ADA_W], 1)
                st.n -= 1

            def ada(w, third):
                for k in range(KD):
                    ada_unit(w, third, k)

            def ffn(p, wgu, wdn, between=lambda k: None):
                def gate(i):
                    load(wgu[:, bass.ds(i * CH, CH)].rearrange("(k p) n -> p k n", p=P))

                def up(i):
                    load(wgu[:, bass.ds(i * CH + FF, CH)].rearrange("(k p) n -> p k n", p=P))

                def down(i):
                    load(wdn[bass.ds(i * CH, CH), :].rearrange("(k p) n -> p k n", p=P), 2)

                gate(0)
                up(0)
                between(0)
                gate(1)
                between(1)
                up(1)
                between(2)
                down(0)
                between(3)
                with st.loop(p, NCH - 3, STEP_UNITS) as j:
                    gate(j + 2)
                    up(j + 2)
                    down(j + 1)
                gate(NCH - 1)
                up(NCH - 1)
                between(4)
                between(5)
                down(NCH - 2)
                between(6)
                down(NCH - 1)
                between(7)

            def out_rows(w):
                for u in range(4):
                    load(wrows(w, u * 2 * P, 2), 2)

            ada(A["w_ada"][0], 0)
            with st.loop("layers", LAYERS, LAYER_UNITS) as l:
                w_in, w_ukv = layer(A["w_in"], l), layer(A["w_ukv"], l)
                w_ada, w_ada_next = layer(A["w_ada"], l), layer(A["w_ada"], other(l))
                load(cols(w_in, C_Q, CH))
                load(cols(w_in, IN_W - CH, CH))
                load(cols(w_in, FOX_V, CH + 4))
                for c in (FOX_Q, FOX_K, MOBA_Q, MOBA_K, MOBA_V):
                    load(cols(w_in, c, CH))
                load(wrows(layer(A["w_uq"], l), 0, 2), 2)
                for c in range(2):
                    load(w_ukv[:, c * 512:c * 512 + 512], 1)
                ada(w_ada, 1)
                ada(w_ada, 2)
                out_rows(layer(A["w_out"], l))
                ffn("F", layer(A["w_gate_up"], l), layer(A["w_down"], l), lambda k: ada_unit(w_ada_next, 0, k))
            for i in range(4):
                ffn(f"{i}a", A["ffn1_w_in_2"][i], A["ffn1_w_out_2"][i])
                if i % 3 == 0:
                    for c in hgrn_units:
                        load(cols(A["hgrn_w_in_2"][i // 3], c, CH))
                    out_rows(A["hgrn_w_out_2"][i // 3])
                elif i == DIFF_LAYER:
                    for c in range(12):
                        load(cols(A["diff_w_in_2"][0], c * CH, CH))
                    out_rows(A["diff_w_out_2"][0])
                else:
                    for c in range(4):
                        load(cols(A["pool_w_in_2"][0], c * CH, CH))
                    load(A["pool_w_group_2"][0].rearrange("g (k p) n -> p (g k) n", p=P))
                    out_rows(A["pool_w_out_2"][0])
                ffn(f"{i}b", A["ffn2_w_in_2"][i], A["ffn2_w_out_2"][i])
            for t in range(NT):
                sp.wait_ge(vector_step, st.at(f"3b.x{t}"))
                sp.dma_start(out[0, t * P:t * P + P, :], x[:, t, :]).then_inc(output_stored, st.step(f"out{t}", output_stored, 16))
            sp.wait_ge(output_stored, st.at("out1"))

        @block.tensor
        def _(pe):
            st = steps(pe, tensor_step, {unit_multiplied.name: RING})
            pe.sem_inc(unit_multiplied, RING)

            def mm3(o, lh, ll, rh, rl, first, last):
                pe.matmul(o, lh, rh, start=first, stop=False)
                pe.matmul(o, lh, rl, start=False, stop=False)
                return pe.matmul(o, ll, rh, start=False, stop=last)

            def unit():
                pe.wait_ge(unit_split, st.units(st.r + 1 + RING, 0))
                slot = st.n % RING
                st.r += 1
                st.n += 1
                return w_hi[slot], w_lo[slot]

            def stationary(o, name, ready=None, kt=KD):
                hi, lo = unit()
                for c in range(2):
                    for k in range(kt):
                        if ready and c == 0 and k % 4 == 0:
                            pe.wait_ge(vector_step, st.at(f"{ready}.h{NT - 1}.{k // 4}"))
                        s = slice(k * CH + c * P, k * CH + c * P + P)
                        mm = mm3(o[:, c * S:c * S + S], hi[:, s], lo[:, s], h_hi[:, k, :], h_lo[:, k, :],
                                 k == 0, k == kt - 1)
                mm.then_inc(unit_multiplied, st.step(name, unit_multiplied))

            def moving(os, name, n, lh, ll, kt, stride):
                hi, lo = unit()
                for t in range(NT):
                    for c, (o, w) in enumerate(os[t]):
                        for k in range(kt):
                            s = slice(k * stride + c * 512, k * stride + c * 512 + w)
                            mm = mm3(o, lh[:, k, t * P:t * P + P], ll[:, k, t * P:t * P + P], hi[:, s], lo[:, s],
                                     k == 0, k == kt - 1)
                mm.then_inc(unit_multiplied, st.step(name, unit_multiplied))

            def into_y(name, lh, ll, first, last):
                hi, lo = unit()
                for t in range(NT):
                    mm = into_y_tile(t, hi, lo, lh, ll, first, last)
                mm.then_inc(unit_multiplied, st.step(name, unit_multiplied))

            def into_y_tile(t, hi, lo, lh, ll, first, last):
                for k in range(2):
                    for c in range(2):
                        s = slice(k * D + c * 512, k * D + c * 512 + 512)
                        mm = mm3(B[4 + 2 * t + c], lh[:, k, t * P:t * P + P], ll[:, k, t * P:t * P + P],
                                 hi[:, s], lo[:, s], first and k == 0, last and k == 1)
                return mm

            def into_y_pair(p, names, parts, first, last, before, between=0):
                units = []
                for t in range(NT):
                    for i, (lh, ll) in enumerate(parts):
                        if t == 0:
                            units.append(unit())
                            st.r += between if i == 0 else 0
                        before(t, i)
                        mm = into_y_tile(t, *units[i], lh, ll, first and i == 0, last and i == 1)
                        if t:
                            mm.then_inc(unit_multiplied, st.step(names[i], unit_multiplied))
                    if last and t == 0:
                        mm.then_inc(tensor_step, st.step(f"{p}.y0"))
                if last:
                    st.alias(f"{p}.y1", names[1])

            def transposes(p, src, t, name="xn"):
                for k in range(KD):
                    if name == "xn" and k % 4 == 0:
                        pe.wait_ge(vector_step, st.at(f"{p}.xn{t}.{k // 4}"))
                    elif k == 0:
                        pe.wait_ge(vector_step, st.at(f"{p}.{name}{t}"))
                    mm = pe.transpose(B[4 + 2 * t + k // 4][:, (k % 4) * P:(k % 4) * P + P],
                                      src[:, t, k * P:k * P + P], ident[:, :])
                    if k % 4 == 3:
                        mm.then_inc(tensor_step, st.step(f"{p}.tr{t}.{k // 4}"))

            def whole_input(p):
                for t in range(NT):
                    transposes(p, xn, t)

            def first_pair(p, works):
                units = []
                transposes(p, xn, 0)
                for i, (work, name) in enumerate(works):
                    units.append(unit())
                    work(*units[i], 0, p if i == 0 else None)
                    if i == 0:
                        transposes(p, xn, 1)
                for i, (work, name) in enumerate(works):
                    work(*units[i], 1, p if i == 0 else None)\
                        .then_inc(unit_multiplied, st.step(name, unit_multiplied))

            def by_tokens(o, n):
                def work(hi, lo, t, ready):
                    for k in range(KD):
                        if ready and k % 4 == 0:
                            pe.wait_ge(vector_step, st.at(f"{ready}.h{t}.{k // 4}"))
                        s = slice(k * n, k * n + n)
                        mm = mm3(o[:, t * n:t * n + n], h_hi[:, k, t * P:t * P + P], h_lo[:, k, t * P:t * P + P],
                                 hi[:, s], lo[:, s], k == 0, k == KD - 1)
                    return mm
                return work

            def ffn(p, between=0, last_columns=None):
                def body(tag, prev):
                    back = 1 if tag == "loop" else 0
                    pe.wait_ge(scalar_step, st.at(f"{p}.{prev}.silu", back))
                    stationary(B[0], f"{p}.{tag}.gate")
                    pe.wait_ge(vector_step, st.at(f"{p}.{prev}.mul", back))
                    stationary(B[1], f"{p}.{tag}.up")

                def down(tag, prev, back, first):
                    pe.wait_ge(vector_step, st.at(f"{p}.{prev}.act", back))
                    into_y(f"{p}.{tag}.down", a_hi, a_lo, first, False)

                def last_inputs(t, i):
                    if t == 0:
                        pe.wait_ge(vector_step, st.at(f"{p}.{('loop', 'last')[i]}.act"))

                whole_input(p)
                stationary(B[0], f"{p}.first.gate", p)
                stationary(B[1], f"{p}.first.up")
                st.r += between and 1
                pe.wait_ge(scalar_step, st.at(f"{p}.first.silu"))
                stationary(B[0], f"{p}.second.gate")
                st.r += between and 1
                pe.wait_ge(vector_step, st.at(f"{p}.first.mul"))
                stationary(B[1], f"{p}.second.up")
                st.r += between and 1
                down("second", "first", 0, True)
                st.r += between and 1
                if last_columns:
                    last_columns()
                with st.loop(p, NCH - 3, STEP_UNITS):
                    body("loop", "loop")
                    down("loop", "loop", 1, False)
                pe.wait_ge(scalar_step, st.at(f"{p}.loop.silu"))
                stationary(B[0], f"{p}.last.gate")
                pe.wait_ge(vector_step, st.at(f"{p}.loop.mul"))
                stationary(B[1], f"{p}.last.up")
                st.r += between and 2
                into_y_pair(p, (f"{p}.last.down", f"{p}.end.down"), ((a_hi, a_lo), (h_hi, h_lo)), False, True,
                            last_inputs, between and 1)
                st.r += between and 1

            def out_product(p, src=None):
                def ready(t, i):
                    if i:
                        return
                    if src is not None:
                        if t:
                            transposes(f"{p}o", src, t, "on")
                        pe.wait_ge(vector_step, st.at(f"{p}o.h{t}.1"))
                    elif t == 0:
                        for b in range(4):
                            pe.wait_ge(vector_step, st.at(f"{p}o.h{b}"))

                if src is not None:
                    transposes(f"{p}o", src, 0, "on")
                for u in (0, 2):
                    into_y_pair(p, (f"{p}.out{u}", f"{p}.out{u + 1}"),
                                [(h_hi[:, 2 * v:2 * v + 2, :], h_lo[:, 2 * v:2 * v + 2, :]) for v in (u, u + 1)],
                                u == 0, u == 2, ready if u == 0 else lambda t, i: None)

            def mixer1():
                p = "M"
                halves = lambda b, w: [[(b[:, t * CH:t * CH + w], w)] for t in range(NT)]
                pe.wait_ge(vector_step, st.at("M.ada0", 1))
                first_pair(p, ((by_tokens(B[0], CH), "M.c_q"), (by_tokens(B[1], CH), "M.c_kv")))
                moving([[(B[2 + t][:, 0:CH + 4], CH + 4)] for t in range(NT)], "M.v_f", CH + 4, h_hi, h_lo, KD, CH + 4)
                pe.wait_ge(scalar_step, st.at("M.c_q.ev"))
                stationary(B[0], "M.q_f")
                for t in range(NT):
                    pe.wait_ge(vector_step, st.at(f"M.latn{t}"))
                    for k in range(3):
                        mm = pe.transpose(B[4 + (k // 2)][:, (k % 2) * S + t * P:(k % 2) * S + t * P + P],
                                          lat[:, t, k * P:k * P + P], ident[:, :])
                mm.then_inc(tensor_step, st.step("M.latT"))
                pe.wait_ge(scalar_step, st.at("M.c_kv.ev"))
                stationary(B[1], "M.k_f")
                pe.wait_ge(gpsimd_step, st.at("M.logf"))
                for n, (src, b) in enumerate(((fa, 6), (fb, 6))):
                    if n:
                        pe.wait_ge(scalar_step, st.at("M.FQ"))
                    for h in range(4):
                        for t in range(NT):
                            mm = pe.matmul(B[b + h // 2][0:2, (h % 2) * S:(h % 2) * S + S], src[:, t, h, :],
                                           tri[:, t, :], start=t == 0, stop=t == NT - 1)
                    mm.then_inc(tensor_step, st.step(f"M.F{n}"))
                    if n == 0:
                        pe.wait_ge(scalar_step, st.at("M.v_f.ev"))
                        stationary(B[2], "M.q_m")
                stationary(B[3], "M.k_m")
                pe.wait_ge(scalar_step, st.at("M.q_f.ev"))
                moving(halves(B[0], CH), "M.v_m", CH, h_hi, h_lo, KD, CH)
                pe.wait_ge(vector_step, st.at("M.latT.h"))
                pe.wait_ge(vector_step, st.at("M.k_f.ev"))
                pe.wait_ge(scalar_step, st.at("M.q_m.ev"))
                pe.wait_ge(vector_step, st.at("M.k_m.ev"))
                pe.wait_ge(scalar_step, st.at("M.FK"))
                moving([[(B[1], 512), (B[2][:, 0:256], 256)], [(B[3], 512), (B[6][:, 0:256], 256)]],
                       "M.uq", 768, a_hi, a_lo, 2, 768)
                pe.wait_ge(scalar_step, st.at("M.v_m.ev"))
                for c in range(2):
                    bs = [(0, 7), (4, 5)][c]
                    moving([[(B[bs[t]], 512)] for t in range(NT)], f"M.ukv{c}", 512, a_hi[:, 2:3, :], a_lo[:, 2:3, :],
                           1, 512)

                def attend(js):
                    def scores(j):
                        kind, h, t, s = js[j]
                        w = (t + 1) * P
                        if j >= 2:
                            pe.wait_ge(vector_step, st.at(f"M.m{js[j - 2][3]}"))
                        if s == 0:
                            for e in ("uq.ev", "uq.ev1", "ukv0.ev", "ukv1.ev"):
                                pe.wait_ge(st.sem_of(f"M.{e}"), st.at(f"M.{e}"))
                        o, qs = B[s % 2][:, 0:w], slice(t * P, t * P + P)
                        if kind == "fox":
                            pe.matmul(o, qf[:, h // 2, qs], kf[:, h, 0:w], start=True, stop=False)
                            mm = pe.matmul(o, FQ[0:2, h, qs], FK[0:2, h // 2, h % 2, 0:w], start=False, stop=True)
                        elif kind == "moba":
                            mm = pe.matmul(o, qm[:, h // 2, qs], km[:, h, 0:w], start=True, stop=True)
                        else:
                            mm = pe.matmul(o, qcT[0:MLA_QK, h, qs], kcT[0:MLA_QK, h, 0:w], start=True, stop=True)
                        mm.then_inc(tensor_step, st.step(f"M.s{s}"))

                    def turn(j):
                        _, h, t, s = js[j]
                        pe.wait_ge(scalar_step, st.at(f"M.e{s}"))
                        if j >= 2:
                            pe.wait_ge(scalar_step, st.at(f"M.pT{js[j - 2][3]}"))
                        for k in range(t + 1):
                            mm = pe.transpose(B[2 + s % 2][:, k * P:k * P + P], pb[:, s % 2, k * P:k * P + P], ident[:, :])
                        mm.then_inc(tensor_step, st.step(f"M.t{s}"))

                    def values(j):
                        kind, h, t, s = js[j]
                        pe.wait_ge(scalar_step, st.at(f"M.pT{s}"))
                        c = {"fox": 0, "moba": 4, "mla": 8}[kind] + h
                        v, vcol = (vc, h) if kind == "mla" else (vfm, c)
                        for k in range(t + 1):
                            mm = pe.matmul(Yt[:, t, c * HD:c * HD + HD], pT[:, s % 2, k * P:k * P + P],
                                           v[:, k, vcol * HD:vcol * HD + HD], start=k == 0, stop=k == t)
                        mm.then_inc(tensor_step, st.step(f"M.o{s}"))

                    scores(0)
                    for j in range(len(js)):
                        if j + 1 < len(js):
                            scores(j + 1)
                        turn(j)
                        if j:
                            values(j - 1)
                    values(len(js) - 1)

                jobs = attention_jobs()
                attend(jobs[:16])
                pe.wait_ge(vector_step, st.at("M.m15"))
                pe.wait_ge(scalar_step, st.at("M.pT15"))
                ada_reduce(1)
                pe.wait_ge(vector_step, st.at("M.ada1"))
                pe.wait_ge(vector_step, st.at("M.gate1"))
                for n in range(8):
                    src, hh = (qlat, klat)[n // 4], (n % 4) * 2
                    pe.wait_ge(gpsimd_step, st.at("M.rope"))
                    if n >= 4:
                        pe.wait_ge(st.sem_of(f"M.cT{n - 4}"), st.at(f"M.cT{n - 4}"))
                    for h in range(2):
                        for t in range(NT):
                            mm = pe.transpose(B[n % 4][0:MLA_QK, h * S + t * P:h * S + t * P + P],
                                              src[:, t, hh + h, :], ident[:, :])
                    mm.then_inc(tensor_step, st.step(f"M.ct{n}"))
                for n in range(4, 8):
                    pe.wait_ge(st.sem_of(f"M.cT{n}"), st.at(f"M.cT{n}"))
                attend(jobs[16:])
                pe.wait_ge(vector_step, st.at("M.m31"))
                pe.wait_ge(scalar_step, st.at("M.pT31"))
                ada_reduce(2)
                st.r += 2 * KD
                pe.wait_ge(vector_step, st.at("M.ada2"))
                pe.wait_ge(vector_step, st.at("M.gate2"))
                out_product(p, osb)

            def ada_reduce(third, m="M"):
                pe.wait_ge(unit_split, st.at(f"{m}.acc{third}"))
                gate = {0: None, 1: 0, 2: 1}[third]
                for half in range(2):
                    if gate == half:
                        for c in range(2):
                            mm = pe.matmul(B[1 + c], ones[:, :], acc[:, half * D + c * 512:half * D + c * 512 + 512],
                                           start=True, stop=True)
                        mm.then_inc(tensor_step, st.step(f"M.rows{third}"))
                    else:
                        for k in range(KD):
                            mm = pe.matmul(B[0 if third else 3][:, half * KD + k:half * KD + k + 1],
                                           acc[:, half * D + k * P:half * D + k * P + P], ones[:, 0:1],
                                           start=True, stop=True)
                        mm.then_inc(tensor_step, st.step(f"{m}.cols{third}.{half}"))

            def hgrn(p):
                def project(c):
                    for u, e in enumerate("qfg"):
                        if c:
                            pe.wait_ge(st.sem_of(f"{p}.{e}{c - 1}.ev"), st.at(f"{p}.{e}{c - 1}.ev"))
                        stationary(B[u], f"{p}.{e}{c}", p if c == 0 and u == 0 else None)
                    if c:
                        pe.wait_ge(scalar_step, st.at(f"{p}.v{c - 1}.ev"))
                    moving([[(B[3][:, t * CH:t * CH + CH], CH)] for t in range(NT)], f"{p}.v{c}", CH, h_hi, h_lo, KD, CH)

                def recur(c):
                    pe.wait_ge(vector_step, st.at(f"{p}.k_s{c}"))
                    if c:
                        pe.wait_ge(vector_step, st.at(f"{p}.on{c - 1}"))
                    for h in range(2):
                        for t in range(NT):
                            mm = pe.transpose(B[4][:, (2 * h + t) * P:(2 * h + t) * P + P],
                                              k_s[c % 2][:, h, t * P:t * P + P], ident[:, :])
                    mm.then_inc(tensor_step, st.step(f"{p}.kst{c}"))
                    pe.wait_ge(scalar_step, st.at(f"{p}.ksT{c}"))
                    for h in range(2):
                        for t in range(NT):
                            ts = slice(t * P, t * P + P)
                            mm = pe.matmul(B[4][:, (2 * h + t) * P:(2 * h + t) * P + P], k_r[c % 2][:, h, ts],
                                           q_r[c % 2][:, h, ts], start=True, stop=True)
                    mm.then_inc(tensor_step, st.step(f"{p}.a{c}"))
                    pe.wait_ge(vector_step, st.at(f"{p}.atm{c}"))
                    for h in range(2):
                        hh = 2 * c + h
                        for t in range(NT):
                            o = B[5][:, h * S + t * P:h * S + t * P + P]
                            for g in range(2):
                                i = (hh * NT + t) * 2 + g
                                if i >= 2:
                                    pe.wait_ge(vector_step, st.at(f"{p}.st{i - 2}"))
                                if g == 0:
                                    pe.wait_ge(gpsimd_step, st.at(f"{p}.vm{hh}.{t}"))
                                mm = pe.matmul(B[6 + g], ksT[:, 2 * h + t, :],
                                               vmask[t][:, g * 4:g * 4 + 4, :].rearrange("p a b -> p (a b)"),
                                               start=True, stop=True)
                                mm.then_inc(tensor_step, st.step(f"{p}.u{i}"))
                            pe.matmul(o, hv[:, t, hh * P:hh * P + P], atm[:, 2 * h + t, :], start=True, stop=False,
                                      skip_group_check=True)
                            for b in range(NHB):
                                n = t * NHB + b
                                if n == 0:
                                    continue
                                pe.wait_ge(vector_step, st.at(f"{p}.S{hh}.{n}"))
                                mm = pe.matmul(o[:, b * HB:b * HB + HB], hist[h][:, n, :],
                                               q_i[c % 2][:, h, n * HB:n * HB + HB], start=False,
                                               stop=b == NHB - 1, skip_group_check=True)
                        mm.then_inc(tensor_step, st.step(f"{p}.ho{hh}"))
                    pe.wait_ge(scalar_step, st.at(f"{p}.osq{c}"))
                    for i in range(4):
                        mm = pe.matmul(B[4][:, i:i + 1], osq[:, i // 2, (i % 2) * P:(i % 2) * P + P], ones[:, 0:1],
                                       start=True, stop=True)
                    mm.then_inc(tensor_step, st.step(f"{p}.oss{c}"))
                    pe.wait_ge(vector_step, st.at(f"{p}.diag{c}"))
                    pe.matmul(B[4], ones[:, :], diag, start=True, stop=True)\
                        .then_inc(tensor_step, st.step(f"{p}.obc{c}"))

                whole_input(p)
                project(0)
                for c in range(4):
                    if c < 3:
                        project(c + 1)
                    recur(c)
                out_product(p)

            def diff(p):
                whole_input(p)
                for u in range(8):
                    b = u % 4
                    if u >= 4:
                        pe.wait_ge(scalar_step, st.at(f"{p}.p{u - 4}.ev"))
                    stationary(B[b], f"{p}.p{u}", p if u == 0 else None)
                for u in range(8, 12):
                    pe.wait_ge(vector_step, st.at(f"{p}.p{u - 4}.ev"))
                    moving([[(B[u % 4][:, t * CH:t * CH + CH], CH)] for t in range(NT)], f"{p}.p{u}", CH,
                           h_hi, h_lo, KD, CH)

                def scores(j):
                    h, t = divmod(j, 2)
                    w = (t + 1) * P
                    for g in range(2):
                        i = 2 * j + g
                        if i >= 2:
                            pe.wait_ge(vector_step, st.at(f"{p}.m{i - 2}"))
                        mm = pe.matmul(B[g][:, 0:w], dq[:, h, t * P:t * P + P], dk[:, 2 * h + g, 0:w],
                                       start=True, stop=True)
                        mm.then_inc(tensor_step, st.step(f"{p}.s{i}"))

                def turn(j):
                    t = j % 2
                    pe.wait_ge(vector_step, st.at(f"{p}.w{j}"))
                    if j >= 2:
                        pe.wait_ge(scalar_step, st.at(f"{p}.pT{j - 2}"))
                    for k in range(t + 1):
                        mm = pe.transpose(B[2 + j % 2][:, k * P:k * P + P], dw[:, j % 2, k * P:k * P + P], ident[:, :])
                    mm.then_inc(tensor_step, st.step(f"{p}.t{j}"))

                def values(j):
                    h, t = divmod(j, 2)
                    pe.wait_ge(scalar_step, st.at(f"{p}.pT{j}"))
                    for k in range(t + 1):
                        mm = pe.matmul(Yt[:, t, h * P:h * P + P], dpT[:, j % 2, k * P:k * P + P],
                                       dv[:, k, h * P:h * P + P], start=k == 0, stop=k == t)
                    mm.then_inc(tensor_step, st.step(f"{p}.o{j}"))

                for u in range(8, 12):
                    pe.wait_ge(scalar_step, st.at(f"{p}.p{u}.ev"))
                scores(0)
                for j in range(16):
                    if j < 15:
                        scores(j + 1)
                    turn(j)
                    if j:
                        values(j - 1)
                values(15)
                out_product(p, do)

            def pooling(p):
                whole_input(p)
                for u in range(4):
                    stationary(B[u], f"{p}.p{u}", p if u == 0 else None)
                hi, lo = unit()
                for g in range(4):
                    pe.wait_ge(vector_step, st.at(f"{p}.pt{g}"))
                    for c in range(2):
                        for k in range(2):
                            s = slice((2 * g + k) * CH + c * P, (2 * g + k) * CH + c * P + P)
                            mm = mm3(B[4 + g][:, c * S:c * S + S], hi[:, s], lo[:, s], h_hi[:, 2 * g + k, :],
                                     h_lo[:, 2 * g + k, :], k == 0, k == 1)
                    if g < 3:
                        mm.then_inc(tensor_step, st.step(f"{p}o.tr{g}"))
                mm.then_inc(unit_multiplied, st.step(f"{p}o.tr3", unit_multiplied))
                out_product(p)

            def bias_rows():
                pe.wait_ge(vector_step, st.at("t5.lhs"))
                for h in range(4):
                    mm = pe.matmul(B[h][:, 0:T5_W], t5_lhs[0:33, h * P:h * P + P], bucket[0:33, :],
                                   start=True, stop=True)
                mm.then_inc(tensor_step, st.step("t5.rows"))

            def columns(name, n, b, src):
                pe.wait_ge(st.sem_of(f"{name}.loaded"), st.at(f"{name}.loaded"))
                st.apart()
                pe.transpose(B[b][:, 0:n], src[0:n, :], ident[0:n, 0:n]).then_inc(tensor_step, st.step(f"{name}.T"))

            columns("c", 8, 4, rows_c)
            pe.wait_ge(inputs_loaded, st.at("const.loaded"))
            bias_rows()
            columns("V", 96, 5, rows_v)
            columns("W", 43, 6, rows_w)
            columns("P", 27, 7, rows)
            pe.wait_ge(scalar_step, st.at("t5.ev"))
            pe.wait_ge(gpsimd_step, st.at("zeros"))
            st.r += KD
            ada_reduce(0, "P")
            pe.wait_ge(vector_step, st.at("P.ada0"))
            with st.loop("layers", LAYERS, LAYER_UNITS):
                mixer1()
                ffn("F", KD, lambda: columns("L", 27, 2, rows))
                ada_reduce(0)
                pe.wait_ge(vector_step, st.at("F.x1"))
            for i in range(4):
                ffn(f"{i}a")
                (hgrn, diff, pooling)[i % 3](f"{i}m")
                ffn(f"{i}b")

        @block.scalar
        def _(act):
            st = steps(act, scalar_step)

            def hi(n):
                act.wait_ge(unit_loaded[st.r % RING], st.units(16 * (st.r // RING + 1), 0, RING))
                act.wait_ge(unit_multiplied, st.units(st.n + 1, 1))
                act.activation(w_hi[st.n % RING][:, 0:n], raw[st.r % RING][:, 0:n], ACT.Copy).then_inc(unit_rounded, 1)
                st.r += 1
                st.n += 1

            def copy(out, in_, scale=1.0):
                return act.activation(out, in_, ACT.Copy, scale=scale)

            def square(name, i, src):
                st.apart()
                act.drain()
                act.activation(junk[:, 0:src.shape[-1]], src, ACT.Square, accum_out=stat[:, 0, i:i + 1]).then_inc(scalar_step, st.step(name))

            def boundary(post, p, prev=None, lead=0):
                for t in range(NT):
                    if post:
                        act.wait_ge(st.sem_of(f"{post}.y{t}"), st.at(f"{post}.y{t}"))
                        square(f"{post}.psq{t}", 4 + t, Yt[:, t, :])
                    if p and (t == 0 or not post):
                        act.wait_ge(vector_step, st.at(f"{prev}{t}"))
                        square(f"{p}.sq{t}", t, x[:, t, :])
                if p:
                    to_h(p, 0)
                    if post:
                        act.wait_ge(vector_step, st.at(f"{prev}1"))
                        square(f"{p}.sq1", 1, x[:, 1, :])
                    to_h(p, 1)
                if lead:
                    hi(lead)

            def to_h(p, t, a=None, b=None):
                a, b = gains(p) if a is None else (a, b)
                for g in range(2):
                    act.wait_ge(tensor_step, st.at(f"{p}.tr{t}.{g}"))
                    for k in range(4 * g, 4 * g + 4):
                        i = act.activation(h_hi[:, k, t * P:t * P + P],
                                           B[4 + 2 * t + k // 4][:, (k % 4) * P:(k % 4) * P + P], ACT.Identity,
                                           scale=a(k), bias=b(k) if b else 0.0)
                    i.then_inc(scalar_step, st.step(f"{p}.hh{t}.{g}"))

            def ffn(p, lead, between=0, columns=None):
                def skip():
                    st.r += between and 1

                def body(tag, prev, before=True, skip=lambda: None):
                    if before:
                        hi(2 * D)
                    skip()
                    hi(KD * CH)
                    act.wait_ge(unit_multiplied, st.at(f"{p}.{tag}.gate"))
                    act.activation(tmp[:, 0:2 * S], B[0], ACT.Silu).then_inc(scalar_step, st.step(f"{p}.{tag}.silu"))
                    if tag == "first":
                        skip()
                    hi(KD * CH)
                    act.wait_ge(vector_step, st.at(f"{p}.{tag}.mul"))
                    if before:
                        act.wait_ge(unit_multiplied, st.at(f"{p}.{tag}.down"))
                    act.activation(a_hi[:, 0:2, :].rearrange("p a b -> p (a b)"), tmp[:, 2 * S:4 * S], ACT.Copy)\
                        .then_inc(scalar_step, st.step(f"{p}.{tag}.ahi"))

                body("first", None, False, skip)
                skip()
                body("second", "first", True, skip)
                if columns:
                    columns()
                with st.loop(p, NCH - 3, STEP_UNITS):
                    body("loop", "loop")
                skip()
                skip()
                hi(2 * D)
                act.wait_ge(unit_multiplied, st.at(f"{p}.last.gate"))
                act.activation(tmp[:, 0:2 * S], B[0], ACT.Silu).then_inc(scalar_step, st.step(f"{p}.last.silu"))
                skip()
                hi(2 * D)
                skip()
                act.wait_ge(vector_step, st.at(f"{p}.last.mul"))
                act.activation(h_hi[:, 0:2, :].rearrange("p a b -> p (a b)"), tmp[:, 2 * S:4 * S], ACT.Copy)\
                    .then_inc(scalar_step, st.step(f"{p}.last.ahi"))
                if lead:
                    hi(lead)

            def lead_out():
                for _ in range(3):
                    hi(2 * D)

            def rest_out():
                hi(2 * D)
                hi(LEAD)

            LEAD = KD * CH

            def mixer1():
                p = "M"
                sizes = [KD * CH, KD * CH, KD * (CH + 4)] + [KD * CH] * 5 + [2 * 768, 512, 512]
                hi(sizes[0])
                hi(sizes[1])
                boundary(None, p, "x.ready")
                hi(sizes[2])
                act.wait_ge(unit_multiplied, st.at("M.c_q"))
                copy(lat[:, :, 0:CH], shape3(B[0], 2)).then_inc(scalar_step, st.step("M.c_q.ev"))
                hi(sizes[3])
                act.wait_ge(unit_multiplied, st.at("M.c_kv"))
                copy(lat[:, :, CH:CH + 160], shape3(B[1], 2)[:, :, CH - 160:CH]).then_inc(scalar_step, st.step("M.c_kv.ev"))
                act.wait_ge(scalar_step, st.at("M.c_kv.ev"))
                for t in range(NT):
                    square(f"M.sqq{t}", 2 * t, lat[:, t, 0:CH])
                    square(f"M.sqk{t}", 2 * t + 1, lat[:, t, CH:CH + P])
                hi(sizes[4])
                act.wait_ge(unit_multiplied, st.at("M.v_f"))
                for t in range(NT):
                    copy(vfm[:, t, 0:CH], B[2 + t][:, 0:CH])
                    copy(lat[:, t, 416:420], B[2 + t][:, CH:CH + 4]).then_inc(scalar_step, st.step(f"M.v_f.ev"))
                hi(sizes[5])
                act.wait_ge(gpsimd_step, st.at("M.z"))
                act.activation(ft[:, 1], ft[:, 0], ACT.Abs).then_inc(scalar_step, st.step("M.absz"))
                act.wait_ge(scalar_step, st.at("M.absz"))
                act.activation(ft[:, 1], ft[:, 1], ACT.Exp, scale=-1.0).then_inc(scalar_step, st.step("M.expz"))
                act.wait_ge(gpsimd_step, st.at("M.onez"))
                act.activation(ft[:, 1], ft[:, 1], ACT.Ln).then_inc(scalar_step, st.step("M.lnz"))
                act.wait_ge(tensor_step, st.at("M.latT"))
                for k in range(3):
                    i = act.activation(a_hi[:, k, :], B[4 + k // 2][:, (k % 2) * S:(k % 2) * S + S], ACT.Copy,
                                       scale=col[:, C_QLAT + k:C_QLAT + k + 1])
                i.then_inc(scalar_step, st.step("M.latT.hh"))
                act.wait_ge(unit_multiplied, st.at("M.q_f"))
                copy(qf[:, :, :], shape3(B[0], 2), scale=HD ** -0.5).then_inc(scalar_step, st.step("M.q_f.ev"))
                hi(sizes[6])
                act.wait_ge(tensor_step, st.at("M.F0"))
                for h in range(2):
                    copy(FQ[0:2, 2 * h:2 * h + 2, :], shape3(B[6 + h][0:2, :], 2)).then_inc(scalar_step, st.step("M.FQ"))
                hi(sizes[7])
                act.wait_ge(tensor_step, st.at("M.F1"))
                for h in range(2):
                    copy(FK[0:2, h, :, :], shape3(B[6 + h][0:2, :], 2)).then_inc(scalar_step, st.step("M.FK"))
                act.wait_ge(unit_multiplied, st.at("M.q_m"))
                copy(qm[:, :, :], shape3(B[2], 2), scale=HD ** -0.5).then_inc(scalar_step, st.step("M.q_m.ev"))
                hi(sizes[8])
                hi(sizes[9])
                act.wait_ge(unit_multiplied, st.at("M.v_m"))
                copy(vfm[:, :, CH:2 * CH], shape3(B[0], 2)).then_inc(scalar_step, st.step("M.v_m.ev"))
                hi(sizes[10])
                act.wait_ge(unit_multiplied, st.at("M.uq"))
                q0 = qlat[:, 0, :, :].rearrange("p h d -> p (h d)")
                copy(q0[:, 0:512], B[1])
                copy(q0[:, 512:768], B[2][:, 0:256]).then_inc(scalar_step, st.step("M.uq.ev"))

                def attend(js):
                    def evac(j):
                        _, _, t, s = js[j]
                        act.wait_ge(tensor_step, st.at(f"M.t{s}"))
                        if s >= 2:
                            act.wait_ge(tensor_step, st.at(f"M.o{s - 2}"))
                        copy(pT[:, s % 2, 0:(t + 1) * P], B[2 + s % 2][:, 0:(t + 1) * P]).then_inc(scalar_step, st.step(f"M.pT{s}"))

                    for j in range(len(js)):
                        _, _, t, s = js[j]
                        w = (t + 1) * P
                        act.wait_ge(vector_step, st.at(f"M.m{s}"))
                        if s >= 2:
                            act.wait_ge(tensor_step, st.at(f"M.t{s - 2}"))
                        act.activation(pb[:, s % 2, 0:w], ssb[:, s % 2, 0:w], ACT.Exp, scale=-1.0,
                                               bias=stats[:, 0, s:s + 1], accum_out=stats[:, 1, s:s + 1]).then_inc(scalar_step, st.step(f"M.e{s}"))
                        if j:
                            evac(j - 1)
                    evac(len(js) - 1)

                jobs = attention_jobs()
                attend(jobs[:16])
                for n in range(0, 8, 2):
                    act.wait_ge(tensor_step, st.at(f"M.ct{n}"))
                    dst = (qcT, kcT)[n // 4]
                    copy(dst[0:MLA_QK, (n % 4) * 2:(n % 4) * 2 + 2, :], shape3(B[n % 4][0:MLA_QK, :], 2)).then_inc(scalar_step, st.step(f"M.cT{n}"))
                attend(jobs[16:])
                st.r += 2 * KD
                lead_out()
                for t in range(NT):
                    act.wait_ge(vector_step, st.at(f"M.ob1.{t}"))
                    for g, (a, b) in enumerate(((0, 256), (256, 512), (512, 1024))):
                        square(f"M.osq{t}" if g == 2 else f"M.osq{t}.{g}", 3 * t + g, osb[:, t, a:b])
                for t in range(NT):
                    to_h("Mo", t, lambda k: col[:, C_GROUP + k:C_GROUP + k + 1])
                rest_out()

            def hgrn(p):
                def project(c):
                    last = c == 3
                    act.wait_ge(unit_multiplied, st.at(f"{p}.q{c}"))
                    if c:
                        act.wait_ge(vector_step, st.at(f"{p}.k_s{c - 1}"))
                    copy(hq[:, :, :], shape3(B[0], 2)).then_inc(scalar_step, st.step(f"{p}.q{c}.ev"))
                    hi(KD * CH)
                    act.wait_ge(unit_multiplied, st.at(f"{p}.f{c}"))
                    act.activation(hf.rearrange("p a b -> p (a b)"), B[1], ACT.Sigmoid).then_inc(scalar_step, st.step(f"{p}.f{c}.ev"))
                    hi(KD * CH)
                    act.wait_ge(unit_multiplied, st.at(f"{p}.g{c}"))
                    act.activation(hg[:, 2 * c:2 * c + 2, :], shape3(B[2], 2), ACT.Sigmoid).then_inc(scalar_step, st.step(f"{p}.g{c}.sig"))
                    if not last:
                        hi(KD * CH)
                    act.wait_ge(unit_multiplied, st.at(f"{p}.v{c}"))
                    copy(hv[:, :, c * CH:c * CH + CH], shape3(B[3], 2)).then_inc(scalar_step, st.step(f"{p}.v{c}.ev"))
                    if not last:
                        hi(KD * CH)

                def gates(c):
                    f = lambda v: v.rearrange("p a b -> p (a b)")
                    act.wait_ge(vector_step, st.at(f"{p}.k{c}"))
                    if c:
                        act.wait_ge(vector_step, st.at(f"{p}.dl{c - 1}"))
                    act.activation(f(hl), f(hf), ACT.Ln).then_inc(scalar_step, st.step(f"{p}.lf{c}"))
                    act.wait_ge(vector_step, st.at(f"{p}.dl{c}"))
                    if c >= 2:
                        act.wait_ge(tensor_step, st.at(f"{p}.oss{c - 2}"))
                    act.activation(f(q_r[c % 2]), f(hd), ACT.Exp)
                    act.activation(f(k_r[c % 2]), f(hd), ACT.Exp, scale=-1.0)
                    act.activation(f(e_b[c % 2]), f(hb), ACT.Exp)
                    act.activation(f(k_s[c % 2]), f(hl), ACT.Exp).then_inc(scalar_step, st.step(f"{p}.e{c}"))

                def recur(c):
                    act.wait_ge(tensor_step, st.at(f"{p}.kst{c}"))
                    copy(ksT.rearrange("p a b -> p (a b)"), B[4]).then_inc(scalar_step, st.step(f"{p}.ksT{c}"))
                    act.wait_ge(tensor_step, st.at(f"{p}.ho{2 * c + 1}"))
                    act.activation(osq.rearrange("p a b -> p (a b)"), B[5], ACT.Square).then_inc(scalar_step, st.step(f"{p}.osq{c}"))

                project(0)
                gates(0)
                project(1)
                recur(0)
                gates(1)
                project(2)
                recur(1)
                gates(2)
                project(3)
                recur(2)
                gates(3)
                recur(3)
                for g in range(4):
                    act.wait_ge(vector_step, st.at(f"{p}.on{g}"))
                    copy(h_hi[:, 2 * g:2 * g + 2, :], ho[:, 2 * g:2 * g + 2, :]).then_inc(scalar_step, st.step(f"{p}o.hh{g}"))
                lead_out()
                rest_out()

            def diff(p):
                for u in range(12):
                    if u < 10:
                        hi(KD * CH)
                    act.wait_ge(unit_multiplied, st.at(f"{p}.p{u}"))
                    if u < 4:
                        copy(dq[:, 2 * u:2 * u + 2, :], shape3(B[u % 4], 2), scale=HD ** -0.5).then_inc(scalar_step, st.step(f"{p}.p{u}.ev"))
                    elif u >= 8:
                        c = (u - 8) * CH
                        copy(dv[:, :, c:c + CH], shape3(B[u % 4], 2)).then_inc(scalar_step, st.step(f"{p}.p{u}.ev"))
                act.wait_ge(vector_step, st.at(f"{p}.lamsum"))
                act.activation(lam2[:, 2:4], lam2[:, 0:2], ACT.Exp).then_inc(scalar_step, st.step(f"{p}.lamexp"))

                def evac(j):
                    t = j % 2
                    act.wait_ge(tensor_step, st.at(f"{p}.t{j}"))
                    if j >= 2:
                        act.wait_ge(tensor_step, st.at(f"{p}.o{j - 2}"))
                    copy(dpT[:, j % 2, 0:(t + 1) * P], B[2 + j % 2][:, 0:(t + 1) * P]).then_inc(scalar_step, st.step(f"{p}.pT{j}"))

                for j in range(16):
                    w = (j % 2 + 1) * P
                    for i in (2 * j, 2 * j + 1):
                        act.wait_ge(vector_step, st.at(f"{p}.m{i}"))
                        if j >= 2:
                            act.wait_ge(vector_step, st.at(f"{p}.w{j - 2}"))
                        act.activation(dp[:, i % 4, 0:w], dss[:, i % 4, 0:w], ACT.Exp, scale=-1.0,
                                               bias=dstat[:, 0, i:i + 1], accum_out=dstat[:, 1, i:i + 1]).then_inc(scalar_step, st.step(f"{p}.e{i}"))
                    if j:
                        evac(j - 1)
                evac(15)
                lead_out()
                for t in range(NT):
                    act.wait_ge(tensor_step, st.at(f"{p}.o{14 + t}"))
                    act.activation(do[:, t, :], Yt[:, t, :], ACT.Square).then_inc(scalar_step, st.step(f"{p}.osq{t}"))
                for t in range(NT):
                    to_h(f"{p}o", t, lambda k: col[:, C_SUBS:C_SUBS + 1])
                rest_out()

            def pooling(p):
                for u in range(4):
                    hi(KD * CH)
                    act.wait_ge(unit_multiplied, st.at(f"{p}.p{u}"))
                    copy(pu[:, 2 * u:2 * u + 2, :], shape3(B[u], 2)).then_inc(scalar_step, st.step(f"{p}.p{u}.ev"))
                for g in range(4):
                    act.wait_ge(vector_step, st.at(f"{p}.pp{g}"))
                    copy(h_hi[:, 2 * g:2 * g + 2, :], ppT[:, 2 * g:2 * g + 2, :]).then_inc(scalar_step, st.step(f"{p}.pth{g}"))
                for g in range(4):
                    act.wait_ge(st.sem_of(f"{p}o.tr{g}"), st.at(f"{p}o.tr{g}"))
                    for k in (2 * g, 2 * g + 1):
                        i = act.activation(h_hi[:, k, :], B[4 + g][:, (k % 2) * S:(k % 2) * S + S], ACT.Identity,
                                           scale=col[:, C_PSCALE + k:C_PSCALE + k + 1])
                    i.then_inc(scalar_step, st.step(f"{p}o.hh{g}"))
                hi(2 * D)
                hi(2 * D)
                rest_out()

            for dst, src in ((rows_c[0:8, :], A["c"].rearrange("a (k p) -> (a k) p", p=P)), (ident[:, :], A["K_ident"])):
                act.dma_start(dst, src).then_inc(c_loaded, st.step("c.loaded", c_loaded, 16))
            for dst, src in ((lat[0:32, 0, 0:4], A["t5_table"]), (bucket, A["K_bucket"]), (firstc, A["K_first"]),
                             (x[:, 0, :], A["x"][0, 0:P, :]), (x[:, 1, :], A["x"][0, P:S, :])):
                act.dma_start(dst, src).then_inc(inputs_loaded, st.step("const.loaded", inputs_loaded, 16))
            act.wait_ge(tensor_step, st.at("c.T"))
            act.activation(col[:, C_C:C_C + KD], B[4][:, 0:KD], ACT.Silu).then_inc(scalar_step, st.step("c.col"))
            for dst, src in ((causal, A["K_causal"]), (tri.rearrange("p a b -> p (a b)"), A["K_tri"]),
                             (cs[:, 0].rearrange("p a b -> p (a b)"), A["K_cos"]),
                             (cs[:, 1].rearrange("p a b -> p (a b)"), A["K_sin"])):
                act.dma_start(dst, src).then_inc(gains_loaded, st.step("W.loaded", gains_loaded, 16))
            for i in range(4):
                for j in range(3):
                    act.dma_start(rows_v[(3 * i + j) * 8:(3 * i + j) * 8 + 8, :],
                                  A["norm_gains_2"][i, 2 * j:2 * j + 1, :].rearrange("a (k p) -> (a k) p", p=P))\
                        .then_inc(gains_loaded, st.step("W.loaded", gains_loaded, 16))
            for v, r, k in (("hgrn_lb_raw_2", 0, 32), ("hgrn_gnorm_2", 32, 2), ("diff_subln_2", 34, 1),
                            ("pool_scale_2", 35, 8)):
                act.dma_start(rows_w[r:r + k, :], A[v].rearrange("a (k p) -> (a k) p", p=P))\
                    .then_inc(gains_loaded, st.step("W.loaded", gains_loaded, 16))
            st.alias("V.loaded", "W.loaded")
            act.wait_ge(tensor_step, st.at("t5.rows"))
            for h in range(4):
                copy(t5_rows[:, h, :], B[h][:, 0:T5_W]).then_inc(scalar_step, st.step("t5.ev"))
            act.wait_ge(scalar_step, st.at("t5.ev"))
            act.dma_start(skew.rearrange("h (p j) -> p h j", j=T5_W + 1)[:, :, 0:T5_W], t5_rows)\
                .then_inc(t5_moved, st.step("t5.out", t5_moved, 16))
            act.wait_ge(tensor_step, st.at("V.T"))
            copy(col[:, C_SUB:C_SUB + 96], B[5][:, 0:96]).then_inc(scalar_step, st.step("V.col"))
            act.wait_ge(tensor_step, st.at("W.T"))
            copy(col[:, C_LB:C_LB + 43], B[6][:, 0:43]).then_inc(scalar_step, st.step("W.col"))
            act.wait_ge(t5_moved, st.at("t5.out"))
            act.dma_start(t5_bias, skew[:, 0:P * T5_W].rearrange("h (p j) -> p h j", j=T5_W)[:, :, P - 1:P - 1 + S])\
                .then_inc(t5_moved, st.step("t5.bias", t5_moved, 16))
            act.wait_ge(tensor_step, st.at("P.T"))
            copy(col[:, 0:27], B[7][:, 0:27]).then_inc(scalar_step, st.step("P.col"))
            act.wait_ge(vector_step, st.at("lb.in"))
            act.activation(col[:, C_LB:C_LB + 32], col[:, C_LB:C_LB + 32], ACT.Exp).then_inc(scalar_step, st.step("lb.exp"))
            st.r += KD

            def next_columns():
                act.wait_ge(tensor_step, st.at("L.T"))
                copy(col[:, 0:27], B[2][:, 0:27]).then_inc(scalar_step, st.step("L.col"))

            with st.loop("layers", LAYERS, LAYER_UNITS):
                mixer1()
                boundary("M", "F", "M.x", LEAD)
                ffn("F", 0, KD, next_columns)
                boundary("F", None)
                act.wait_ge(vector_step, st.at("F.x1"))
            hi(LEAD)
            hi(LEAD)
            boundary(None, names[0], "x.ready")
            for s, p in enumerate(names):
                if p[1] == "m":
                    (hgrn, diff, pooling)[int(p[0]) % 3](p)
                else:
                    ffn(p, LEAD if s + 1 < len(names) else 0)
                if s + 1 < len(names):
                    boundary(p, names[s + 1], f"{p}.x", LEAD)
                else:
                    boundary(p, None)

        @block.vector
        def _(dve):
            st = steps(dve, vector_step, {unit_split.name: RING})
            dve.sem_inc(unit_split, RING)
            flat = lambda v: v.rearrange("p a b -> p (a b)")

            def lo(n):
                dve.wait_ge(unit_rounded, st.units(st.n + 1, 1))
                s = st.n % RING
                dve.tensor_tensor(w_lo[s][:, 0:n], raw[st.r % RING][:, 0:n], w_hi[s][:, 0:n].bitcast(F32),
                                          ALU.subtract).then_inc(unit_split, st.step("", unit_split))
                st.r += 1
                st.n += 1

            def ts(o, i, a, b, op0=ALU.mult, op1=ALU.add):
                return dve.tensor_scalar(o, i, a, b, op0, op1) if b is not None else \
                    dve.tensor_scalar(o, i, a, None, op0)

            def tt(o, a, b, op):
                return dve.tensor_tensor(o, a, b, op)

            def pre(p, t):
                dve.wait_ge(gpsimd_step, st.at(f"{p}.rs{t}"))
                for g in range(2):
                    ts(xn[:, t, g * 512:g * 512 + 512], x[:, t, g * 512:g * 512 + 512], stat[:, 2, t:t + 1], None)\
                        .then_inc(vector_step, st.step(f"{p}.xn{t}.{g}"))

            def boundary(done, p, n=0, factor=1.0, lead=0):
                for t in range(NT):
                    if done:
                        dve.wait_ge(gpsimd_step, st.at(f"{done}.prs{t}"))
                        dve.wait_ge(st.sem_of(f"{done}.post"), st.at(f"{done}.post"))
                        if t:
                            dve.wait_ge(vector_step, st.at(f"{done}.x0"))
                        dve.scalar_tensor_tensor(tmp[:, :], Yt[:, t, :], stat[:, 2, 4 + t:5 + t], post[n][:, :],
                                                 ALU.mult, ALU.mult)
                        dve.drain()
                        dve.scalar_tensor_tensor(x[:, t, :], tmp[:, :], factor, x[:, t, :], ALU.mult, ALU.add)\
                            .then_inc(vector_step, st.step(f"{done}.x{t}"))
                    if p and t == 0:
                        pre(p, 0)
                if p:
                    if done:
                        dve.wait_ge(vector_step, st.at(f"{done}.x1"))
                    to_h(p, 0)
                    pre(p, 1)
                    to_h(p, 1)
                if lead:
                    lo(lead)

            def to_h(p, t, a=None, b=None):
                a, b = gains(p) if a is None else (a, b)
                for g in range(2):
                    dve.wait_ge(scalar_step, st.at(f"{p}.hh{t}.{g}"))
                    part = lambda k: B[4 + 2 * t + k // 4][:, (k % 4) * P:(k % 4) * P + P]
                    if b:
                        for k in range(4 * g, 4 * g + 4):
                            ts(tmp[:, k * P:k * P + P], part(k), a(k), b(k))
                        dve.drain()
                    for k in range(4 * g, 4 * g + 4):
                        o, h = h_lo[:, k, t * P:t * P + P], h_hi[:, k, t * P:t * P + P].bitcast(F32)
                        if b:
                            i = dve.tensor_tensor(o, tmp[:, k * P:k * P + P], h, ALU.subtract)
                        else:
                            i = dve.scalar_tensor_tensor(o, part(k), a(k), h, ALU.mult, ALU.subtract)
                    i.then_inc(vector_step, st.step(f"{p}.h{t}.{g}"))

            def ffn(p, lead, between=lambda k: None):
                def body(tag, prev, before=True, k=None):
                    if before:
                        lo(2 * D)
                    if k is not None:
                        between(k)
                    lo(KD * CH)
                    if before:
                        dve.wait_ge(vector_step, st.at(f"{p}.{prev}.act", int(tag == "loop")))
                    dve.wait_ge(scalar_step, st.at(f"{p}.{tag}.silu"))
                    dve.wait_ge(unit_multiplied, st.at(f"{p}.{tag}.up"))
                    tt(tmp[:, 2 * S:4 * S], tmp[:, 0:2 * S], B[1], ALU.mult)\
                        .then_inc(vector_step, st.step(f"{p}.{tag}.mul"))
                    if tag == "first":
                        between(1)
                    lo(KD * CH)
                    dve.wait_ge(scalar_step, st.at(f"{p}.{tag}.ahi"))
                    tt(flat(a_lo[:, 0:2, :]), tmp[:, 2 * S:4 * S], flat(a_hi[:, 0:2, :].bitcast(F32)), ALU.subtract)\
                        .then_inc(vector_step, st.step(f"{p}.{tag}.act"))

                body("first", None, False, 0)
                between(2)
                body("second", "first", True, 3)
                with st.loop(p, NCH - 3, STEP_UNITS):
                    body("loop", "loop")
                between(4)
                between(5)
                lo(2 * D)
                between(6)
                lo(2 * D)
                dve.wait_ge(vector_step, st.at(f"{p}.loop.act"))
                dve.wait_ge(scalar_step, st.at(f"{p}.last.silu"))
                dve.wait_ge(unit_multiplied, st.at(f"{p}.last.up"))
                tt(tmp[:, 2 * S:4 * S], tmp[:, 0:2 * S], B[1], ALU.mult)\
                    .then_inc(vector_step, st.step(f"{p}.last.mul"))
                dve.wait_ge(scalar_step, st.at(f"{p}.last.ahi"))
                tt(flat(h_lo[:, 0:2, :]), tmp[:, 2 * S:4 * S], flat(h_hi[:, 0:2, :].bitcast(F32)), ALU.subtract)\
                    .then_inc(vector_step, st.step(f"{p}.last.act"))
                between(7)
                if lead:
                    lo(lead)

            def lead_out():
                for _ in range(3):
                    lo(2 * D)

            def rest_out():
                lo(2 * D)
                lo(LEAD)

            LEAD = KD * CH

            def mac(third, k, m="M"):
                if k == 0:
                    dve.wait_ge(bias_loaded, st.at(f"{m}.bias{third}"))
                dve.wait_ge(unit_loaded[st.r % RING], st.units(16 * (st.r // RING + 1), 0, RING))
                dve.wait_ge(unit_split, st.units(st.r + RING, 0))
                dve.scalar_tensor_tensor(acc, raw[st.r % RING][:, 0:ADA_W], col[:, C_C + k:C_C + k + 1], acc,
                                                 ALU.mult, ALU.add).then_inc(unit_split, st.step(f"{m}.acc{third}", unit_split))
                st.r += 1

            def first_modulation(m, columns):
                dve.wait_ge(scalar_step, st.at(columns))
                dve.wait_ge(tensor_step, st.at(f"{m}.cols0.1"))
                ts(col[:, C_MIXB:C_MIXB + KD], B[3][:, 0:KD], 1.0, None)
                dve.scalar_tensor_tensor(col[:, C_MIXA:C_MIXA + KD], B[3][:, KD:2 * KD], 1.0, col[:, C_MIX:C_MIX + KD],
                                         ALU.add, ALU.mult).then_inc(vector_step, st.step(f"{m}.ada0"))

            def modulation(third):
                cb = B[0]
                if third == 1:
                    dve.wait_ge(tensor_step, st.at("M.cols1.1"))
                    ts(col[:, C_FFNB:C_FFNB + KD], cb[:, KD:2 * KD], 1.0, None).then_inc(vector_step, st.step("M.ada1"))
                else:
                    dve.wait_ge(tensor_step, st.at("M.cols2.0"))
                    dve.scalar_tensor_tensor(col[:, C_FFNA:C_FFNA + KD], cb[:, 0:KD], 1.0,
                                                     col[:, C_FFN:C_FFN + KD], ALU.add, ALU.mult).then_inc(vector_step, st.step("M.ada2"))
                dve.wait_ge(tensor_step, st.at(f"M.rows{third}"))
                dve.wait_ge(post_gain_loaded[0], st.at("L.post"))
                g = post[third - 1]
                for c in range(2):
                    tt(g[:, c * 512:c * 512 + 512], g[:, c * 512:c * 512 + 512], B[1 + c], ALU.mult).then_inc(vector_step, st.step(f"M.gate{third}"))
                st.alias("MF"[third - 1] + ".post", f"M.gate{third}")

            def mixer1():
                sizes = [KD * CH, KD * CH, KD * (CH + 4)] + [KD * CH] * 5 + [2 * 768, 512, 512]
                lo(sizes[0])
                lo(sizes[1])
                boundary(None, "M")
                lo(sizes[2])
                lo(sizes[3])
                dve.wait_ge(gpsimd_step, st.at("M.rsl"))
                for t in range(NT):
                    ts(lat[:, t, 0:CH], lat[:, t, 0:CH], stat[:, 2, 2 * t:2 * t + 1], None)
                    ts(lat[:, t, CH:CH + P], lat[:, t, CH:CH + P], stat[:, 2, 2 * t + 1:2 * t + 2], None).then_inc(vector_step, st.step(f"M.latn{t}"))
                lo(sizes[4])
                lo(sizes[5])
                dve.wait_ge(scalar_step, st.at("M.latT.hh"))
                for k in range(3):
                    i = dve.scalar_tensor_tensor(a_lo[:, k, :], B[4 + k // 2][:, (k % 2) * S:(k % 2) * S + S],
                                                 col[:, C_QLAT + k:C_QLAT + k + 1], a_hi[:, k, :].bitcast(F32),
                                                 ALU.mult, ALU.subtract)
                i.then_inc(vector_step, st.step("M.latT.h"))
                lo(sizes[6])
                heads = lambda dst, b, name: (
                    ts(dst[0:HD, 0:4:2, :], shape3(b[0:HD, :], 2), 1.0, None),
                    ts(dst[HD:P, 1:4:2, :], shape3(b[HD:P, :], 2), 1.0, None).then_inc(vector_step, st.step(name)))
                dve.wait_ge(unit_multiplied, st.at("M.k_f"))
                heads(kf, B[1], "M.k_f.ev")
                lo(sizes[7])
                lo(sizes[8])
                dve.wait_ge(unit_multiplied, st.at("M.k_m"))
                heads(km, B[3], "M.k_m.ev")
                lo(sizes[9])
                lo(sizes[10])
                dve.wait_ge(unit_multiplied, st.at("M.uq"))
                q1 = qlat[:, 1, :, :].rearrange("p h d -> p (h d)")
                ts(q1[:, 0:512], B[3], 1.0, None)
                ts(q1[:, 512:768], B[6][:, 0:256], 1.0, None).then_inc(vector_step, st.step("M.uq.ev1"))
                for c in range(2):
                    dve.wait_ge(unit_multiplied, st.at(f"M.ukv{c}"))
                    for t in range(NT):
                        v = B[[(0, 7), (4, 5)][c][t]].rearrange("p (h d) -> p h d", h=4)
                        ts(klat[:, t, 4 * c:4 * c + 4, 0:HD], v[:, :, 0:HD], 1.0, None)
                        ts(vc[:, t, c * CH:c * CH + CH].rearrange("p (h d) -> p h d", h=4), v[:, :, HD:P], 1.0, None).then_inc(vector_step, st.step(f"M.ukv{c}.ev"))

                def attend(js, third):
                    dve.wait_ge(t5_moved, st.at("t5.bias"))
                    for j, (kind, h, t, s) in enumerate(js):
                        w = (t + 1) * P
                        bias = t5_bias[:, h, S - w:S] if kind == "moba" else causal[:, S - w:S]
                        dve.wait_ge(tensor_step, st.at(f"M.s{s}"))
                        if s >= 2:
                            dve.wait_ge(scalar_step, st.at(f"M.e{s - 2}"))
                        st.apart()
                        dve.tensor_tensor_reduce(ssb[:, s % 2, 0:w], B[s % 2][:, 0:w], bias,
                                                         -(MLA_QK ** -0.5) if kind == "mla" else -1.0, BIG,
                                                         ALU.add, ALU.min, stats[:, 0, s:s + 1]).then_inc(vector_step, st.step(f"M.m{s}"))
                        if j % 2:
                            mac(third, j // 2)
                    h0 = js[0][3]
                    dve.wait_ge(scalar_step, st.at(f"M.e{js[-1][3]}"))
                    dve.reciprocal(stats[:, 2, h0:h0 + 16], stats[:, 1, h0:h0 + 16]).then_inc(vector_step, st.step(f"M.ri{h0}"))
                    dve.wait_ge(tensor_step, st.at(f"M.o{js[-1][3]}"))
                    dve.wait_ge(vector_step, st.at(f"M.ri{h0}"))
                    half = h0 // 16
                    dve.wait_ge(gpsimd_step, st.at("M.rope"))
                    for t in range(NT):
                        r = stats[:, 2, h0:h0 + 16].rearrange("p (h t) -> p h t", t=NT)[:, :, t:t + 1]
                        cs_ = slice(half * 512, half * 512 + 512)
                        tt(osb[:, t, cs_].rearrange("p (h d) -> p h d", h=8), Yt[:, t, cs_].rearrange("p (h d) -> p h d", h=8), r.to_broadcast([P, 8, HD]), ALU.mult).then_inc(vector_step, st.step(f"M.ob{half}.{t}"))

                jobs = attention_jobs()
                attend(jobs[:16], 1)
                modulation(1)
                for n in range(1, 8, 2):
                    dve.wait_ge(tensor_step, st.at(f"M.ct{n}"))
                    dst = (qcT, kcT)[n // 4]
                    ts(dst[0:MLA_QK, (n % 4) * 2:(n % 4) * 2 + 2, :], shape3(B[n % 4][0:MLA_QK, :], 2), 1.0, None).then_inc(vector_step, st.step(f"M.cT{n}"))
                attend(jobs[16:], 2)
                modulation(2)
                lead_out()
                for t in range(NT):
                    dve.wait_ge(gpsimd_step, st.at(f"M.ors{t}"))
                    for g, (a, b) in enumerate(((0, 256), (256, 512), (512, 1024))):
                        ts(osb[:, t, a:b], osb[:, t, a:b], stat[:, 2, 3 * t + g:3 * t + g + 1], None).then_inc(vector_step, st.step(f"Mo.on{t}"))
                for t in range(NT):
                    to_h("Mo", t, lambda k: col[:, C_GROUP + k:C_GROUP + k + 1])
                rest_out()

            def hgrn(p):
                layer = int(p[0]) // 3

                def project(c):
                    lo(KD * CH)
                    dve.wait_ge(scalar_step, st.at(f"{p}.f{c}.ev"))
                    for h in range(2):
                        k = 2 * c + h + 8 * layer
                        ts(hf[:, h, :], hf[:, h, :], col[:, C_OML + k:C_OML + k + 1], col[:, C_LBV + k:C_LBV + k + 1]).then_inc(vector_step, st.step(f"{p}.f{c}.{h}"))
                    lo(KD * CH)
                    dve.wait_ge(vector_step, st.at(f"{p}.f{c}.1"))
                    ts(flat(hk), flat(hf), -1.0, 1.0).then_inc(vector_step, st.step(f"{p}.k{c}"))
                    dve.wait_ge(scalar_step, st.at(f"{p}.g{c}.sig"))
                    tt(hg[:, 2 * c:2 * c + 2, :], hg[:, 2 * c:2 * c + 2, :], shape3(B[2], 2), ALU.mult).then_inc(vector_step, st.step(f"{p}.g{c}.ev"))
                    if c < 3:
                        lo(KD * CH)
                        lo(KD * CH)

                def gates(c):
                    blocks = lambda v: flat(v).rearrange("p (b i) -> p b i", i=HB)
                    dve.wait_ge(scalar_step, st.at(f"{p}.lf{c}"))
                    dve.tensor_tensor_scan(flat(hb), scan_mask, flat(hl), 0.0, ALU.mult, ALU.add).then_inc(vector_step, st.step(f"{p}.b{c}"))
                    dve.wait_ge(vector_step, st.at(f"{p}.b{c}"))
                    full = [P, 2 * S // HB, HB]
                    tt(blocks(hd), blocks(hb), blocks(hb)[:, :, HB // 2:HB // 2 + 1].to_broadcast(full), ALU.subtract)
                    tt(blocks(hl), blocks(hb)[:, :, HB - 1:HB].to_broadcast(full), blocks(hb), ALU.subtract).then_inc(vector_step, st.step(f"{p}.dl{c}"))
                    dve.wait_ge(scalar_step, st.at(f"{p}.e{c}"))
                    i = c % 2
                    tt(flat(q_r[i]), flat(q_r[i]), flat(hq), ALU.mult)
                    tt(flat(k_r[i]), flat(k_r[i]), flat(hk), ALU.mult)
                    tt(flat(q_i[i]), flat(e_b[i]), flat(hq), ALU.mult)
                    tt(flat(k_s[i]), flat(k_s[i]), flat(hk), ALU.mult).then_inc(vector_step, st.step(f"{p}.k_s{c}"))

                def recur(c):
                    dve.wait_ge(tensor_step, st.at(f"{p}.a{c}"))
                    dve.copy_predicated(flat(atm), intra.bitcast(U32), B[4]).then_inc(vector_step, st.step(f"{p}.atm{c}"))
                    for h in range(2):
                        hh = 2 * c + h
                        if hh >= 2:
                            dve.wait_ge(tensor_step, st.at(f"{p}.ho{hh - 2}"))
                        for nb in range(2 * NHB - 1):
                            i = hh * 4 + nb // 4
                            if nb % 4 == 0:
                                dve.wait_ge(tensor_step, st.at(f"{p}.u{i}"))
                            u = B[6 + i % 2][:, (nb % 4) * P:(nb % 4) * P + P]
                            if nb == 0:
                                ts(hist[h][:, 1, :], u, 1.0, None).then_inc(vector_step, st.step(f"{p}.S{hh}.1"))
                            else:
                                dve.wait_ge(vector_step, st.at(f"{p}.S{hh}.{nb}"))
                                dve.scalar_tensor_tensor(
                                    hist[h][:, nb + 1, :], hist[h][:, nb, :],
                                    e_b[c % 2][:, h, nb * HB + HB - 1:nb * HB + HB], u, ALU.mult, ALU.add).then_inc(vector_step, st.step(f"{p}.S{hh}.{nb + 1}"))
                            if nb % 4 == 3 or nb == 2 * NHB - 2:
                                st.alias(f"{p}.st{i}", f"{p}.S{hh}.{nb + 1}")
                    dve.wait_ge(tensor_step, st.at(f"{p}.oss{c}"))
                    dve.scalar_tensor_tensor(ho[:, 2 * c:2 * c + 2, :], shape3(B[5], 2),
                                             col[:, C_GN + layer:C_GN + layer + 1], hg[:, 2 * c:2 * c + 2, :],
                                             ALU.mult, ALU.mult).then_inc(vector_step, st.step(f"{p}.hog{c}"))
                    ts(hstat[:, 0:4], B[4][:, 0:4], 1.0 / P, EPS).then_inc(vector_step, st.step(f"{p}.oms{c}"))
                    dve.wait_ge(gpsimd_step, st.at(f"{p}.orr{c}"))
                    full = [P, 4, P]
                    tt(diag.rearrange("p (a b) -> p a b", a=4), ident[:, :].unsqueeze(1).to_broadcast(full),
                       hstat[:, 4:8].unsqueeze(2).to_broadcast(full), ALU.mult)\
                        .then_inc(vector_step, st.step(f"{p}.diag{c}"))
                    dve.wait_ge(tensor_step, st.at(f"{p}.obc{c}"))
                    tt(ho[:, 2 * c:2 * c + 2, :], ho[:, 2 * c:2 * c + 2, :], shape3(B[4], 2), ALU.mult)\
                        .then_inc(vector_step, st.step(f"{p}.on{c}"))

                dve.memset(flat(atm), 0.0)
                dve.wait_ge(vectors_loaded, st.at(f"{p}.const"))
                project(0)
                gates(0)
                project(1)
                recur(0)
                gates(1)
                project(2)
                recur(1)
                gates(2)
                project(3)
                recur(2)
                gates(3)
                recur(3)
                for g in range(4):
                    dve.wait_ge(scalar_step, st.at(f"{p}o.hh{g}"))
                    tt(h_lo[:, 2 * g:2 * g + 2, :], ho[:, 2 * g:2 * g + 2, :], h_hi[:, 2 * g:2 * g + 2, :].bitcast(F32), ALU.subtract).then_inc(vector_step, st.step(f"{p}o.h{g}"))
                lead_out()
                rest_out()

            def diff(p):
                dve.wait_ge(vectors_loaded, st.at(f"{p}.const"))
                for h in range(DIFF_H):
                    ts(dbias[:, h, :], cdist, -(2.0 ** (-8.0 * (h + 1) / DIFF_H)), None)
                for g in range(2):
                    ins = dve.tensor_tensor_reduce(dw[:, g, 0:HD], lamrow[:, 2 * g, :], lamrow[:, 2 * g + 1, :], 1.0, 0.0,
                                             ALU.mult, ALU.add, lam2[:, g:g + 1])
                    if g:
                        ins.then_inc(vector_step, st.step(f"{p}.lamsum"))
                dve.wait_ge(gpsimd_step, st.at(f"{p}.zero"))
                for u in range(12):
                    if u < 10:
                        lo(KD * CH)
                    if 4 <= u < 8:
                        c = 4 * (u - 4)
                        dve.wait_ge(unit_multiplied, st.at(f"{p}.p{u}"))
                        ts(dk[0:HD, c:c + 4:2, :], shape3(B[u % 4][0:HD, :], 2), 1.0, None)
                        ts(dk[HD:P, c + 1:c + 4:2, :], shape3(B[u % 4][HD:P, :], 2), 1.0, None).then_inc(vector_step, st.step(f"{p}.p{u}.ev"))
                lam_init = 0.8 - 0.6 * float(np.exp(-0.3 * DIFF_LAYER))
                dve.wait_ge(scalar_step, st.at(f"{p}.lamexp"))
                tt(lam2[:, 4:5], lam2[:, 3:4], lam2[:, 2:3], ALU.subtract)
                ts(col[:, C_SUBS:C_SUBS + 1], col[:, C_SUBLN:C_SUBLN + 1], 1.0 - lam_init, None)
                dve.drain()
                ts(lam2[:, 5:6], lam2[:, 4:5], -lam_init, None, ALU.add)

                def scores(j):
                    h, t = divmod(j, 2)
                    w = (t + 1) * P
                    for i in (2 * j, 2 * j + 1):
                        dve.wait_ge(tensor_step, st.at(f"{p}.s{i}"))
                        if i >= 4:
                            dve.wait_ge(scalar_step, st.at(f"{p}.e{i - 4}"))
                        dve.tensor_tensor_reduce(dss[:, i % 4, 0:w], B[i % 2][:, 0:w], dbias[:, h, S - w:S],
                                                         -1.0, BIG, ALU.add, ALU.min, dstat[:, 0, i:i + 1]).then_inc(vector_step, st.step(f"{p}.m{i}"))

                def combine(j):
                    w = (j % 2 + 1) * P
                    i = 2 * j
                    dve.wait_ge(scalar_step, st.at(f"{p}.e{i + 1}"))
                    if j >= 2:
                        dve.wait_ge(tensor_step, st.at(f"{p}.t{j - 2}"))
                    dve.reciprocal(dstat[:, 2, i:i + 2], dstat[:, 1, i:i + 2])
                    dve.drain()
                    ts(dt1[:, j % 2, 0:w], dp[:, (i + 1) % 4, 0:w], dstat[:, 2, i + 1:i + 2], lam2[:, 5:6],
                       ALU.mult, ALU.mult)
                    dve.drain()
                    dve.scalar_tensor_tensor(dw[:, j % 2, 0:w], dp[:, i % 4, 0:w], dstat[:, 2, i:i + 1],
                                                     dt1[:, j % 2, 0:w], ALU.mult, ALU.add).then_inc(vector_step, st.step(f"{p}.w{j}"))

                scores(0)
                for j in range(16):
                    if j < 15:
                        scores(j + 1)
                    combine(j)
                lead_out()
                for t in range(NT):
                    dve.wait_ge(scalar_step, st.at(f"{p}.osq{t}"))
                    dve.tensor_reduce(dstat[:, 3, 8 * t:8 * t + 8],
                                              do[:, t, :].rearrange("p (h d) -> p h d", h=DIFF_H), AXX, ALU.add).then_inc(vector_step, st.step(f"{p}.oss{t}"))
                for t in range(NT):
                    dve.wait_ge(gpsimd_step, st.at(f"{p}.ors{t}"))
                    r = dstat[:, 3, 16 + 8 * t:24 + 8 * t].unsqueeze(2)
                    tt(do[:, t, :].rearrange("p (h d) -> p h d", h=DIFF_H), Yt[:, t, :].rearrange("p (h d) -> p h d", h=DIFF_H), r.to_broadcast([P, DIFF_H, P]), ALU.mult).then_inc(vector_step, st.step(f"{p}o.on{t}"))
                for t in range(NT):
                    to_h(f"{p}o", t, lambda k: col[:, C_SUBS:C_SUBS + 1])
                rest_out()

            def pooling(p):
                dve.wait_ge(vectors_loaded, st.at(f"{p}.const"))
                for g, w in enumerate(POOL_WINDOWS):
                    lo(KD * CH)
                    dve.wait_ge(scalar_step, st.at(f"{p}.p{g}.ev"))
                    if g:
                        dve.wait_ge(vector_step, st.at(f"{p}.pp{g - 1}"))
                    u = cur = pu[:, 2 * g:2 * g + 2, :]
                    d, i = 1, 0
                    while d < w:
                        nxt = ps_a[i % 2]
                        tt(nxt[:, :, d:S], cur[:, :, d:S], cur[:, :, 0:S - d], ALU.add)
                        ts(nxt[:, :, 0:d], cur[:, :, 0:d], 1.0, None)
                        dve.drain()
                        cur, d, i = nxt, 2 * d, i + 1
                    nxt = ps_a[i % 2]
                    tt(nxt, cur, counts[:, g:g + 1, :].to_broadcast([P, 2, S]), ALU.mult)
                    dve.drain()
                    tt(ppT[:, 2 * g:2 * g + 2, :], nxt, u, ALU.subtract).then_inc(vector_step, st.step(f"{p}.pp{g}"))
                for g in range(4):
                    dve.wait_ge(scalar_step, st.at(f"{p}.pth{g}"))
                    tt(h_lo[:, 2 * g:2 * g + 2, :], ppT[:, 2 * g:2 * g + 2, :], h_hi[:, 2 * g:2 * g + 2, :].bitcast(F32), ALU.subtract).then_inc(vector_step, st.step(f"{p}.pt{g}"))
                for g in range(4):
                    dve.wait_ge(scalar_step, st.at(f"{p}o.hh{g}"))
                    for k in (2 * g, 2 * g + 1):
                        i = dve.scalar_tensor_tensor(h_lo[:, k, :], B[4 + g][:, (k % 2) * S:(k % 2) * S + S],
                                                     col[:, C_PSCALE + k:C_PSCALE + k + 1],
                                                     h_hi[:, k, :].bitcast(F32), ALU.mult, ALU.subtract)
                    i.then_inc(vector_step, st.step(f"{p}o.h{g}"))
                lo(2 * D)
                lo(2 * D)
                rest_out()

            def lower_bounds():
                lb = lambda i: col[:, C_LB + 8 * i:C_LB + 8 * i + 8]
                mx, sm = xn[:, 0, 0:8], xn[:, 0, 8:16]
                dve.wait_ge(scalar_step, st.at("W.col"))
                tt(mx, lb(0), lb(1), ALU.max)
                for i in (2, 3):
                    dve.drain()
                    tt(mx, mx, lb(i), ALU.max)
                dve.drain()
                for i in range(4):
                    tt(lb(i), lb(i), mx, ALU.subtract).then_inc(vector_step, st.step("lb.in"))
                dve.wait_ge(scalar_step, st.at("lb.exp"))
                tt(sm, lb(0), lb(1), ALU.add)
                for i in (2, 3):
                    dve.drain()
                    tt(sm, sm, lb(i), ALU.add)
                dve.drain()
                dve.reciprocal(mx, sm)
                dve.drain()
                for i in range(4):
                    tt(lb(i), lb(i), mx, ALU.mult)
                dve.drain()
                tt(sm, lb(0), lb(1), ALU.add)
                dve.drain()
                tt(sm, sm, lb(2), ALU.add)
                dve.drain()
                tt(sm, sm, lb(3), ALU.add)
                dve.drain()
                v = lambda i: col[:, C_LBV + 8 * i:C_LBV + 8 * i + 8]
                tt(v(0), lb(0), lb(0), ALU.subtract)
                tt(v(1), sm, lb(0), ALU.subtract)
                dve.drain()
                ts(col[:, C_OML:C_OML + 16], col[:, C_LBV:C_LBV + 16], -1.0, 1.0)

            dve.wait_ge(scalar_step, st.at("c.col"))
            for k in range(2):
                mac(0, k, "P")
            dve.wait_ge(inputs_loaded, st.at("const.loaded"))
            for h in range(4):
                ts(t5_lhs[0:32, h * P:h * P + P], lat[0:32, 0, h:h + 1].to_broadcast([32, P]), 1.0, None)
            dve.memset(t5_lhs[32:33, :], NEG).then_inc(vector_step, st.step("t5.lhs"))
            for t in range(NT):
                ts(fa[:, t, :, 1], firstc[:, t:t + 1].to_broadcast([P, 4]), 1.0, None)
                ts(fb[:, t, :, 0], firstc[:, t:t + 1].to_broadcast([P, 4]), 1.0, None)\
                    .then_inc(vector_step, st.step("x.ready0"))
            st.alias("x.ready1", "x.ready0")
            for k in range(2, KD):
                mac(0, k, "P")
            first_modulation("P", "P.col")
            lower_bounds()
            with st.loop("layers", LAYERS, LAYER_UNITS):
                mixer1()
                boundary("M", "F", 0, 1.0, LEAD)
                ffn("F", 0, lambda k: mac(0, k))
                boundary("F", None, 1)
                first_modulation("M", "L.col")
            lo(LEAD)
            lo(LEAD)
            boundary(None, names[0])
            for s, p in enumerate(names):
                more = s + 1 < len(names)
                if p[1] == "m":
                    (hgrn, diff, pooling)[int(p[0]) % 3](p)
                else:
                    ffn(p, LEAD if more else 0)
                boundary(p, names[s + 1] if more else None, s % 2, 1.0 if p[1] == "m" else 0.5, LEAD if more else 0)

        @block.gpsimd
        def _(pool):
            st = steps(pool, gpsimd_step)

            def rms(name, after, i0, i1, n, i2=1):
                pool.wait_ge(scalar_step, st.at(after))
                st.apart()
                a = slice(i0, i1, i2)
                pool.tensor_scalar(stat[:, 1, a], stat[:, 0, a], 1.0 / n, EPS, ALU.mult, ALU.add).then_inc(gpsimd_step, st.step(f"{name}.ms"))
                pool.wait_ge(gpsimd_step, st.at(f"{name}.ms"))
                st.apart()
                pool.tensor_tensor(stat[:, 2, a], stat[:, 1, a], half_power[:, 0:(i1 - i0 + i2 - 1) // i2],
                                           ALU.pow).then_inc(gpsimd_step, st.step(name))

            def boundary(post, p):
                for t in range(NT):
                    if post:
                        rms(f"{post}.prs{t}", f"{post}.psq{t}", 4 + t, 5 + t, D)
                    if p:
                        rms(f"{p}.rs{t}", f"{p}.sq{t}", t, t + 1, D)

            def acc_bias(third, l, m="M"):
                if m == "M":
                    before = {1: "M.cols0.1", 2: "M.cols1.1", 0: "M.cols2.0"}[third]
                    pool.wait_ge(tensor_step, st.at(before, int(third == 1)))
                    st.apart()
                pool.memset(acc, 0.0).then_inc(gpsimd_step, st.step(f"{m}.zero{third}"))
                pool.wait_ge(gpsimd_step, st.at(f"{m}.zero{third}"))
                st.apart()
                pool.dma_start(acc[0:1, :], A["b_ada"][bass.ds(l, 1), third * ADA_W:third * ADA_W + ADA_W])\
                    .then_inc(bias_loaded, st.step(f"{m}.bias{third}", bias_loaded, 16))

            def vec(t, l):
                return t[bass.ds(l, 1), :].rearrange("a (k p) -> (a k) p", p=P)

            def mixer1(l):
                boundary(None, "M")
                acc_bias(1, l)
                for n, i0, w in (("q", 0, CH), ("k", 1, P)):
                    pool.wait_ge(scalar_step, st.at("M.sqk1"))
                    st.apart()
                    pool.tensor_scalar(stat[:, 1, i0:4:2], stat[:, 0, i0:4:2], 1.0 / w, EPS, ALU.mult, ALU.add).then_inc(gpsimd_step, st.step(f"M.lms{n}"))
                pool.wait_ge(gpsimd_step, st.at("M.lmsk"))
                st.apart()
                pool.tensor_tensor(stat[:, 2, 0:4], stat[:, 1, 0:4], half_power[:, 0:4], ALU.pow).then_inc(gpsimd_step, st.step("M.rsl"))
                pool.wait_ge(scalar_step, st.at("M.v_f.ev"))
                st.apart()
                pool.wait_ge(vectors_loaded, st.at("L.loaded", 1))
                st.apart()
                pool.tensor_tensor(ft[:, 0], lat[:, :, 416:420], bforget.unsqueeze(1).to_broadcast([P, NT, 4]),
                                           ALU.add).then_inc(gpsimd_step, st.step("M.z"))
                pool.wait_ge(scalar_step, st.at("M.expz"))
                st.apart()
                pool.tensor_scalar(ft[:, 1], ft[:, 1], 1.0, None, ALU.add).then_inc(gpsimd_step, st.step("M.onez"))
                pool.tensor_scalar(ft[:, 0], ft[:, 0], 0.0, None, ALU.min).then_inc(gpsimd_step, st.step("M.minz"))
                pool.wait_ge(scalar_step, st.at("M.lnz"))
                st.apart()
                pool.wait_ge(gpsimd_step, st.at("M.minz"))
                st.apart()
                pool.tensor_tensor(logf, ft[:, 0], ft[:, 1], ALU.subtract).then_inc(gpsimd_step, st.step("M.lf"))
                pool.wait_ge(gpsimd_step, st.at("M.lf"))
                st.apart()
                pool.tensor_copy(fa[:, :, :, 0], logf)
                pool.tensor_scalar(fb[:, :, :, 1], logf, -1.0, None, ALU.mult).then_inc(gpsimd_step, st.step("M.logf"))
                for e in ("uq.ev", "uq.ev1", "ukv1.ev"):
                    pool.wait_ge(st.sem_of(f"M.{e}"), st.at(f"M.{e}"))
                    st.apart()
                half = ROPE // 2
                for tag, v, heads in (("q", qlat, MLA_H), ("k", None, 1)):
                    if v is None:
                        x1 = lat[:, :, 384:384 + half]
                        x2 = lat[:, :, 384 + half:384 + ROPE]
                        o1, o2 = krot[:, :, 0:half], krot[:, :, half:ROPE]
                        c_, s_ = cs[:, 0], cs[:, 1]
                        r = [m_[:, 0:NT * half].rearrange("p (t d) -> p t d", t=NT) for m_ in rot]
                    else:
                        x1, x2 = v[:, :, :, HD:HD + half], v[:, :, :, HD + half:]
                        o1, o2 = x1, x2
                        c_, s_ = (cs[:, i].unsqueeze(2).to_broadcast([P, NT, heads, half]) for i in range(2))
                        r = [m_.rearrange("p (t h d) -> p t h d", t=NT, h=heads) for m_ in rot]
                    for i, (a, b) in enumerate(((x1, c_), (x2, s_), (x2, c_), (x1, s_))):
                        pool.tensor_tensor(r[i], a, b, ALU.mult).then_inc(gpsimd_step, st.step(f"M.r{tag}{i}"))
                    pool.wait_ge(gpsimd_step, st.at(f"M.r{tag}3"))
                    st.apart()
                    pool.tensor_tensor(o1, r[0], r[1], ALU.subtract)
                    pool.tensor_tensor(o2, r[2], r[3], ALU.add).then_inc(gpsimd_step, st.step(f"M.r{tag}"))
                    pool.wait_ge(gpsimd_step, st.at(f"M.r{tag}"))
                    st.apart()
                for t in range(NT):
                    i = pool.tensor_copy(klat[:, t, :, HD:], krot[:, t, :].unsqueeze(1).to_broadcast([P, MLA_H, ROPE]))
                i.then_inc(gpsimd_step, st.step("M.rope"))
                acc_bias(2, l)
                for t in range(NT):
                    pool.wait_ge(scalar_step, st.at(f"M.osq{t}"))
                    st.apart()
                    for g, w in enumerate((256, 256, 512)):
                        i = 3 * t + g
                        pool.tensor_scalar(stat[:, 1, i:i + 1], stat[:, 0, i:i + 1], 1.0 / w, EPS, ALU.mult,
                                                   ALU.add).then_inc(gpsimd_step, st.step(f"M.oms{t}.{g}"))
                    pool.wait_ge(gpsimd_step, st.at(f"M.oms{t}.2"))
                    st.apart()
                    pool.tensor_tensor(stat[:, 2, 3 * t:3 * t + 3], stat[:, 1, 3 * t:3 * t + 3],
                                               half_power[:, 0:3], ALU.pow).then_inc(gpsimd_step, st.step(f"M.ors{t}"))

            def hgrn(p):
                for c in range(4):
                    pool.wait_ge(scalar_step, st.at(f"{p}.v{c}.ev"))
                    pool.wait_ge(vectors_loaded, st.at(f"{p}.const"))
                    for h in (2 * c, 2 * c + 1):
                        for t in range(NT):
                            if h:
                                pool.wait_ge(tensor_step, st.at(f"{p}.u{(h - 1) * 4 + 2 * t + 1}"))
                            full = [P, NHB, P]
                            pool.tensor_tensor(vmask[t], hv[:, t, h * P:h * P + P].unsqueeze(1).to_broadcast(full),
                                                       blockm.unsqueeze(2).to_broadcast(full), ALU.mult).then_inc(gpsimd_step, st.step(f"{p}.vm{h}.{t}"))
                    pool.wait_ge(vector_step, st.at(f"{p}.oms{c}"))
                    pool.tensor_tensor(hstat[:, 4:8], hstat[:, 0:4], half_power[:, 0:4], ALU.pow)\
                        .then_inc(gpsimd_step, st.step(f"{p}.orr{c}"))

            def diff(p):
                for t in range(NT):
                    pool.wait_ge(vector_step, st.at(f"{p}.oss{t}"))
                    a, b = dstat[:, 3, 8 * t:8 * t + 8], dstat[:, 3, 16 + 8 * t:24 + 8 * t]
                    pool.tensor_scalar(b, a, 1.0 / P, EPS, ALU.mult, ALU.add).then_inc(gpsimd_step, st.step(f"{p}.oms{t}"))
                    pool.wait_ge(gpsimd_step, st.at(f"{p}.oms{t}"))
                    pool.tensor_tensor(b, b, half_power[:, 0:8], ALU.pow).then_inc(gpsimd_step, st.step(f"{p}.ors{t}"))

            def constants_for(i):
                pool.wait_ge(vector_step, st.at("F.x1" if i == 0 else f"{i - 1}m.x1"))
                if i == 0:
                    pool.wait_ge(vector_step, st.at("M.ada0"))
                p = f"{i}m"
                if i % 3 == 0:
                    pool.dma_start(scan_mask, A["K_scan"])\
                        .then_inc(vectors_loaded, st.step(f"{p}.c0", vectors_loaded, 16))
                    pool.dma_start(intra, A["K_intra"])\
                        .then_inc(vectors_loaded, st.step(f"{p}.c1", vectors_loaded, 16))
                    pool.dma_start(blockm, A["K_block"])\
                        .then_inc(vectors_loaded, st.step(f"{p}.const", vectors_loaded, 16))
                elif i == 1:
                    pool.dma_start(cdist, A["K_chunk_dist"])\
                        .then_inc(vectors_loaded, st.step(f"{p}.c0", vectors_loaded, 16))
                    pool.dma_start(lamrow.rearrange("p a b -> p (a b)"), A["diff_lambda_2"].rearrange("a b c -> a (b c)").to_broadcast([P, 4 * HD]))\
                        .then_inc(vectors_loaded, st.step(f"{p}.const", vectors_loaded, 16))
                    pool.memset(dk, 0.0).then_inc(gpsimd_step, st.step(f"{p}.zero"))
                else:
                    pool.dma_start(counts.rearrange("p a b -> p (a b)"), A["K_counts"])\
                        .then_inc(vectors_loaded, st.step(f"{p}.const", vectors_loaded, 16))

            def layer_vectors(l, name, m):
                for v, r, k in (("g_mix_pre", 0, 8), ("g_ffn_pre", 8, 8), ("g_group", 16, 8), ("g_q_lat", 24, 2),
                                ("g_kv_lat", 26, 1)):
                    pool.dma_start(rows[r:r + k, :], vec(A[v], l))\
                        .then_inc(vectors_loaded, st.step(f"{name}.{v}", vectors_loaded, 16))
                pool.dma_start(bforget, A["b_forget"][bass.ds(l, 1), :].to_broadcast([P, 4]))\
                    .then_inc(vectors_loaded, st.step(f"{name}.loaded", vectors_loaded, 16))

            acc_bias(0, 0, "P")
            pool.memset(half_power[:, :], -0.5).then_inc(gpsimd_step, st.step("half"))
            pool.memset(ones[:, :], 1.0)
            pool.memset(kf, 0.0)
            pool.memset(km, 0.0).then_inc(gpsimd_step, st.step("zeros"))
            layer_vectors(0, "P", "P")
            with st.loop("layers", LAYERS, LAYER_UNITS) as l:
                for g, v in enumerate(("g_mix_post", "g_ffn_post")):
                    pool.dma_start(post[g][:, :], A[v][bass.ds(l, 1), :].to_broadcast([P, D]))\
                        .then_inc(post_gain_loaded[0], st.step("L.post", post_gain_loaded[0], 16))
                mixer1(l)
                boundary("M", "F")
                acc_bias(0, other(l))
                layer_vectors(other(l), "L", "M")
                boundary("F", None)
                pool.wait_ge(vector_step, st.at("F.x1"))
                st.apart()
                st.r, st.n = st.r + LAYER_UNITS[0], st.n + LAYER_UNITS[1]

            def post_gain(s):
                i, j = divmod(s, 3)
                if s >= 2:
                    pool.wait_ge(vector_step, st.at(f"{names[s - 2]}.x1"))
                pool.dma_start(post[s % 2][:, :], A["norm_gains_2"][i, 2 * j + 1:2 * j + 2, :].to_broadcast([P, D]))\
                    .then_inc(post_gain_loaded[s % 2], st.step(f"{names[s]}.post", post_gain_loaded[s % 2], 16))

            post_gain(0)
            post_gain(1)
            constants_for(0)
            boundary(None, names[0])
            for s, p in enumerate(names):
                if p[1] == "m" and int(p[0]) % 3 < 2:
                    (hgrn, diff)[int(p[0]) % 3](p)
                boundary(p, names[s + 1] if s + 1 < len(names) else None)
                if s + 2 < len(names):
                    post_gain(s + 2)
                if p[1] == "m" and p != "3m":
                    constants_for(int(p[0]) + 1)


_OUT = (1, S, D)


def kernel(**inputs):
    import concourse.bacc as _bacc
    from concourse.bass_utils import run_bass_kernel_spmd as _run

    arrays = {f"in_{k}": np.ascontiguousarray(v) for k, v in inputs.items()}
    arrays.update({f"in_K_{k}": v for k, v in constants().items()})

    def build(table, per, trips):
        nc = _bacc.Bacc("TRN2", target_bir_lowering=False, num_devices=1)
        A = {k[3:]: nc.dram_tensor(k, a.shape, mybir.dt.from_np(a.dtype), kind="ExternalInput").ap()
             for k, a in arrays.items()}
        out = nc.dram_tensor("out_0", _OUT, F32, kind="ExternalOutput").ap()
        program(nc, A, out, table, per, trips)
        return nc

    table, per, trips = {}, {}, {}
    build(table, per, trips)
    nc = build(table, per, trips)
    r = _run(nc, [arrays], core_ids=[0])
    return r.results[0]["out_0"]
```
